# Optimizing a Trainium2 kernel written in Bass

```python
import math
import jax, jax.numpy as jnp
from jax import lax
import numpy as np

D_MODEL = 2048
BATCH = 1
SEQ = 512
DEPTH = 1
DEC_BATCH = 8
DEC_SEQ = 4
PAST_LEN = 1024
PAGE_SIZE = 128

HEAD_DIM = 128
N_HEADS = D_MODEL // HEAD_DIM
N_KV_HEADS = N_HEADS // 4
GROUP = N_HEADS // N_KV_HEADS
Q_DIM = N_HEADS * HEAD_DIM
KV_DIM = N_KV_HEADS * HEAD_DIM
QKV_DIM = Q_DIM + 2 * KV_DIM
D_FF = 4 * D_MODEL
N_MIXERS = 2
N_FOX_LAYERS = (DEPTH + 1) // 2
FOX_Q_BLOCK = 128
MOBA_BLOCK = 256
MOBA_TOPK = 3
MOBA_Q_BLOCK = 32
FGATE_BIAS = 3.0
RMS_EPS = 1e-6
F32 = jnp.float32

kernel_name = "fox_moba_hybrid_decode_step"

def rms_norm(x, g):
    xf = x.astype(F32)
    y = xf * lax.rsqrt(jnp.mean(xf * xf, axis=-1, keepdims=True) + RMS_EPS)
    return (y * g.astype(F32)).astype(x.dtype)

def project_qkv(xn, w_qkv, q_gain, k_gain):
    b, t, _ = xn.shape
    qkv = xn @ w_qkv
    q = qkv[..., :Q_DIM].reshape(b, t, N_HEADS, HEAD_DIM)
    k = qkv[..., Q_DIM:Q_DIM + KV_DIM].reshape(b, t, N_KV_HEADS, HEAD_DIM)
    v = qkv[..., Q_DIM + KV_DIM:].reshape(b, t, N_KV_HEADS, HEAD_DIM)
    return rms_norm(q, q_gain), rms_norm(k, k_gain), v

def gather_past(pool, page_table):
    g = pool[page_table]
    return g.reshape((page_table.shape[0], page_table.shape[1] * pool.shape[1]) + pool.shape[2:])

def fox_attention(q, k, v, c_q, c_k, q_offset, q_block):
    b, tq = q.shape[:2]
    L = k.shape[1]
    nb = tq // q_block
    qb = q.reshape(b, nb, q_block, N_KV_HEADS, GROUP, HEAD_DIM).swapaxes(0, 1)
    cqb = c_q.reshape(b, nb, q_block, N_KV_HEADS, GROUP).transpose(1, 0, 3, 4, 2)
    ck = c_k.reshape(b, L, N_KV_HEADS, GROUP).transpose(0, 2, 3, 1)
    k_pos = jnp.arange(L)
    starts = q_offset + jnp.arange(nb) * q_block
    scale = HEAD_DIM ** -0.5

    def one_block(args):
        qi, cqi, start = args
        s = jnp.einsum('btkgd,bskd->bkgts', qi, k, preferred_element_type=F32) * scale
        logits = s + (cqi[..., :, None] - ck[..., None, :])
        q_pos = start + jnp.arange(q_block)
        causal = k_pos[None, :] <= q_pos[:, None]
        p = jax.nn.softmax(jnp.where(causal, logits, -jnp.inf), axis=-1)
        return jnp.einsum('bkgts,bskd->btkgd', p.astype(v.dtype), v)

    out = lax.map(one_block, (qb, cqb, starts))
    return out.swapaxes(0, 1).reshape(b, tq, Q_DIM)

def moba_attention(q, k, v, q_offset, q_block):
    b, tq = q.shape[:2]
    L = k.shape[1]
    n_blk = max(-(-L // MOBA_BLOCK), MOBA_TOPK)
    pad = n_blk * MOBA_BLOCK - L

    def blockify(a):
        a = jnp.pad(a, ((0, 0), (0, pad), (0, 0), (0, 0)))
        return a.reshape(b, n_blk, MOBA_BLOCK, N_KV_HEADS, HEAD_DIM).transpose(0, 3, 1, 2, 4)

    kb, vb = blockify(k), blockify(v)
    k_mean = jnp.mean(kb.astype(F32), axis=3)
    slopes = jnp.exp2(-8.0 * jnp.arange(1, N_HEADS + 1, dtype=F32) / N_HEADS).reshape(N_KV_HEADS, GROUP)
    nbq = tq // q_block
    qb = q.reshape(b, nbq, q_block, N_KV_HEADS, GROUP, HEAD_DIM).swapaxes(0, 1)
    starts = q_offset + jnp.arange(nbq) * q_block
    b_idx = jnp.arange(b)[:, None, None, None, None]
    h_idx = jnp.arange(N_KV_HEADS)[None, None, :, None, None]
    blk_ids = jnp.arange(n_blk)
    in_blk = jnp.arange(MOBA_BLOCK)
    scale = HEAD_DIM ** -0.5

    def one_block(args):
        qi, start = args
        q_pos = start + jnp.arange(q_block)
        own = q_pos // MOBA_BLOCK
        gate = jnp.einsum('btkgd,bknd->btkgn', qi.astype(F32), k_mean)
        fully_past = blk_ids[None, :] < own[:, None]
        gate = jnp.where(fully_past[None, :, None, None, :], gate, -jnp.inf)
        _, top = lax.top_k(gate, MOBA_TOPK)
        own_b = jnp.broadcast_to(own[None, :, None, None, None], top.shape[:-1] + (1,)).astype(top.dtype)
        sel = jnp.concatenate([top, own_b], axis=-1)
        sel_ok = jnp.concatenate([top < own[None, :, None, None, None],
                                  jnp.ones(own_b.shape, dtype=bool)], axis=-1)
        kg = kb[b_idx, h_idx, sel]
        vg = vb[b_idx, h_idx, sel]
        s = jnp.einsum('btkgd,btkgnjd->btkgnj', qi, kg, preferred_element_type=F32) * scale
        dist = (q_pos[None, :, None, None, None, None]
                - (sel[..., None] * MOBA_BLOCK + in_blk)).astype(F32)
        ok = sel_ok[..., None] & (dist >= 0)
        logits = jnp.where(ok, s - slopes[None, None, :, :, None, None] * dist, -jnp.inf)
        p = jax.nn.softmax(logits.reshape(logits.shape[:4] + (-1,)), axis=-1).reshape(logits.shape)
        return jnp.einsum('btkgnj,btkgnjd->btkgd', p.astype(v.dtype), vg)

    out = lax.map(one_block, (qb, starts))
    return out.swapaxes(0, 1).reshape(b, tq, Q_DIM)

def sq_relu_mlp(x, g, w_up, w_down):
    h = rms_norm(x, g) @ w_up
    return jnp.square(jax.nn.relu(h)) @ w_down

def setup_inputs(seed: int = 0) -> dict:
    key = jax.random.key(seed)
    ks = jax.random.split(key, 20)
    n_pages = PAST_LEN // PAGE_SIZE
    n_used = DEC_BATCH * n_pages
    n_pool = n_used + n_used // 4
    nrm = jax.random.normal
    x_prompt = nrm(ks[0], (BATCH, SEQ, D_MODEL), F32)
    x_sample = nrm(ks[1], (DEC_BATCH, DEC_SEQ, D_MODEL), F32)
    cache_k = nrm(ks[2], (DEPTH, n_pool, PAGE_SIZE, N_KV_HEADS, HEAD_DIM), F32)
    cache_v = nrm(ks[3], (DEPTH, n_pool, PAGE_SIZE, N_KV_HEADS, HEAD_DIM), F32)
    cache_logf = jax.nn.log_sigmoid(FGATE_BIAS + nrm(ks[4], (N_FOX_LAYERS, n_pool, PAGE_SIZE, N_HEADS), F32))
    page_table = jax.random.permutation(ks[5], n_pool)[:n_used].reshape(DEC_BATCH, n_pages).astype(jnp.int32)
    attn_norm = 1.0 + 0.02 * nrm(ks[6], (DEPTH, D_MODEL), F32)
    w_qkv = nrm(ks[7], (DEPTH, D_MODEL, QKV_DIM), F32) * D_MODEL ** -0.5
    q_norm = 1.0 + 0.02 * nrm(ks[8], (DEPTH, HEAD_DIM), F32)
    k_norm = 1.0 + 0.02 * nrm(ks[9], (DEPTH, HEAD_DIM), F32)
    w_fgate = nrm(ks[10], (N_FOX_LAYERS, D_MODEL, N_HEADS), F32) * D_MODEL ** -0.5
    b_fgate = FGATE_BIAS + 0.1 * nrm(ks[11], (N_FOX_LAYERS, N_HEADS), F32)
    w_o = nrm(ks[12], (DEPTH, Q_DIM, D_MODEL), F32) * Q_DIM ** -0.5
    mlp_norm = 1.0 + 0.02 * nrm(ks[13], (DEPTH, D_MODEL), F32)
    w_up = nrm(ks[14], (DEPTH, D_MODEL, D_FF), F32) * D_MODEL ** -0.5
    w_down = nrm(ks[15], (DEPTH, D_FF, D_MODEL), F32) * D_FF ** -0.5
    return {"x_prompt": x_prompt, "x_sample": x_sample, "cache_k": cache_k, "cache_v": cache_v,
            "cache_logf": cache_logf, "page_table": page_table, "attn_norm": attn_norm, "w_qkv": w_qkv,
            "q_norm": q_norm, "k_norm": k_norm, "w_fgate": w_fgate, "b_fgate": b_fgate, "w_o": w_o,
            "mlp_norm": mlp_norm, "w_up": w_up, "w_down": w_down}

def reference(x_prompt, x_sample, cache_k, cache_v, cache_logf, page_table, attn_norm, w_qkv, q_norm, k_norm,
              w_fgate, b_fgate, w_o, mlp_norm, w_up, w_down):
    past_len = page_table.shape[1] * cache_k.shape[2]
    hp, hs = x_prompt, x_sample
    k_p, v_p, f_p, k_s, v_s, f_s = [], [], [], [], [], []
    for i in range(DEPTH):
        xp = rms_norm(hp, attn_norm[i])
        xs = rms_norm(hs, attn_norm[i])
        qp, kp, vp = project_qkv(xp, w_qkv[i], q_norm[i], k_norm[i])
        qs, ks_, vs = project_qkv(xs, w_qkv[i], q_norm[i], k_norm[i])
        k_all = jnp.concatenate([gather_past(cache_k[i], page_table).astype(ks_.dtype), ks_], axis=1)
        v_all = jnp.concatenate([gather_past(cache_v[i], page_table).astype(vs.dtype), vs], axis=1)
        k_p.append(kp); v_p.append(vp); k_s.append(ks_); v_s.append(vs)
        if i % N_MIXERS == 0:
            j = i // N_MIXERS
            lf_p = jax.nn.log_sigmoid((xp @ w_fgate[j]).astype(F32) + b_fgate[j].astype(F32))
            lf_s = jax.nn.log_sigmoid((xs @ w_fgate[j]).astype(F32) + b_fgate[j].astype(F32))
            c_p = jnp.cumsum(lf_p, axis=1)
            c_s = jnp.cumsum(jnp.concatenate([gather_past(cache_logf[j], page_table).astype(F32), lf_s], axis=1), axis=1)
            mix_p = fox_attention(qp, kp, vp, c_p, c_p, 0, FOX_Q_BLOCK)
            mix_s = fox_attention(qs, k_all, v_all, c_s[:, past_len:], c_s, past_len, qs.shape[1])
            f_p.append(lf_p.astype(cache_logf.dtype)); f_s.append(lf_s.astype(cache_logf.dtype))
        else:
            mix_p = moba_attention(qp, kp, vp, 0, MOBA_Q_BLOCK)
            mix_s = moba_attention(qs, k_all, v_all, past_len, 1)
        hp = hp + mix_p @ w_o[i]
        hs = hs + mix_s @ w_o[i]
        hp = hp + sq_relu_mlp(hp, mlp_norm[i], w_up[i], w_down[i])
        hs = hs + sq_relu_mlp(hs, mlp_norm[i], w_up[i], w_down[i])
    return (hp, hs, jnp.stack(k_p), jnp.stack(v_p), jnp.stack(f_p), jnp.stack(k_s), jnp.stack(v_s), jnp.stack(f_s))


_drawn_inputs = setup_inputs


def setup_inputs(seed=0):
    import zlib

    import numpy as np

    out = dict(_drawn_inputs(seed))
    spreads = {}
    factors = {'attn_norm': 2.779, 'q_norm': 8.0, 'mlp_norm': 3.134}
    for name, (base, spread) in spreads.items():
        noise = np.random.default_rng([zlib.crc32(name.encode()), seed]).standard_normal(out[name].shape)
        drawn = base * np.exp(spread * noise) if base else spread * noise
        out[name] = __import__('jax').numpy.asarray(drawn.astype(out[name].dtype))
    for name, factor in factors.items():
        out[name] = (out[name] * factor).astype(out[name].dtype)
    return out
```

```python
from contextlib import ExitStack

import concourse.bass as bass
from concourse import mybir

F32 = mybir.dt.float32
F32R = mybir.dt.float32r
I32 = mybir.dt.int32
ACT = mybir.ActivationFunctionType
ALU = mybir.AluOpType
AX = mybir.AxisListType

P = 128
BIG = 1.0e30


def fox_layer(nc, x_prompt, x_sample, cache_k, cache_v, cache_logf, page_table, attn_norm, w_qkv, q_norm,
              k_norm, w_fgate, b_fgate, w_o, mlp_norm, w_up, w_down,
              y_prompt, y_sample, nk_prompt, nv_prompt, nf_prompt, nk_sample, nv_sample, nf_sample):
    _, SEQ, D = x_prompt.shape
    NB, DS, _ = x_sample.shape
    _, NPOOL, PAGE, NKV, HD = cache_k.shape
    NH = cache_logf.shape[3]
    NPG = page_table.shape[1]
    DFF = w_up.shape[2]
    GRP = NH // NKV
    NS = NB * DS
    T = SEQ + NS
    HALF = T // 2
    QT = SEQ // P
    TT = QT + 1
    LAST = T - P
    KC = D // P
    UC = 8
    FB = UC
    NBLK = DFF // P // FB
    KVC = NKV * HD
    SCALE = float(HD) ** -0.5
    EPS = 1e-6
    NP9 = NPG + 1
    QS = NH * DS
    assert PAGE == P and HD == P and SEQ == 4 * P and HALF * 4 <= 2048 and NPG == 8 and KC == 2 * UC
    assert NH == 16 and GRP == 4 and NB == 8

    with ExitStack() as ctx:
        def sem(name):
            return ctx.enter_context(nc.semaphore(name))

        base = -(-nc.sbuf_base // 64) * 64
        top = [base]

        def at(name, shape, dt, offset=None):
            n = 4
            for s in shape[1:]:
                n *= s
            if offset is None:
                offset = top[0]
                top[0] += -(-n // 64) * 64
            return nc.alloc_sbuf_tensor_at(name, shape, dt, offset=offset), offset, offset + n

        xT, _, _ = at("xT", [P, KC, T], F32)
        act_hi, act_at, _ = at("act_hi", [P, KC, T], F32R)
        act_lo, _, act_end = at("act_lo", [P, KC, T], F32R)
        kq, kq_at, _ = at("kq", [P, NKV + NH, T], F32)
        vT, _, _ = at("vT", [P, NKV, T], F32)
        w_raw, _, _ = at("w_raw", [P, 4, UC, P], F32)
        w_hi, _, _ = at("w_hi", [P, 2, UC, P], F32R)
        w_lo, _, _ = at("w_lo", [P, 2, UC, P], F32R)
        tmp_a, tmp_a_at, _ = at("tmp_a", [P, 2, T], F32)
        tmp_b, tmp_b_at, _ = at("tmp_b", [P, 2, T], F32)
        tmp_c, tmp_c_at, _ = at("tmp_c", [P, 2, T], F32)
        ident, _, _ = at("ident", [P, P], F32)
        ones, _, _ = at("ones", [P, P], F32)
        tri, _, _ = at("tri", [P, P], F32)
        tri4, _, _ = at("tri4", [P, P], F32)
        causal, _, _ = at("causal", [P, P], F32)
        allow, _, _ = at("allow", [P, NB, DS], F32)
        newmask, _, _ = at("newmask", [P, NB, DS], F32)
        eps_t, _, _ = at("eps_t", [P, 1], F32)
        g_attn, _, _ = at("g_attn", [P, KC], F32)
        g_mlp, _, _ = at("g_mlp", [P, KC], F32)
        g_kq, _, _ = at("g_kq", [P, NKV + NH], F32)
        g_qk1, _, _ = at("g_qk1", [P, 2], F32)
        bf, _, _ = at("bf", [NH, 1], F32)
        pages, _, _ = at("pages", [1, NB * NPG], I32)
        tokc, _, _ = at("tokc", [P, TT + QT, NH], F32)
        nmax, _, _ = at("nmax", [P, 2, QT], F32)
        rsum, _, _ = at("rsum", [P, 2, QT], F32)
        rinv, _, _ = at("rinv", [P, 2, QT], F32)
        m64, _, _ = at("m64", [QS, 1], F32)
        colmax, _, _ = at("colmax", [P, P], F32)
        diag, _, _ = at("diag", [QS, QS], F32)
        colsum, _, _ = at("colsum", [P, QS], F32)
        rden, _, end = at("rden", [P, QS], F32)
        assert end <= nc.sbuf_usable_end, (end, nc.sbuf_usable_end)

        x_tok, _, e = at("x_tok", [P, TT, D], F32, act_at)
        assert e <= act_end
        u_hi, _, e = at("u_hi", [P, FB, T], F32R, kq_at)
        u_lo, _, e = at("u_lo", [P, FB, T], F32R, e)
        fz, _, _ = at("fz", [NH, 2, T], F32, tmp_a_at)
        fe, _, _ = at("fe", [NH, 2, T], F32, tmp_b_at)
        lfT, _, o = at("lfT", [NH, T], F32, tmp_c_at)
        cT, _, _ = at("cT", [NH, T], F32, o)
        v_tok, _, o = at("v_tok", [P, TT, KVC], F32, act_at)
        scr = o
        k_tok, _, _ = at("k_tok", [P, TT, KVC], F32, scr)
        probs, _, o = at("probs", [P, 4, QT, SEQ], F32, scr)
        pT, _, o = at("pT", [P, 2, 10 * P], F32, o)
        c_row, _, o = at("c_row", [P, 2, SEQ], F32, o)
        c_diag, _, o = at("c_diag", [P, 2, QT, P], F32, o)
        q_st, _, o = at("q_st", [P, 2, SEQ], F32, o)
        v_st, _, o = at("v_st", [P, QT, P], F32, o)
        assert o <= act_end
        k_page, _, o = at("k_page", [P, 4, KVC], F32, scr)
        v_page, _, o = at("v_page", [P, 2, NPG, KVC], F32, o)
        kcT, _, o = at("kcT", [P, 2, KVC], F32, o)
        dbias, _, o = at("dbias", [P, 2, NP9, QS], F32, o)
        sprob, _, o = at("sprob", [P, 2, NP9, QS], F32, o)
        assert o <= act_end
        lf_page, _, o = at("lf_page", [P, NB * NPG, NH], F32, tmp_a_at)
        ck, _, o = at("ck", [P, NB * NPG, NH], F32, tmp_b_at)
        pre, _, o = at("pre", [P, NPG, NB, NH], F32, tmp_c_at)
        assert o <= tmp_c_at + 8 * T
        cq, _, o = at("cq", [P, NB, NH, DS], F32, top[0])
        ck_new, _, o = at("ck_new", [P, NB, NH], F32, o)
        lf_rep, _, o = at("lf_rep", [P, NB, NH, DS], F32, o)
        assert o <= nc.sbuf_usable_end, (o, nc.sbuf_usable_end)

        ps = ctx.enter_context(nc.psum_tensor("ps", [P, 8, 512], F32))
        psf = ps[:, :, :].rearrange("p b n -> p (b n)")
        c_rows = nc.dram_tensor("c_rows", [NH, SEQ], F32).ap()

        def halves(ap):
            return ap.rearrange("p (a n) -> p a n", a=2)

        def acc(slot, rows=P):
            return ps[0:rows, 2 * slot:2 * slot + 2, 0:HALF]

        const_made = sem("const_made")
        const_loaded = sem("const_loaded")
        gains_made = sem("gains_made")
        pages_loaded = sem("pages_loaded")
        x_loaded = [sem(f"x_loaded{i}") for i in range(4)]
        x_turned = sem("x_turned")
        xT_made = sem("xT_made")
        sq_made = sem("sq_made")
        sq_added_dve = sem("sq_added_dve")
        sq_added_pool = sem("sq_added_pool")
        ssq_ready = sem("ssq_ready")
        std_ready = sem("std_ready")
        rstd_ready = sem("rstd_ready")
        scaled = sem("scaled")
        act_hi_made = sem("act_hi_made")
        act_lo_dve = sem("act_lo_dve")
        act_lo_pool = sem("act_lo_pool")
        w_loaded = [sem(f"w_loaded{i}") for i in range(4)]
        w_hi_made = sem("w_hi_made")
        w_lo_made = sem("w_lo_made")
        unit_used = sem("unit_used")
        acc_free = [sem("acc_free0"), sem("acc_free1")]
        f_chain = sem("f_chain")
        f_exp = sem("f_exp")
        f_turned = sem("f_turned")
        tokc_made = sem("tokc_made")
        c_stored = sem("c_stored")
        head_ssq = sem("head_ssq")
        head_std = sem("head_std")
        head_rec = sem("head_rec")
        head_done = sem("head_done")
        v_evac = sem("v_evac")
        lf_loaded = sem("lf_loaded")
        kv_turned = sem("kv_turned")
        vtok_made = sem("vtok_made")
        ktok_made = sem("ktok_made")
        kv_stored = sem("kv_stored")
        lf_stored = sem("lf_stored")
        csum_done = sem("csum_done")
        csum_chain = sem("csum_chain")
        q_staged = sem("q_staged")
        v_staged = sem("v_staged")
        c_loaded = [sem("c_loaded0"), sem("c_loaded1")]
        cdiag_made = sem("cdiag_made")
        score_done = sem("score_done")
        logit_made = sem("logit_made")
        max_made = sem("max_made")
        exp_made = sem("exp_made")
        rinv_made = sem("rinv_made")
        normed = sem("normed")
        p_turned = sem("p_turned")
        pT_act = sem("pT_act")
        pT_dve = sem("pT_dve")
        pv_done = sem("pv_done")
        out_evac = sem("out_evac")
        page_loaded = [sem(f"page_loaded{i}") for i in range(4)]
        vpage_loaded = [sem("vpage_loaded0"), sem("vpage_loaded1")]
        k_turned = sem("k_turned")
        kcT_act = sem("kcT_act")
        kcT_dve = sem("kcT_dve")
        page_scored = sem("page_scored")
        new_scored = sem("new_scored")
        dbias_chain = sem("dbias_chain")
        dbias_made = sem("dbias_made")
        s_logit = sem("s_logit")
        s_colmax = sem("s_colmax")
        s_maxT = sem("s_maxT")
        s_chain = sem("s_chain")
        s_diag = sem("s_diag")
        s_maxrow = sem("s_maxrow")
        s_shift = sem("s_shift")
        s_exp = sem("s_exp")
        s_colsum = sem("s_colsum")
        s_den = sem("s_den")
        s_rden = sem("s_rden")
        s_pv = sem("s_pv")
        s_out = sem("s_out")
        mix_hi = sem("mix_hi")
        mix_lo = sem("mix_lo")
        relu_made = sem("relu_made")
        relu_sq = sem("relu_sq")
        u_hi_made = sem("u_hi_made")
        u_lo_made = sem("u_lo_made")
        y_turned = sem("y_turned")
        y_evac_act = sem("y_evac_act")
        y_evac_dve = sem("y_evac_dve")
        y_stored = sem("y_stored")

        U_V, U_K, U_Q, U_O, U_M = 2, 10, 18, 50, 82
        T_V, T_K, T_Q, T_O, T_M = 1, 5, 9, 25, 41
        BLK_U, BLK_T = 32, 24
        assert U_M + BLK_U * NBLK == 338

        w_f_v = w_fgate[0].rearrange("(k p) n -> p k n", p=P)
        w_qkv_v = w_qkv[0].rearrange("(k p) n -> p k n", p=P)
        w_o_v = w_o[0].rearrange("(k p) n -> p k n", p=P)
        w_up_v = w_up[0].rearrange("(k p) n -> p k n", p=P)
        w_down_v = w_down[0].rearrange("(k p) n -> p k n", p=P)

        block = ctx.enter_context(nc.Block())

        @block.sync
        def _(sp):
            def load_unit(i, k, src):
                if not isinstance(i, int) or 4 * i + k >= 4:
                    sp.wait_ge(w_lo_made, 4 * i + (k - 3))
                sp.dma_start(w_raw[:, k % 4, :, 0:src.shape[2]], src).then_inc(w_loaded[k % 4], 16)

            def cols(view, half, col):
                return view[:, half * UC:(half + 1) * UC, col:col + P] if isinstance(col, int) else \
                    view[:, half * UC:(half + 1) * UC, bass.ds(col, P)]

            gw = D // 4
            for n in range(4):
                sp.dma_start(x_tok[:, 0:QT, n * gw:(n + 1) * gw],
                             x_prompt[0].rearrange("(t p) d -> p t d", p=P)[:, :, n * gw:(n + 1) * gw]
                             ).then_inc(x_loaded[n], 16)
                sp.dma_start(x_tok[0:NS, QT, n * gw:(n + 1) * gw],
                             x_sample.rearrange("b i d -> (b i) d")[:, n * gw:(n + 1) * gw]
                             ).then_inc(x_loaded[n], 16)
            load_unit(0, 0, w_f_v[:, 0:UC, :])
            load_unit(0, 1, w_f_v[:, UC:KC, :])
            load_unit(0, 2, cols(w_qkv_v, 0, D + KVC))
            load_unit(0, 3, cols(w_qkv_v, 1, D + KVC))
            with nc.allow_non_contiguous_dma(reason="small vectors, one element a partition"):
                sp.dma_start(g_attn[:], attn_norm[0].rearrange("(c p) -> p c", p=P)).then_inc(const_loaded, 16)
                sp.dma_start(g_mlp[:], mlp_norm[0].rearrange("(c p) -> p c", p=P)).then_inc(const_loaded, 16)
                sp.dma_start(g_qk1[:, 0:1], k_norm.rearrange("o p -> p o")).then_inc(const_loaded, 16)
                sp.dma_start(g_qk1[:, 1:2], q_norm.rearrange("o p -> p o")).then_inc(const_loaded, 16)
                sp.dma_start(bf[:], b_fgate.rearrange("o h -> h o")).then_inc(const_loaded, 16)

            load_unit(1, 0, cols(w_qkv_v, 0, D + KVC + P))
            load_unit(1, 1, cols(w_qkv_v, 1, D + KVC + P))
            for n in range(2, NKV):
                for half in range(2):
                    u = U_V + 2 * n + half
                    load_unit(u // 4, u % 4, cols(w_qkv_v, half, D + KVC + n * P))
            for n in range(NKV):
                for half in range(2):
                    u = U_K + 2 * n + half
                    load_unit(u // 4, u % 4, cols(w_qkv_v, half, D + n * P))
                if n == 0:
                    sp.wait_ge(f_chain, 5)
                    sp.dma_start(c_rows, cT[:, 0:SEQ]).then_inc(c_stored, 16)
            with sp.Fori(0, NH // 2) as i:
                for k in range(4):
                    load_unit(i + (U_Q + k) // 4, (U_Q + k) % 4, cols(w_qkv_v, k % 2, i * (2 * P) + (k // 2) * P))
            for u in range(U_O, U_O + 4):
                k = u - U_O
                load_unit(u // 4, u % 4, cols(w_o_v, k % 2, (k // 2) * P))

            sp.wait_ge(tokc_made, 1)
            sp.dma_start(nf_prompt[0, 0].rearrange("(t p) h -> p t h", p=P), tokc[:, 0:QT, :]).then_inc(lf_stored, 16)
            sp.dma_start(nf_sample[0].rearrange("b i h -> (b i) h"), tokc[P - NS:P, QT, :]).then_inc(lf_stored, 16)
            sp.wait_ge(vtok_made, NKV)
            sp.dma_start(nv_prompt[0, 0].rearrange("(t p) g d -> p t (g d)", p=P), v_tok[:, 0:QT, :]).then_inc(kv_stored, 16)
            sp.dma_start(nv_sample[0].rearrange("b i g d -> (b i) (g d)"), v_tok[P - NS:P, QT, :]).then_inc(kv_stored, 16)
            sp.wait_ge(ktok_made, NKV)
            sp.dma_start(nk_prompt[0, 0].rearrange("(t p) g d -> p t (g d)", p=P), k_tok[:, 0:QT, :]).then_inc(kv_stored, 16)
            sp.dma_start(nk_sample[0].rearrange("b i g d -> (b i) (g d)"), k_tok[P - NS:P, QT, :]).then_inc(kv_stored, 16)

            sp.wait_ge(c_stored, 16)

            def load_c_row(i, k):
                if not isinstance(i, int) or 4 * i + k >= 2:
                    sp.wait_ge(max_made, 16 * i + 4 * (k - 1))
                row = c_rows[bass.ds(4 * i + k, 1), :] if not isinstance(i, int) else c_rows[4 * i + k:4 * i + k + 1, :]
                sp.dma_start(c_row[:, k % 2, :], row.rearrange("o s -> (o s)").partition_broadcast(P)
                             ).then_inc(c_loaded[k % 2], 16)

            for k in range(4):
                load_c_row(0, k)
            with sp.Fori(1, NKV) as i:
                for k in range(4):
                    load_c_row(i, k)

            sp.wait_ge(pages_loaded, 16)
            sp.wait_ge(out_evac, NH)
            kp = cache_k[0].rearrange("n p g d -> n p (g d)")
            vp = cache_v[0].rearrange("n p g d -> n p (g d)")

            def load_pages(i, k):
                first = isinstance(i, int)
                regs = [sp.value_load(pages[0:1, bass.ds((2 * i + k) * NPG + p, 1)] if not first else
                                      pages[0:1, (2 * i + k) * NPG + p:(2 * i + k) * NPG + p + 1],
                                      min_val=0, max_val=NPOOL - 1) for p in range(NPG)]
                for p in range(NPG):
                    if not (first and 2 * i + k == 0 and p < 4):
                        sp.wait_ge(k_turned, (2 * i + k) * NPG + (p - 3))
                    sp.dma_start(k_page[:, p % 4, :], kp[bass.ds(regs[p], 1)].rearrange("o p f -> p (o f)")
                                 ).then_inc(page_loaded[p % 4], 16)
                    if p == 0 and not (first and 2 * i + k < 2):
                        sp.wait_ge(s_pv, 2 * i + (k - 1))
                    sp.dma_start(v_page[:, k % 2, p, :], vp[bass.ds(regs[p], 1)].rearrange("o p f -> p (o f)")
                                 ).then_inc(vpage_loaded[k % 2], 16)

            load_pages(0, 0)
            load_pages(0, 1)
            with sp.Fori(1, NB // 2) as i:
                for k in range(2):
                    load_pages(i, k)

            for u in range(U_O + 4, U_O + 6):
                k = u - U_O
                load_unit(u // 4, u % 4, cols(w_o_v, k % 2, (k // 2) * P))
            with sp.Fori(0, 6) as i:
                for k in range(4):
                    u = U_O + 6 + k
                    load_unit(i + u // 4, u % 4, cols(w_o_v, k % 2, i * (2 * P) + (3 + k // 2) * P))
            for u in range(U_O + 30, U_O + 32):
                k = u - U_O
                load_unit(u // 4, u % 4, cols(w_o_v, k % 2, (k // 2) * P))
            with sp.Fori(0, NBLK) as j:
                with sp.Fori(0, FB // 2) as i:
                    for k in range(4):
                        u = U_M + k
                        load_unit(j * (BLK_U // 4) + i + u // 4, u % 4,
                                  cols(w_up_v, k % 2, j * (FB * P) + i * (2 * P) + (k // 2) * P))
                with sp.Fori(0, KC // 4) as i:
                    for k in range(4):
                        u = U_M + 2 * FB + k
                        sp.wait_ge(w_lo_made, j * BLK_U + i * 4 + (u - 3))
                        sp.dma_start(w_raw[:, u % 4, :, :],
                                     w_down_v[:, bass.ds(j * FB, FB), bass.ds(i * (4 * P) + k * P, P)]
                                     ).then_inc(w_loaded[u % 4], 16)
            for c in range(KC):
                sp.wait_ge(y_evac_act, c + 1)
                sp.dma_start(y_prompt[0].rearrange("(t p) d -> p t d", p=P)[:, :, c * P:(c + 1) * P],
                             x_tok[:, 0:QT, c * P:(c + 1) * P]).then_inc(y_stored, 16)
                sp.wait_ge(y_evac_dve, c + 1)
                sp.dma_start(y_sample.rearrange("b i d -> (b i) d")[:, c * P:(c + 1) * P],
                             x_tok[0:NS, QT, c * P:(c + 1) * P]).then_inc(y_stored, 16)
            sp.wait_ge(y_stored, 32 * KC)
            sp.wait_ge(kv_stored, 64)
            sp.wait_ge(lf_stored, 32)

        @block.gpsimd
        def _(pool):
            nc.gpsimd.memset(ident[:], 0.0).then_inc(const_made, 1)
            nc.gpsimd.memset(ones[:], 1.0).then_inc(const_made, 1)
            nc.gpsimd.memset(causal[:], 0.0).then_inc(const_made, 1)
            nc.gpsimd.memset(eps_t[:], EPS).then_inc(const_made, 1)
            pool.wait_ge(const_made, 4)
            nc.gpsimd.affine_select(out=ident[:], in_=ident[:], compare_op=ALU.not_equal, fill=1.0, base=0,
                                    pattern=[[-1, P]], channel_multiplier=1).then_inc(const_made, 1)
            nc.gpsimd.affine_select(out=tri[:], in_=ones[:], compare_op=ALU.is_ge, fill=0.0, base=0,
                                    pattern=[[1, P]], channel_multiplier=-1).then_inc(const_made, 1)
            nc.gpsimd.affine_select(out=causal[:], in_=causal[:], compare_op=ALU.is_ge, fill=BIG, base=0,
                                    pattern=[[-1, P]], channel_multiplier=1).then_inc(const_made, 1)
            nc.gpsimd.affine_select(out=allow[:].rearrange("p b i -> p (b i)").rearrange("p (b i) -> p b i", b=NB),
                                    in_=ones[:, 0:NS].rearrange("p (b i) -> p b i", b=NB),
                                    compare_op=ALU.is_ge, fill=0.0, base=NS - P,
                                    pattern=[[-DS, NB], [0, DS]], channel_multiplier=1).then_inc(const_made, 1)
            pool.wait_ge(const_made, 8)
            nc.gpsimd.affine_select(out=tri4[:].rearrange("p (a c) -> p a c", c=DS),
                                    in_=tri[:].rearrange("p (a c) -> p a c", c=DS),
                                    compare_op=ALU.is_ge, fill=0.0, base=0,
                                    pattern=[[-DS, P // DS], [0, DS]], channel_multiplier=1).then_inc(const_made, 1)
            nc.gpsimd.affine_select(out=allow[:], in_=allow[:], compare_op=ALU.is_ge, fill=0.0, base=P - NS,
                                    pattern=[[DS, NB], [1, DS]], channel_multiplier=-1).then_inc(const_made, 1)
            pool.wait_ge(const_made, 10)
            nc.gpsimd.tensor_scalar(newmask[:], allow[:], -1.0, BIG, ALU.add, ALU.mult).then_inc(const_made, 1)
            pool.dma_start(pages[:], page_table.rearrange("(o b) n -> o (b n)", o=1)).then_inc(pages_loaded, 16)
            pool.wait_ge(const_loaded, 16 * 5)
            nc.gpsimd.tensor_copy(g_kq[:, 0:NKV], g_qk1[:, 0:1].to_broadcast([P, NKV])).then_inc(gains_made, 1)
            nc.gpsimd.tensor_copy(g_kq[:, NKV:NKV + NH], g_qk1[:, 1:2].to_broadcast([P, NH])).then_inc(gains_made, 1)

            def add_squares(c0):
                for c in range(3, KC, 2):
                    pool.wait_ge(sq_made, c0 + c + 1)
                    if c > 3:
                        pool.wait_ge(sq_added_pool, (c0 // KC) * 7 + (c - 3) // 2)
                    nc.gpsimd.tensor_tensor(tmp_c[:, 1, :], tmp_c[:, 1, :], tmp_b[:, 1, :], ALU.add
                                            ).then_inc(sq_added_pool, 1)

            def lo_of_chunks(n0):
                for c in range(1, KC, 2):
                    pool.wait_ge(act_hi_made, n0 + c + 1)
                    nc.gpsimd.tensor_tensor(act_lo[:, c, :], tmp_a[:, 1, :], act_hi[:, c, :], ALU.subtract
                                            ).then_inc(act_lo_pool, 1)

            add_squares(0)
            lo_of_chunks(0)

            pool.wait_ge(head_done, NKV + NH)
            pool.wait_ge(pages_loaded, 16)
            with pool.Fori(0, NB * NPG // 8) as i:
                regs = [pool.value_load(pages[0:1, bass.ds(i * 8 + p, 1)], min_val=0, max_val=NPOOL - 1)
                        for p in range(8)]
                for p in range(8):
                    pool.dma_start(lf_page[:, bass.ds(i * 8 + p, 1), :],
                                   cache_logf[0, bass.ds(regs[p], 1)].rearrange("o p h -> p o h")
                                   ).then_inc(lf_loaded, 16)

            def stage(i, k):
                later = not isinstance(i, int) or 4 * i + k >= 2
                if not later and k == 0:
                    pool.wait_ge(kv_stored, 64)
                if later:
                    pool.wait_ge(score_done, 16 * i + 4 * (k - 1))
                nc.gpsimd.tensor_copy(q_st[:, k % 2, :], kq[:, bass.ds(4 * i + (k + NKV), 1), 0:SEQ].rearrange("p o s -> p (o s)")
                                      if not isinstance(i, int) else kq[:, 4 * i + k + NKV, 0:SEQ]).then_inc(q_staged, 1)
                if later:
                    pool.wait_ge(max_made, 16 * i + 4 * (k - 1))
                pool.wait_ge(c_loaded[k % 2], 32 * i + 16 * (k // 2) + 16)
                nc.gpsimd.tensor_tensor(c_diag[:, k % 2], c_row[:, k % 2].rearrange("p (t s) -> p t s", s=P),
                                        causal[:].unsqueeze(1).to_broadcast([P, QT, P]), ALU.add
                                        ).then_inc(cdiag_made, 1)
                if k == 3:
                    if not isinstance(i, int) or i >= 1:
                        pool.wait_ge(pv_done, 4 * i)
                    nc.gpsimd.tensor_copy(v_st[:], v_tok[:, 0:QT, bass.ds(i * P, P)] if not isinstance(i, int)
                                          else v_tok[:, 0:QT, i * P:(i + 1) * P]).then_inc(v_staged, 1)

            for k in range(4):
                stage(0, k)
            with pool.Fori(1, NKV) as i:
                for k in range(4):
                    stage(i, k)

            pool.wait_ge(csum_chain, 11)
            pool.wait_ge(out_evac, NH)

            def make_bias(i, k):
                b = 2 * i + k
                sl = (lambda t, n=1: t[:, bass.ds(b * n, n)]) if not isinstance(i, int) else \
                    (lambda t, n=1: t[:, b * n:(b + 1) * n])
                if not isinstance(i, int):
                    pool.wait_ge(s_logit, 2 * i + (k - 1))
                out = dbias[:, k % 2].rearrange("p n (h i) -> p n h i", i=DS)
                for p in range(NP9):
                    row = sl(ck, NPG)[:, p, :] if p < NPG else sl(ck_new)[:, 0, :]
                    nc.gpsimd.tensor_tensor(out[:, p], sl(cq)[:, 0], row.unsqueeze(2).to_broadcast([P, NH, DS]),
                                            ALU.subtract).then_inc(dbias_chain, 1)
                pool.wait_ge(dbias_chain, NP9 * 2 * i + NP9 * (k + 1))
                nc.gpsimd.tensor_tensor(out[:, NPG], out[:, NPG],
                                        sl(newmask)[:, 0].unsqueeze(1).to_broadcast([P, NH, DS]), ALU.add
                                        ).then_inc(dbias_made, 1)

            make_bias(0, 0)
            make_bias(0, 1)
            with pool.Fori(1, NB // 2) as i:
                for k in range(2):
                    make_bias(i, k)

            add_squares(KC)
            lo_of_chunks(KC)

        @block.scalar
        def _(act):
            def split(i, k):
                act.wait_ge(w_loaded[k % 4], 16 * i + (k // 4) * 16 + 16)
                if not isinstance(i, int) or 4 * i + k >= 2:
                    act.wait_ge(unit_used, 4 * i + (k - 1))
                nc.scalar.copy(w_hi[:, k % 2], w_raw[:, k % 4]).then_inc(w_hi_made, 1)

            act.wait_ge(const_made, 4)
            for c in range(KC):
                act.wait_ge(xT_made, c + 1)
                if c >= 4:
                    (act.wait_ge(sq_added_dve, (c - 2) // 2) if c % 2 == 0 else
                     act.wait_ge(sq_added_pool, (c - 3) // 2))
                dst = tmp_c[:, c, :] if c < 2 else tmp_b[:, c % 2, :]
                nc.scalar.activation(dst, xT[:, c, :], ACT.Square).then_inc(sq_made, 1)

            def root_of_mean(n):
                act.wait_ge(ssq_ready, n + 1)
                nc.scalar.activation(halves(tmp_c[:, 0, :]), acc(2), ACT.Sqrt, bias=eps_t[:], scale=1.0 / D
                                     ).then_inc(std_ready, 1)

            def hi_of_chunks(n0):
                for c in range(KC):
                    act.wait_ge(scaled, n0 + c + 1)
                    nc.scalar.copy(act_hi[:, c, :], tmp_a[:, c % 2, :]).then_inc(act_hi_made, 1)

            act.wait_ge(gains_made, 3)
            split(0, 0)
            split(0, 1)
            root_of_mean(0)
            hi_of_chunks(0)

            split(0, 2)
            split(0, 3)
            act.wait_ge(unit_used, U_V)
            nc.scalar.copy(halves(fz[:, 0, :]), acc(0, NH)).then_inc(acc_free[0], 1)
            act.wait_ge(f_chain, 3)
            nc.scalar.activation(fe[:, 0, :], fz[:, 1, :], ACT.Exp).then_inc(f_exp, 1)
            act.wait_ge(f_exp, 1)
            nc.scalar.activation(fe[:, 1, :], fe[:, 0, :], ACT.Ln, bias=1.0).then_inc(f_exp, 1)

            def v_tile(i, k):
                u = U_V + 2 * k
                split(i + (u + 2) // 4, (u + 2) % 4)
                split(i + (u + 3) // 4, (u + 3) % 4)
                t = T_V + k
                act.wait_ge(unit_used, 4 * i + u + 2)
                nc.scalar.copy(halves(vT[:, 2 * i + k, :]), acc(t % 2)).then_inc(acc_free[t % 2], 1)

            for i in range(NKV // 2):
                for k in range(2):
                    v_tile(i, k)

            def head_root(m):
                if not (isinstance(m, int) and m == 0):
                    act.wait_ge(head_rec, m)
                act.wait_ge(head_ssq, m + 1)
                nc.scalar.activation(halves(tmp_c[:, 0, :]), acc(2), ACT.Sqrt, bias=eps_t[:], scale=1.0 / HD
                                     ).then_inc(head_std, 1)

            def kq_tile(i, k, u0, t0, m0):
                u, t, m = u0 + 2 * k, t0 + k, m0 + k
                first = isinstance(i, int) and m + 2 * i == 0
                split(i + (u + 2) // 4, (u + 2) % 4)
                if not first:
                    head_root(2 * i + m - 1)
                split(i + (u + 3) // 4, (u + 3) % 4)
                act.wait_ge(unit_used, 4 * i + u + 2)
                if not (isinstance(i, int) and m + 2 * i < 2):
                    act.wait_ge(head_done, 2 * i + m - 1)
                elif first:
                    act.wait_ge(f_chain, 5)
                nc.scalar.copy(halves(tmp_a[:, m % 2, :]), acc(t % 2))
                nc.scalar.activation(halves(tmp_b[:, m % 2, :]), acc(t % 2), ACT.Square).then_inc(acc_free[t % 2], 1)

            for i in range(NKV // 2):
                for k in range(2):
                    kq_tile(i, k, U_K, T_K, 0)
            with act.Fori(0, NH // 2) as i:
                for k in range(2):
                    kq_tile(i, k, U_Q, T_Q, NKV)
            head_root(NKV + NH - 1)

            for g in range(NKV):
                act.wait_ge(kv_turned, 2 * g + 1)
                nc.scalar.copy(v_tok[:, :, g * P:(g + 1) * P],
                               psf[:, 0:TT * P].rearrange("p (t d) -> p t d", d=P)).then_inc(vtok_made, 1)

            def logits(i, k):
                for t in range(QT):
                    w = (t + 1) * P
                    act.wait_ge(score_done, 16 * i + 4 * k + t + 1)
                    if t == 0 and not isinstance(i, int):
                        act.wait_ge(p_turned, 4 * i + (k - 3))
                    bias = tokc[:, TT + t, bass.ds(4 * i + k, 1)] if not isinstance(i, int) else \
                        tokc[:, TT + t, 4 * i + k:4 * i + k + 1]
                    nc.scalar.activation(probs[:, k, t, 0:w], ps[:, t, 0:w], ACT.Identity, bias=bias, scale=SCALE
                                         ).then_inc(logit_made, 1)

            def exps(i, k):
                if not isinstance(i, int) or 4 * i + k >= 2:
                    act.wait_ge(rinv_made, 4 * i + (k - 1))
                for t in range(QT):
                    w = (t + 1) * P
                    act.wait_ge(max_made, 16 * i + 4 * k + t + 1)
                    nc.scalar.activation(probs[:, k, t, 0:w], probs[:, k, t, 0:w], ACT.Exp,
                                         bias=nmax[:, k % 2, t:t + 1], accum_out=rsum[:, k % 2, t:t + 1]
                                         ).then_inc(exp_made, 1)

            def take_pT(i, k):
                act.wait_ge(p_turned, 4 * i + k + 1)
                if not isinstance(i, int) or 4 * i + k >= 2:
                    act.wait_ge(pv_done, 4 * i + (k - 1))
                nc.scalar.copy(pT[:, k % 2, 0:4 * P], ps[:, 4, :]).then_inc(pT_act, 1)

            def take_out(i, k):
                act.wait_ge(pv_done, 4 * i + k + 1)
                dst = kq[:, bass.ds(4 * i + (k + NKV), 1), 0:SEQ].rearrange("p o s -> p (o s)") \
                    if not isinstance(i, int) else kq[:, 4 * i + k + NKV, 0:SEQ]
                nc.scalar.copy(dst, ps[:, 7, :]).then_inc(out_evac, 1)

            act.wait_ge(kv_stored, 64)
            for k in range(4):
                logits(0, k)
                exps(0, k)
                if k >= 2:
                    take_pT(0, k - 2)
                if k >= 3:
                    take_out(0, k - 3)
            with act.Fori(1, NKV) as i:
                for k in range(4):
                    logits(i, k)
                    exps(i, k)
                    take_pT(*((i, k - 2) if k >= 2 else (i - 1, k + 2)))
                    take_out(*((i, k - 3) if k >= 3 else (i - 1, k + 1)))
            take_pT(NKV - 1, 2)
            take_out(NKV - 1, 1)
            take_pT(NKV - 1, 3)
            take_out(NKV - 1, 2)
            take_out(NKV - 1, 3)

            def take_kT(i, k, p):
                act.wait_ge(k_turned, 2 * NPG * i + NPG * k + p + 1)
                if not (isinstance(i, int) and 2 * i + k == 0 and p < 2):
                    act.wait_ge(page_scored, 2 * NPG * i + NPG * k + p - 1)
                nc.scalar.copy(kcT[:, 0, :], ps[:, 0, :]).then_inc(kcT_act, 1)

            def s_exps(i, k):
                act.wait_ge(s_shift, 2 * i + k + 1)
                nc.scalar.activation(sprob[:, k, :, :], sprob[:, k, :, :], ACT.Exp).then_inc(s_exp, 1)

            def s_step(i, k, prev):
                take_kT(i, k, 0)
                take_kT(i, k, 2)
                take_kT(i, k, 4)
                if prev is not None:
                    s_exps(*prev)
                take_kT(i, k, 6)

            s_step(0, 0, None)
            s_step(0, 1, (0, 0))
            with act.Fori(1, NB // 2) as i:
                s_step(i, 0, (i - 1, 1))
                s_step(i, 1, (i, 0))
            s_exps(NB // 2 - 1, 1)

            act.wait_ge(s_out, NB)
            for c in range(KC):
                nc.scalar.copy(act_hi[:, c, :], kq[:, NKV + c, :]).then_inc(mix_hi, 1)

            def o_tile(i, k, start):
                u, t = U_O + 2 * k, T_O + k
                split(i + (u + 2) // 4, (u + 2) % 4)
                split(i + (u + 3) // 4, (u + 3) % 4)
                act.wait_ge(acc_free[t % 2], i + t // 2 + 1)
                if not start:
                    (act.wait_ge(sq_added_dve, 6 + i) if k == 0 else act.wait_ge(sq_added_pool, 6 + i))
                src = xT[:, 2 * i + k, :] if isinstance(i, int) else \
                    xT[:, bass.ds(2 * i + k, 1), :].rearrange("p o t -> p (o t)")
                nc.scalar.activation(tmp_c[:, k, :] if start else tmp_b[:, k, :], src, ACT.Square
                                     ).then_inc(sq_made, 1)

            o_tile(0, 0, True)
            o_tile(0, 1, True)
            with act.Fori(1, KC // 2) as i:
                for k in range(2):
                    o_tile(i, k, False)
            root_of_mean(1)
            hi_of_chunks(KC)

            def up_tile(j, i, k):
                u, t = U_M + 2 * k, T_M + k
                split(j * (BLK_U // 4) + i + (u + 2) // 4, (u + 2) % 4)
                split(j * (BLK_U // 4) + i + (u + 3) // 4, (u + 3) % 4)
                act.wait_ge(unit_used, j * BLK_U + 4 * i + (u + 2))
                nc.scalar.activation(halves(tmp_a[:, k, :]), acc(t % 2), ACT.Relu).then_inc(acc_free[t % 2], 1)
                act.wait_ge(relu_sq, j * FB + 2 * i + (k + 1))
                nc.scalar.copy(u_hi[:, bass.ds(2 * i + k, 1), :].rearrange("p o t -> p (o t)"), tmp_b[:, k, :]
                               ).then_inc(u_hi_made, 1)

            def up_tiles(j):
                with act.Fori(0, FB // 2) as i:
                    for k in range(2):
                        up_tile(j, i, k)

            def down_units(j, i, ks):
                for k in ks:
                    u = U_M + 2 * FB + k
                    split(j * (BLK_U // 4) + i + (u + 2) // 4, (u + 2) % 4)

            with act.Fori(0, NBLK - 1) as j:
                up_tiles(j)
                with act.Fori(0, KC // 4) as i:
                    down_units(j, i, range(4))
            up_tiles(NBLK - 1)
            with act.Fori(0, KC // 4 - 1) as i:
                down_units(NBLK - 1, i, range(4))
            down_units(NBLK - 1, KC // 4 - 1, range(2))

            for c in range(KC):
                act.wait_ge(y_turned, c + 1)
                nc.scalar.copy(x_tok[:, 0:QT, c * P:(c + 1) * P],
                               psf[:, 1024 * (c % 4):1024 * (c % 4) + SEQ].rearrange("p (t d) -> p t d", d=P)
                               ).then_inc(y_evac_act, 1)

        @block.vector
        def _(dve):
            def split(i, k):
                dve.wait_ge(w_hi_made, 4 * i + k + 1)
                nc.vector.tensor_tensor(w_lo[:, k % 2], w_raw[:, k % 4], w_hi[:, k % 2], ALU.subtract
                                        ).then_inc(w_lo_made, 1)

            for k in range(2):
                nc.vector.memset(w_raw[:, k, :, NH:P], 0.0)
            nc.vector.memset(colmax[:], 0.0).then_inc(gains_made, 1)

            for c in range(KC + 1):
                if c < KC:
                    dve.wait_ge(x_turned, c + 1)
                    nc.vector.tensor_copy(xT[:, c, :], psf[:, 1024 * (c % 2):1024 * (c % 2) + T]).then_inc(xT_made, 1)
                if c >= 3 and c % 2 == 1:
                    dve.wait_ge(sq_made, c)
                    nc.vector.tensor_tensor(tmp_c[:, 0, :], tmp_c[:, 0, :], tmp_b[:, 0, :], ALU.add
                                            ).then_inc(sq_added_dve, 1)

            def scale_chunks(n, gain):
                dve.wait_ge(std_ready, n + 1)
                nc.vector.reciprocal(tmp_b[:, 0, :], tmp_c[:, 0, :]).then_inc(rstd_ready, 1)
                dve.wait_ge(rstd_ready, n + 1)
                for c in range(KC):
                    if c >= 2 and c % 2 == 1:
                        dve.wait_ge(act_lo_pool, 8 * n + (c - 1) // 2)
                    nc.vector.scalar_tensor_tensor(out=tmp_a[:, c % 2, :], in0=xT[:, c, :], scalar=gain[:, c:c + 1],
                                                   in1=tmp_b[:, 0, :], op0=ALU.mult, op1=ALU.mult
                                                   ).then_inc(scaled, 1)
                    if c % 2 == 1:
                        dve.wait_ge(act_hi_made, KC * n + c)
                        nc.vector.tensor_tensor(act_lo[:, c - 1, :], tmp_a[:, 0, :], act_hi[:, c - 1, :], ALU.subtract
                                                ).then_inc(act_lo_dve, 1)
                        dve.wait_ge(act_lo_dve, 8 * n + c // 2 + 1)

            split(0, 0)
            split(0, 1)
            dve.wait_ge(const_loaded, 16 * 5)
            scale_chunks(0, g_attn)

            split(0, 2)
            split(0, 3)
            dve.wait_ge(acc_free[0], 1)
            nc.vector.tensor_scalar(fz[:, 0, :], fz[:, 0, :], bf[:, 0:1], None, ALU.add).then_inc(f_chain, 1)
            dve.wait_ge(f_chain, 1)
            nc.vector.tensor_scalar(fz[:, 1, :], fz[:, 0, :], 0.0, -2.0, ALU.max, ALU.mult).then_inc(f_chain, 1)
            dve.wait_ge(f_chain, 2)
            nc.vector.tensor_tensor(fz[:, 1, :], fz[:, 1, :], fz[:, 0, :], ALU.add).then_inc(f_chain, 1)
            dve.wait_ge(f_exp, 2)
            nc.vector.scalar_tensor_tensor(out=lfT[:], in0=fz[:, 0, :], scalar=0.0, in1=fe[:, 1, :],
                                           op0=ALU.min, op1=ALU.subtract).then_inc(f_chain, 1)
            dve.wait_ge(f_chain, 4)
            nc.vector.tensor_tensor_scan(cT[:, 0:SEQ], ones[0:NH, 0:1].to_broadcast([NH, SEQ]), lfT[:, 0:SEQ], 0.0,
                                         ALU.mult, ALU.add).then_inc(f_chain, 1)

            def v_tile(i, k):
                u = U_V + 2 * k
                split(i + (u + 2) // 4, (u + 2) % 4)
                split(i + (u + 3) // 4, (u + 3) % 4)

            v_tile(0, 0)
            dve.wait_ge(f_turned, 1)
            nc.vector.tensor_copy(tokc[:], ps[:, 6, 0:(TT + QT) * NH].rearrange("p (t h) -> p t h", h=NH)
                                  ).then_inc(tokc_made, 1)
            v_tile(0, 1)
            for i in range(1, NKV // 2):
                for k in range(2):
                    v_tile(i, k)

            def norm_head(m, s):
                if not (isinstance(m, int) and m == 0):
                    dve.wait_ge(head_done, m)
                dve.wait_ge(head_std, m + 1)
                nc.vector.reciprocal(tmp_c[:, 1, :], tmp_c[:, 0, :]).then_inc(head_rec, 1)
                dve.wait_ge(head_rec, m + 1)
                dst = kq[:, m, :] if isinstance(m, int) else kq[:, bass.ds(m, 1), :].rearrange("p o t -> p (o t)")
                gain = g_kq[:, m:m + 1] if isinstance(m, int) else g_kq[:, bass.ds(m, 1)]
                nc.vector.scalar_tensor_tensor(out=dst, in0=tmp_a[:, s, :], scalar=gain, in1=tmp_c[:, 1, :],
                                               op0=ALU.mult, op1=ALU.mult).then_inc(head_done, 1)

            def kq_tile(i, k, u0, m0):
                u, m = u0 + 2 * k, m0 + k
                split(i + (u + 2) // 4, (u + 2) % 4)
                if not (isinstance(i, int) and m + 2 * i == 0):
                    norm_head(2 * i + (m - 1), (m - 1) % 2)
                split(i + (u + 3) // 4, (u + 3) % 4)

            dve.wait_ge(gains_made, 3)
            dve.wait_ge(c_stored, 16)
            for i in range(NKV // 2):
                for k in range(2):
                    kq_tile(i, k, U_K, 0)
            with dve.Fori(0, NH // 2) as i:
                for k in range(2):
                    kq_tile(i, k, U_Q, NKV)
            norm_head(NKV + NH - 1, 1)

            for g in range(NKV):
                dve.wait_ge(kv_turned, 2 * g + 2)
                nc.vector.tensor_copy(k_tok[:, :, g * P:(g + 1) * P],
                                      psf[:, 1024:1024 + TT * P].rearrange("p (t d) -> p t d", d=P)
                                      ).then_inc(ktok_made, 1)

            dve.wait_ge(csum_done, 1)
            sums = psf[:, 1024:2048].rearrange("p (b n h) -> p n b h", b=NB, n=NPG)
            nc.vector.tensor_copy(pre[:, 0], sums[:, 0]).then_inc(csum_chain, 1)
            for p in range(1, NPG):
                dve.wait_ge(csum_chain, p)
                nc.vector.tensor_tensor(pre[:, p], pre[:, p - 1], sums[:, p], ALU.add).then_inc(csum_chain, 1)
            dve.wait_ge(csum_chain, NPG)
            inpage = psf[:, 0:1024].rearrange("p (b n h) -> p b n h", b=NB, n=NPG)
            ckv = ck[:].rearrange("p (b n) h -> p b n h", b=NB)
            nc.vector.tensor_copy(ckv[:, :, 0, :], inpage[:, :, 0, :])
            for p in range(1, NPG):
                ins = nc.vector.tensor_tensor(ckv[:, :, p, :], inpage[:, :, p, :], pre[:, p - 1], ALU.add)
            ins.then_inc(csum_chain, 1)
            nc.vector.tensor_tensor(lf_rep[:], tokc[:, QT, :].unsqueeze(1).unsqueeze(3).to_broadcast([P, NB, NH, DS]),
                                    allow[:].unsqueeze(2).to_broadcast([P, NB, NH, DS]), ALU.mult
                                    ).then_inc(csum_chain, 1)
            dve.wait_ge(csum_done, 2)
            nc.vector.tensor_tensor(cq[:], ps[:, 4, :].rearrange("p (b h i) -> p b h i", b=NB, h=NH),
                                    pre[:, NPG - 1].unsqueeze(3).to_broadcast([P, NB, NH, DS]), ALU.add
                                    )
            nc.vector.tensor_tensor(ck_new[:], ps[:, 5, 0:NH].unsqueeze(1).to_broadcast([P, NB, NH]),
                                    pre[:, NPG - 1], ALU.add).then_inc(csum_chain, 1)

            def bias_and_max(i, k):
                dve.wait_ge(cdiag_made, 4 * i + k + 1)
                for t in range(QT):
                    dve.wait_ge(logit_made, 16 * i + 4 * k + t + 1)
                    if t:
                        nc.vector.tensor_tensor(probs[:, k, t, 0:t * P], probs[:, k, t, 0:t * P],
                                                c_row[:, k % 2, 0:t * P], ALU.subtract)
                    ins = nc.vector.tensor_tensor(probs[:, k, t, t * P:(t + 1) * P], probs[:, k, t, t * P:(t + 1) * P],
                                                  c_diag[:, k % 2, t], ALU.subtract)
                    ins.then_inc(s_chain, 1)
                    dve.wait_ge(s_chain, 16 * i + 4 * k + t + 1)
                    nc.vector.tensor_reduce(nmax[:, k % 2, t:t + 1], probs[:, k, t, 0:(t + 1) * P], AX.X, ALU.max,
                                            negate=True).then_inc(max_made, 1)

            def normalise(i, k):
                dve.wait_ge(exp_made, 16 * i + 4 * k + 4)
                nc.vector.reciprocal(rinv[:, k % 2, :], rsum[:, k % 2, :]).then_inc(rinv_made, 1)
                dve.wait_ge(rinv_made, 4 * i + k + 1)
                for t in range(QT):
                    w = (t + 1) * P
                    ins = nc.vector.tensor_scalar(probs[:, k, t, 0:w], probs[:, k, t, 0:w],
                                                  rinv[:, k % 2, t:t + 1], None, ALU.mult)
                ins.then_inc(normed, 1)

            def take_pT(i, k):
                dve.wait_ge(p_turned, 4 * i + k + 1)
                if not isinstance(i, int) or 4 * i + k >= 2:
                    dve.wait_ge(pv_done, 4 * i + (k - 1))
                nc.vector.tensor_copy(pT[:, k % 2, 4 * P:10 * P], psf[:, 5 * 512:5 * 512 + 6 * P]).then_inc(pT_dve, 1)

            dve.wait_ge(kv_stored, 64)
            for k in range(4):
                bias_and_max(0, k)
                if k >= 1:
                    normalise(0, k - 1)
                if k >= 2:
                    take_pT(0, k - 2)
            with dve.Fori(1, NKV) as i:
                for k in range(4):
                    bias_and_max(i, k)
                    normalise(*((i, k - 1) if k >= 1 else (i - 1, 3)))
                    take_pT(*((i, k - 2) if k >= 2 else (i - 1, k + 2)))
            normalise(NKV - 1, 3)
            take_pT(NKV - 1, 2)
            take_pT(NKV - 1, 3)

            def take_kT(i, k, p):
                dve.wait_ge(k_turned, 2 * NPG * i + NPG * k + p + 1)
                if not (isinstance(i, int) and 2 * i + k == 0 and p < 2):
                    dve.wait_ge(page_scored, 2 * NPG * i + NPG * k + p - 1)
                nc.vector.tensor_copy(kcT[:, 1, :], ps[:, 1, :]).then_inc(kcT_dve, 1)

            S_BASE = 4 * NH

            def s_logits(i, k):
                dve.wait_ge(new_scored, 2 * i + k + 1)
                dve.wait_ge(dbias_made, 2 * i + k + 1)
                s0 = 1024 * (1 + k % 2)
                nc.vector.scalar_tensor_tensor(out=sprob[:, k].rearrange("p n q -> p (n q)"), in0=psf[:, s0:s0 + NP9 * QS],
                                               scalar=SCALE, in1=dbias[:, k].rearrange("p n q -> p (n q)"),
                                               op0=ALU.mult, op1=ALU.add).then_inc(s_logit, 1)
                dve.wait_ge(s_logit, 2 * i + k + 1)
                nc.vector.tensor_reduce(colmax[:, 0:QS], sprob[:, k].rearrange("p n q -> p q n"), AX.X, ALU.max
                                        ).then_inc(s_colmax, 1)

            def s_max(i, k):
                dve.wait_ge(s_maxT, 2 * i + k + 1)
                nc.vector.tensor_reduce(m64[:], ps[0:QS, 6, 0:P], AX.X, ALU.max).then_inc(s_chain, 1)
                dve.wait_ge(s_chain, S_BASE + 2 * i + k + 1)
                nc.vector.tensor_scalar(diag[:], ident[0:QS, 0:QS], m64[:, 0:1], None, ALU.mult).then_inc(s_diag, 1)

            def s_subtract(i, k):
                dve.wait_ge(s_maxrow, 2 * i + k + 1)
                nc.vector.tensor_tensor(sprob[:, k], sprob[:, k],
                                        ps[:, 6, P:P + QS].unsqueeze(1).to_broadcast([P, NP9, QS]), ALU.subtract
                                        ).then_inc(s_shift, 1)

            def s_sum(i, k):
                dve.wait_ge(s_exp, 2 * i + k + 1)
                nc.vector.tensor_reduce(colsum[:], sprob[:, k].rearrange("p n q -> p q n"), AX.X, ALU.add
                                        ).then_inc(s_colsum, 1)

            def s_output(i, k):
                if not (isinstance(i, int) and 2 * i + k == 0):
                    dve.wait_ge(s_out, 2 * i + k)
                dve.wait_ge(s_den, 2 * i + k + 1)
                nc.vector.reciprocal(rden[:], ps[:, 6, P + QS:P + 2 * QS]).then_inc(s_rden, 1)
                dve.wait_ge(s_rden, 2 * i + k + 1)
                dve.wait_ge(s_pv, 2 * i + k + 1)
                c0 = SEQ + 2 * DS * i + DS * k
                dst = kq[:, NKV:NKV + NH, c0:c0 + DS] if isinstance(i, int) else kq[:, NKV:NKV + NH, bass.ds(c0, DS)]
                nc.vector.tensor_tensor(dst, ps[:, 7, 0:QS].rearrange("p (h i) -> p h i", i=DS),
                                        rden[:].rearrange("p (h i) -> p h i", i=DS), ALU.mult).then_inc(s_out, 1)

            def s_step(i, k, prev):
                if prev is not None:
                    s_logits(*prev)
                take_kT(i, k, 1)
                if prev is not None:
                    s_max(*prev)
                take_kT(i, k, 3)
                if prev is not None:
                    s_subtract(*prev)
                take_kT(i, k, 5)
                if prev is not None:
                    s_sum(*prev)
                take_kT(i, k, 7)
                if prev is not None:
                    s_output(*prev)

            s_step(0, 0, None)
            s_step(0, 1, (0, 0))
            with dve.Fori(1, NB // 2) as i:
                s_step(i, 0, (i - 1, 1))
                s_step(i, 1, (i, 0))
            last = (NB // 2 - 1, 1)
            s_logits(*last)
            s_max(*last)
            s_subtract(*last)
            s_sum(*last)
            s_output(*last)

            for c in range(KC):
                dve.wait_ge(mix_hi, c + 1)
                nc.vector.tensor_tensor(act_lo[:, c, :], kq[:, NKV + c, :], act_hi[:, c, :], ALU.subtract
                                        ).then_inc(mix_lo, 1)

            def o_tile(i, k, start):
                u, t = U_O + 2 * k, T_O + k
                split(i + (u + 2) // 4, (u + 2) % 4)
                split(i + (u + 3) // 4, (u + 3) % 4)
                dve.wait_ge(unit_used, 4 * i + u + 2)
                dst = xT[:, 2 * i + k, :] if isinstance(i, int) else \
                    xT[:, bass.ds(2 * i + k, 1), :].rearrange("p o t -> p (o t)")
                nc.vector.tensor_tensor(halves(dst), halves(dst), acc(t % 2), ALU.add).then_inc(acc_free[t % 2], 1)
                if k == 0 and not start:
                    dve.wait_ge(sq_made, KC + 2 * i + k + 1)
                    nc.vector.tensor_tensor(tmp_c[:, 0, :], tmp_c[:, 0, :], tmp_b[:, 0, :], ALU.add
                                            ).then_inc(sq_added_dve, 1)

            o_tile(0, 0, True)
            o_tile(0, 1, True)
            with dve.Fori(1, KC // 2) as i:
                for k in range(2):
                    o_tile(i, k, False)
            scale_chunks(1, g_mlp)

            def up_tile(j, i, k):
                u = U_M + 2 * k
                split(j * (BLK_U // 4) + i + (u + 2) // 4, (u + 2) % 4)
                split(j * (BLK_U // 4) + i + (u + 3) // 4, (u + 3) % 4)
                t = T_M + k
                dve.wait_ge(acc_free[t % 2], j * (BLK_T // 2) + i + (t // 2 + 1))
                dve.wait_ge(u_lo_made, j * FB + 2 * i + k)
                nc.vector.tensor_tensor(tmp_b[:, k, :], tmp_a[:, k, :], tmp_a[:, k, :], ALU.mult).then_inc(relu_sq, 1)
                dve.wait_ge(u_hi_made, j * FB + 2 * i + (k + 1))
                sl = lambda t: t[:, bass.ds(2 * i + k, 1), :].rearrange("p o t -> p (o t)")
                nc.vector.tensor_tensor(sl(u_lo), tmp_b[:, k, :], sl(u_hi), ALU.subtract).then_inc(u_lo_made, 1)

            def up_tiles(j):
                with dve.Fori(0, FB // 2) as i:
                    for k in range(2):
                        up_tile(j, i, k)

            def down_tile(j, i, k, ahead=True):
                u, t = U_M + 2 * FB + k, T_M + FB + k
                if ahead:
                    split(j * (BLK_U // 4) + i + (u + 2) // 4, (u + 2) % 4)
                dve.wait_ge(unit_used, j * BLK_U + 4 * i + (u + 1))
                dst = xT[:, bass.ds(4 * i + k, 1), :].rearrange("p o t -> p (o t)") if not isinstance(i, int) \
                    else xT[:, 4 * i + k, :]
                nc.vector.tensor_tensor(halves(dst), halves(dst), acc(t % 2), ALU.add).then_inc(acc_free[t % 2], 1)

            with dve.Fori(0, NBLK - 1) as j:
                up_tiles(j)
                with dve.Fori(0, KC // 4) as i:
                    for k in range(4):
                        down_tile(j, i, k)
            up_tiles(NBLK - 1)
            with dve.Fori(0, KC // 4 - 1) as i:
                for k in range(4):
                    down_tile(NBLK - 1, i, k)
            for k in range(4):
                down_tile(NBLK - 1, KC // 4 - 1, k, ahead=k < 2)

            for c in range(KC):
                dve.wait_ge(y_turned, c + 1)
                nc.vector.tensor_copy(x_tok[0:NS, QT, c * P:(c + 1) * P],
                                      psf[0:NS, 1024 * (c % 4) + SEQ:1024 * (c % 4) + SEQ + P]).then_inc(y_evac_dve, 1)

        @block.tensor
        def _(pe):
            token_tiles = [(t * P, P) for t in range(QT)] + [(SEQ, NS)]

            pe.wait_ge(const_made, 5)
            for c in range(KC):
                if c % 4 == 0:
                    pe.wait_ge(x_loaded[c // 4], 32)
                if c >= 2:
                    pe.wait_ge(xT_made, c - 1)
                for t, (t0, n) in enumerate(token_tiles):
                    o = 1024 * (c % 2) + t0
                    ins = pe.transpose(psf[:, o:o + n], x_tok[0:n, t, c * P:(c + 1) * P], ident[0:n, 0:n])
                ins.then_inc(x_turned, 1)

            def column_sums(srcs, out, signal):
                for a in range(2):
                    for n, src in enumerate(srcs):
                        ins = pe.matmul(out[:, a, :], ones[:], src[:, a * HALF:(a + 1) * HALF],
                                        start=n == 0, stop=n == len(srcs) - 1)
                ins.then_inc(signal, 1)

            def unit(i, k, out, hi, lo, first, last, chunk_waits=None):
                pe.wait_ge(w_lo_made, 4 * i + k + 1)
                s = k % 2
                for c in range(UC):
                    if chunk_waits is not None:
                        chunk_waits(c)
                    for a in range(2):
                        h, l = hi(c)[:, a * HALF:(a + 1) * HALF], lo(c)[:, a * HALF:(a + 1) * HALF]
                        pe.matmul(out[:, a, :], w_hi[:, s, c, :], l, start=first and c == 0, stop=False)
                        pe.matmul(out[:, a, :], w_hi[:, s, c, :], h, start=False, stop=False)
                    for a in range(2):
                        h = hi(c)[:, a * HALF:(a + 1) * HALF]
                        ins = pe.matmul(out[:, a, :], w_lo[:, s, c, :], h, start=False, stop=last and c == UC - 1)
                ins.then_inc(unit_used, 1)
                return ins

            def model_tile(i, u, t, waits=None, between=None, wait_acc=True):
                if wait_acc:
                    pe.wait_ge(acc_free[t % 2], i + t // 2)
                out = acc(t % 2)
                for half in range(2):
                    uu = u + half
                    unit(i + uu // 4, uu % 4, out, lambda c: act_hi[:, half * UC + c, :],
                         lambda c: act_lo[:, half * UC + c, :], half == 0, half == 1,
                         None if waits is None else (lambda c: waits(half * UC + c)))
                    if half == 0 and between is not None:
                        between()

            def norm_waits(n):
                def waits(c):
                    (pe.wait_ge(act_lo_dve, 8 * n + c // 2 + 1) if c % 2 == 0 else
                     pe.wait_ge(act_lo_pool, 8 * n + c // 2 + 1))
                return waits

            pe.wait_ge(sq_added_dve, 7)
            pe.wait_ge(sq_added_pool, 7)
            column_sums([tmp_c[:, 0, :], tmp_c[:, 1, :]], acc(2), ssq_ready)

            model_tile(0, 0, 0, waits=norm_waits(0), wait_acc=False)

            def turn_gates():
                pe.wait_ge(f_chain, 5)
                for n in range(TT + QT):
                    t0 = n * P if n < QT else (LAST if n == QT else (n - TT) * P)
                    src = (lfT if n < TT else cT)[:, t0:t0 + P]
                    ins = pe.transpose(ps[:, 6, n * NH:(n + 1) * NH], src, ident[0:NH, 0:NH])
                ins.then_inc(f_turned, 1)

            for i in range(NKV // 2):
                for k in range(2):
                    u, t = U_V + 2 * k, T_V + k
                    model_tile(i, u, t, wait_acc=not (i == 0 and k == 0), between=turn_gates if i + k == 0 else None)

            def head_sums(i, m):
                t, s = T_K + m, m % 2
                pe.wait_ge(acc_free[t % 2], i + t // 2 + 1)
                if not (isinstance(i, int) and 2 * i + m == 0):
                    pe.wait_ge(head_std, 2 * i + m)
                column_sums([tmp_b[:, s, :]], acc(2), head_ssq)

            def kq_tile(i, k, u0, t0, m0):
                u, t, m = u0 + 2 * k, t0 + k, m0 + k
                first = isinstance(i, int) and m + 2 * i == 0
                model_tile(i, u, t, between=None if first else (lambda: head_sums(i, m - 1)))

            for i in range(NKV // 2):
                for k in range(2):
                    kq_tile(i, k, U_K, T_K, 0)
            with pe.Fori(0, NH // 2) as i:
                for k in range(2):
                    kq_tile(i, k, U_Q, T_Q, NKV)
            head_sums(0, NKV + NH - 1)

            pe.wait_ge(acc_free[0], T_O // 2)
            pe.wait_ge(acc_free[1], T_O // 2)
            for g in range(NKV):
                for which, (src, made, off) in enumerate(((vT, vtok_made, 0), (kq, ktok_made, 1024))):
                    if g:
                        pe.wait_ge(made, g)
                    for t in range(TT):
                        t0 = t * P if t < QT else LAST
                        ins = pe.transpose(psf[:, off + t * P:off + (t + 1) * P], src[:, g, t0:t0 + P], ident[:])
                    ins.then_inc(kv_turned, 1)

            pe.wait_ge(lf_loaded, 16 * NB * NPG)
            pe.wait_ge(vtok_made, NKV)
            pe.wait_ge(ktok_made, NKV)
            lf_flat = lf_page[:].rearrange("p n h -> p (n h)")
            for a in range(2):
                pe.matmul(ps[:, a, :], tri[:], lf_flat[:, 512 * a:512 * a + 512], start=True, stop=True)
                ins = pe.matmul(ps[:, 2 + a, :], ones[:], lf_flat[:, 512 * a:512 * a + 512], start=True, stop=True)
            ins.then_inc(csum_done, 1)
            pe.wait_ge(csum_chain, 10)
            pe.wait_ge(head_std, NKV + NH)
            pe.matmul(ps[:, 4, :], ones[:], lf_rep[:].rearrange("p b h i -> p (b h i)"), start=True, stop=True)
            pe.matmul(ps[:, 5, 0:NH], tri4[:], tokc[:, QT, :], start=True, stop=True).then_inc(csum_done, 1)
            pe.wait_ge(csum_chain, 11)

            def scores(i, k):
                pe.wait_ge(q_staged, 4 * i + k + 1)
                if not (isinstance(i, int) and 4 * i + k == 0):
                    pe.wait_ge(logit_made, 16 * i + 4 * k)
                for t in range(QT):
                    w = (t + 1) * P
                    keys = kq[:, i, 0:w] if isinstance(i, int) else kq[:, bass.ds(i, 1), 0:w].rearrange("p o s -> p (o s)")
                    pe.matmul(ps[:, t, 0:w], q_st[:, k % 2, t * P:(t + 1) * P], keys, start=True, stop=True
                              ).then_inc(score_done, 1)

            PT_AT = [0, 4 * P, 8 * P, 7 * P]

            def turn_probs(i, k):
                pe.wait_ge(normed, 4 * i + k + 1)
                if not (isinstance(i, int) and 4 * i + k == 0):
                    pe.wait_ge(pT_act, 4 * i + k)
                    pe.wait_ge(pT_dve, 4 * i + k)
                for j in range(QT):
                    for t in range(j, QT):
                        o = 4 * 512 + PT_AT[j] + (t - j) * P
                        ins = pe.transpose(psf[:, o:o + P], probs[:, k, t, j * P:(j + 1) * P], ident[:])
                ins.then_inc(p_turned, 1)

            def values(i, k):
                pe.wait_ge(v_staged, i + 1)
                pe.wait_ge(pT_act, 4 * i + k + 1)
                pe.wait_ge(pT_dve, 4 * i + k + 1)
                if not (isinstance(i, int) and 4 * i + k == 0):
                    pe.wait_ge(out_evac, 4 * i + k)
                for j in range(QT):
                    w = (QT - j) * P
                    ins = pe.matmul(ps[:, 7, j * P:SEQ], v_st[:, j, :], pT[:, k % 2, PT_AT[j]:PT_AT[j] + w],
                                    start=j == 0, stop=j == QT - 1, skip_group_check=True)
                ins.then_inc(pv_done, 1)

            for k in range(4):
                scores(0, k)
                if k >= 2:
                    turn_probs(0, k - 2)
                if k >= 3:
                    values(0, k - 3)
            with pe.Fori(1, NKV) as i:
                for k in range(4):
                    scores(i, k)
                    turn_probs(*((i, k - 2) if k >= 2 else (i - 1, k + 2)))
                    values(*((i, k - 3) if k >= 3 else (i - 1, k + 1)))
            turn_probs(NKV - 1, 2)
            values(NKV - 1, 1)
            turn_probs(NKV - 1, 3)
            values(NKV - 1, 2)
            values(NKV - 1, 3)
            pe.wait_ge(out_evac, NH)

            def queries(i, k, g):
                c0 = SEQ + 2 * DS * i + DS * k
                return kq[:, NKV + GRP * g:NKV + GRP * (g + 1), c0:c0 + DS] if isinstance(i, int) else \
                    kq[:, NKV + GRP * g:NKV + GRP * (g + 1), bass.ds(c0, DS)]

            def turn_page(i, k, p):
                if not (isinstance(i, int) and 2 * i + k == 0 and p < 2):
                    (pe.wait_ge(kcT_act, NPG * i + NPG // 2 * k + p // 2) if p % 2 == 0 else
                     pe.wait_ge(kcT_dve, NPG * i + NPG // 2 * k + p // 2))
                pe.wait_ge(page_loaded[p % 4], 64 * i + 32 * k + 16 * (p // 4) + 16)
                for g in range(NKV):
                    ins = pe.transpose(ps[:, p % 2, g * P:(g + 1) * P], k_page[:, p % 4, g * P:(g + 1) * P], ident[:])
                ins.then_inc(k_turned, 1)

            def score_page(i, k, p):
                (pe.wait_ge(kcT_act, NPG * i + NPG // 2 * k + p // 2 + 1) if p % 2 == 0 else
                 pe.wait_ge(kcT_dve, NPG * i + NPG // 2 * k + p // 2 + 1))
                if p == 0 and not isinstance(i, int):
                    pe.wait_ge(s_logit, 2 * i + (k - 1))
                for g in range(NKV):
                    o = 1024 * (1 + k) + p * QS + g * GRP * DS
                    ins = pe.matmul(psf[:, o:o + GRP * DS], kcT[:, p % 2, g * P:(g + 1) * P], queries(i, k, g),
                                    start=True, stop=True)
                ins.then_inc(page_scored, 1)

            def score_new(i, k):
                for g in range(NKV):
                    o = 1024 * (1 + k) + NPG * QS + g * GRP * DS
                    ins = pe.matmul(psf[:, o:o + GRP * DS], kq[:, g, LAST:T], queries(i, k, g), start=True, stop=True)
                ins.then_inc(new_scored, 1)

            def max_turn(i, k):
                pe.wait_ge(s_colmax, 2 * i + k + 1)
                pe.transpose(ps[:, 6, 0:P], colmax[:], ident[:]).then_inc(s_maxT, 1)

            def max_rows(i, k):
                pe.wait_ge(s_diag, 2 * i + k + 1)
                pe.matmul(ps[:, 6, P:P + QS], ones[0:QS, :], diag[:], start=True, stop=True).then_inc(s_maxrow, 1)

            def denominators(i, k):
                pe.wait_ge(s_colsum, 2 * i + k + 1)
                pe.matmul(ps[:, 6, P + QS:P + 2 * QS], ones[:], colsum[:], start=True, stop=True).then_inc(s_den, 1)

            def s_values(i, k):
                pe.wait_ge(vpage_loaded[k], 16 * NPG * i + 16 * NPG)
                if not (isinstance(i, int) and 2 * i + k == 0):
                    pe.wait_ge(s_out, 2 * i + k)
                for g in range(NKV):
                    o = g * GRP * DS
                    for p in range(NP9):
                        v = v_page[:, k, p, g * P:(g + 1) * P] if p < NPG else v_tok[:, QT, g * P:(g + 1) * P]
                        ins = pe.matmul(ps[:, 7, o:o + GRP * DS], v, sprob[:, k, p, o:o + GRP * DS],
                                        start=p == 0, stop=p == NPG)
                ins.then_inc(s_pv, 1)

            def s_step(i, k, prev):
                turn_page(i, k, 0)
                for p in range(NPG):
                    if p + 1 < NPG:
                        turn_page(i, k, p + 1)
                    score_page(i, k, p)
                    if prev is not None and p == 1:
                        max_turn(*prev)
                    if prev is not None and p == 3:
                        max_rows(*prev)
                score_new(i, k)
                if prev is not None:
                    denominators(*prev)
                    s_values(*prev)

            s_step(0, 0, None)
            s_step(0, 1, (0, 0))
            with pe.Fori(1, NB // 2) as i:
                s_step(i, 0, (i - 1, 1))
                s_step(i, 1, (i, 0))
            last = (NB // 2 - 1, 1)
            max_turn(*last)
            max_rows(*last)
            denominators(*last)
            s_values(*last)

            for k in range(2):
                u, t = U_O + 2 * k, T_O + k
                model_tile(0, u, t, waits=(lambda c: pe.wait_ge(mix_lo, c + 1)) if k == 0 else None)
            with pe.Fori(1, KC // 2) as i:
                for k in range(2):
                    u, t = U_O + 2 * k, T_O + k
                    model_tile(i, u, t)
            pe.wait_ge(sq_added_dve, 14)
            pe.wait_ge(sq_added_pool, 14)
            column_sums([tmp_c[:, 0, :], tmp_c[:, 1, :]], acc(2), ssq_ready)

            def up_tiles(j, i, waits=None):
                for k in range(2):
                    u, t = U_M + 2 * k, T_M + k
                    pe.wait_ge(acc_free[t % 2], j * (BLK_T // 2) + i + t // 2)
                    for half in range(2):
                        uu = u + half
                        unit(j * (BLK_U // 4) + i + uu // 4, uu % 4, acc(t % 2),
                             lambda c: act_hi[:, half * UC + c, :], lambda c: act_lo[:, half * UC + c, :],
                             half == 0, half == 1,
                             None if waits is None or k else (lambda c: waits(half * UC + c)))

            def down_tiles(j, i, waits=None):
                for k in range(4):
                    u, t = U_M + 2 * FB + k, T_M + FB + k
                    pe.wait_ge(acc_free[t % 2], j * (BLK_T // 2) + 2 * i + t // 2)
                    unit(j * (BLK_U // 4) + i + u // 4, u % 4, acc(t % 2), lambda c: u_hi[:, c, :],
                         lambda c: u_lo[:, c, :], True, True, waits if k == 0 else None)

            def mlp_block(j, first_waits=None):
                if first_waits is not None:
                    up_tiles(j, 0, first_waits)
                with pe.Fori(1 if first_waits is not None else 0, FB // 2) as i:
                    up_tiles(j, i)
                down_tiles(j, 0, lambda c: pe.wait_ge(u_lo_made, FB * j + c + 1))
                with pe.Fori(1, KC // 4) as i:
                    down_tiles(j, i)

            mlp_block(0, norm_waits(1))
            with pe.Fori(1, NBLK) as j:
                mlp_block(j)

            pe.wait_ge(acc_free[0], (T_M + NBLK * BLK_T) // 2 + 1)
            pe.wait_ge(acc_free[1], (T_M + NBLK * BLK_T) // 2)
            for c in range(KC):
                if c >= 4:
                    pe.wait_ge(y_evac_act, c - 3)
                    pe.wait_ge(y_evac_dve, c - 3)
                o = 1024 * (c % 4)
                for t in range(QT):
                    pe.transpose(psf[:, o + t * P:o + (t + 1) * P], xT[:, c, t * P:(t + 1) * P], ident[:])
                pe.transpose(psf[0:NS, o + SEQ:o + SEQ + P], xT[:, c, SEQ:T], ident[:]).then_inc(y_turned, 1)


_INS = ["x_prompt", "x_sample", "cache_k", "cache_v", "cache_logf", "page_table", "attn_norm", "w_qkv", "q_norm",
        "k_norm", "w_fgate", "b_fgate", "w_o", "mlp_norm", "w_up", "w_down"]


def kernel(**inputs):
    import numpy as _np
    import concourse.bacc as _bacc
    from concourse import mybir as _mybir
    from concourse.bass_utils import run_bass_kernel_spmd as _run

    nc = _bacc.Bacc("TRN2", target_bir_lowering=False, num_devices=1)
    arrays, args = {}, []
    for name in _INS:
        a = _np.ascontiguousarray(inputs[name])
        arrays[f"in_{name}"] = a
        args.append(nc.dram_tensor(f"in_{name}", a.shape, _mybir.dt.from_np(a.dtype), kind="ExternalInput").ap())
    xp, xs = inputs["x_prompt"].shape, inputs["x_sample"].shape
    depth, _, _, nkv, hd = inputs["cache_k"].shape
    nfox, _, _, nh = inputs["cache_logf"].shape
    outs = [xp, xs, (depth, *xp[:2], nkv, hd), (depth, *xp[:2], nkv, hd), (nfox, *xp[:2], nh),
            (depth, *xs[:2], nkv, hd), (depth, *xs[:2], nkv, hd), (nfox, *xs[:2], nh)]
    for i, shape in enumerate(outs):
        args.append(nc.dram_tensor(f"out_{i}", shape, F32, kind="ExternalOutput").ap())
    fox_layer(nc, *args)
    r = _run(nc, [arrays], core_ids=[0])
    return tuple(r.results[0][f"out_{i}"] for i in range(len(outs)))
```

```python
from contextlib import ExitStack

import concourse.bass as bass
from concourse import mybir

F32 = mybir.dt.float32
F32R = mybir.dt.float32r
I32 = mybir.dt.int32
ACT = mybir.ActivationFunctionType
ALU = mybir.AluOpType
AX = mybir.AxisListType

P = 128
BIG = 1.0e30


def fox_layer(nc, x_prompt, x_sample, cache_k, cache_v, cache_logf, page_table, attn_norm, w_qkv, q_norm,
              k_norm, w_fgate, b_fgate, w_o, mlp_norm, w_up, w_down,
              y_prompt, y_sample, nk_prompt, nv_prompt, nf_prompt, nk_sample, nv_sample, nf_sample):
    _, SEQ, D = x_prompt.shape
    NB, DS, _ = x_sample.shape
    _, NPOOL, PAGE, NKV, HD = cache_k.shape
    NH = cache_logf.shape[3]
    NPG = page_table.shape[1]
    DFF = w_up.shape[2]
    GRP = NH // NKV
    NS = NB * DS
    T = SEQ + NS
    HALF = T // 2
    QT = SEQ // P
    TT = QT + 1
    KC = D // P
    UC = 8
    FB = UC
    NBLK = DFF // P // FB
    KVC = NKV * HD
    SCALE = float(HD) ** -0.5
    EPS = 1e-6
    PAST = NPG * PAGE
    R = 32
    RQ = GRP * DS
    assert PAGE == P and HD == P and SEQ == 4 * P and HALF * 4 <= 2048 and NPG == 8 and KC == 2 * UC
    assert NH == 16 and GRP == 4 and NB == 8 and NKV * R == P and NPG * NH == P

    with ExitStack() as ctx:
        def sem(name):
            return ctx.enter_context(nc.semaphore(name))

        base = -(-nc.sbuf_base // 64) * 64
        top = [base]

        def at(name, shape, dt, offset=None):
            n = 4
            for s in shape[1:]:
                n *= s
            if offset is None:
                offset = top[0]
                top[0] += -(-n // 64) * 64
            return nc.alloc_sbuf_tensor_at(name, shape, dt, offset=offset), offset, offset + n

        xT, _, _ = at("xT", [P, KC, T], F32)
        act_hi, act_at, _ = at("act_hi", [P, KC, T], F32R)
        act_lo, _, act_end = at("act_lo", [P, KC, T], F32R)
        kq, kq_at, _ = at("kq", [P, NKV + NH, T], F32)
        vT, vT_at, _ = at("vT", [P, NKV, T], F32)
        w_raw, _, _ = at("w_raw", [P, 4, UC, P], F32)
        w_hi, _, _ = at("w_hi", [P, 2, UC, P], F32R)
        w_lo, _, _ = at("w_lo", [P, 2, UC, P], F32R)
        tmp_a, tmp_a_at, _ = at("tmp_a", [P, 2, T], F32)
        tmp_b, tmp_b_at, _ = at("tmp_b", [P, 2, T], F32)
        tmp_c, tmp_c_at, _ = at("tmp_c", [P, 2, T], F32)
        ident, _, _ = at("ident", [P, P], F32)
        ones, _, _ = at("ones", [P, P], F32)
        tri, _, _ = at("tri", [P, P], F32)
        earlier, _, _ = at("earlier", [P, P], F32)
        causal, _, _ = at("causal", [P, P], F32)
        expand, _, _ = at("expand", [NH, P], F32)
        own, _, _ = at("own", [P, NB, NB], F32)
        tok_sel, _, _ = at("tok_sel", [P, DS], F32)
        tok_mask, _, _ = at("tok_mask", [P, DS], F32)
        eps_t, _, _ = at("eps_t", [P, 1], F32)
        g_attn, _, _ = at("g_attn", [P, KC], F32)
        g_mlp, _, _ = at("g_mlp", [P, KC], F32)
        g_kq, _, _ = at("g_kq", [P, NKV + NH], F32)
        g_qk1, _, _ = at("g_qk1", [P, 2], F32)
        bf, _, _ = at("bf", [NH, 1], F32)
        pages, _, _ = at("pages", [1, NB * NPG], I32)
        tokc, _, _ = at("tokc", [P, TT + QT, NH], F32)
        nmax, _, _ = at("nmax", [P, 2, QT], F32)
        rsum, _, _ = at("rsum", [P, 2, QT], F32)
        rinv, _, _ = at("rinv", [P, 2, QT], F32)
        pg_off, _, _ = at("pg_off", [P, NB], F32)
        new_sum, _, _ = at("new_sum", [P, NB, DS], F32)
        new_key, _, _ = at("new_key", [P, NB, DS], F32)
        new_q, _, _ = at("new_q", [P, NB], F32)
        s_ckn, _, _ = at("s_ckn", [P, 2, DS], F32)
        s_cq, _, _ = at("s_cq", [P, 2, 1], F32)
        s_nmax, _, _ = at("s_nmax", [P, 2, 1], F32)
        s_nbias, _, _ = at("s_nbias", [P, 2, 1], F32)
        s_rsum, _, _ = at("s_rsum", [P, 2, 1], F32)
        s_rinv, _, _ = at("s_rinv", [P, 2, 1], F32)
        p_new, _, _ = at("p_new", [P, NS], F32)
        p_newT, _, _ = at("p_newT", [NS, P], F32)
        s_outr, _, _ = at("s_outr", [P, P], F32)
        k_pack, _, _ = at("k_pack", [P, 2, NKV, DS], F32)
        q_pack, _, end = at("q_pack", [P, 2, NKV, R], F32)
        assert end <= nc.sbuf_usable_end, (end, nc.sbuf_usable_end)

        x_tok, _, e = at("x_tok", [P, TT, D], F32, act_at)
        assert e <= act_end
        u_hi, _, e = at("u_hi", [P, FB, T], F32R, kq_at)
        u_lo, _, e = at("u_lo", [P, FB, T], F32R, e)
        fz, _, _ = at("fz", [NH, 2, T], F32, tmp_a_at)
        fe, _, _ = at("fe", [NH, 2, T], F32, tmp_b_at)
        lfT, _, o = at("lfT", [NH, T], F32, tmp_c_at)
        cT, _, _ = at("cT", [NH, T], F32, o)
        v_tok, _, o = at("v_tok", [P, TT, KVC], F32, act_at)
        scr = o
        k_tok, _, _ = at("k_tok", [P, TT, KVC], F32, scr)
        probs, _, o = at("probs", [P, 4, QT, SEQ], F32, scr)
        pT, _, o = at("pT", [P, 2, 10 * P], F32, o)
        c_row, _, o = at("c_row", [P, 2, SEQ], F32, o)
        c_diag, _, o = at("c_diag", [P, 2, QT, P], F32, o)
        q_st, _, o = at("q_st", [P, 2, SEQ], F32, o)
        v_st, _, o = at("v_st", [P, QT, P], F32, o)
        assert o <= act_end
        v_page, _, o = at("v_page", [P, 2, NPG, KVC], F32, scr)
        kcT, _, o = at("kcT", [P, 2, NKV, 4 * P], F32, o)
        sprob, _, o = at("sprob", [P, 2, PAST + NS], F32, o)
        assert o <= act_end
        k_page, _, o = at("k_page", [P, 4, KVC], F32, vT_at)
        assert o <= vT_at + 4 * NKV * T
        c_dec, _, o = at("c_dec", [P, 2, PAST], F32, tmp_a_at)
        assert o <= tmp_c_at
        spT, _, _ = at("spT", [P, NPG, P], F32, tmp_c_at)
        lf_page, _, _ = at("lf_page", [P, NB * NPG, NH], F32, kq_at + 4 * T * (NKV + NH - 4))
        c_pg, _, _ = at("c_pg", [P, NB, PAGE], F32, kq_at + 4 * T * (NKV + NH - 2))
        ps = ctx.enter_context(nc.psum_tensor("ps", [P, 8, 512], F32))
        psf = ps[:, :, :].rearrange("p b n -> p (b n)")
        c_rows = nc.dram_tensor("c_rows", [NH, SEQ], F32).ap()
        c_cache = nc.dram_tensor("c_cache", [NB, NH, NPG, PAGE], F32).ap()

        def halves(ap):
            return ap.rearrange("p (a n) -> p a n", a=2)

        def acc(slot, rows=P):
            return ps[0:rows, 2 * slot:2 * slot + 2, 0:HALF]

        const_made = sem("const_made")
        const_loaded = sem("const_loaded")
        gains_made = sem("gains_made")
        sel_made = sem("sel_made")
        pages_loaded = sem("pages_loaded")
        x_loaded = [sem(f"x_loaded{i}") for i in range(4)]
        x_turned = sem("x_turned")
        xT_made = sem("xT_made")
        sq_made = sem("sq_made")
        sq_added_dve = sem("sq_added_dve")
        sq_added_pool = sem("sq_added_pool")
        ssq_ready = sem("ssq_ready")
        std_ready = sem("std_ready")
        rstd_ready = sem("rstd_ready")
        scaled = sem("scaled")
        act_hi_made = sem("act_hi_made")
        act_lo_dve = sem("act_lo_dve")
        act_lo_pool = sem("act_lo_pool")
        w_loaded = [sem(f"w_loaded{i}") for i in range(4)]
        w_hi_made = sem("w_hi_made")
        w_lo_made = sem("w_lo_made")
        unit_used = sem("unit_used")
        acc_free = [sem("acc_free0"), sem("acc_free1")]
        f_chain = sem("f_chain")
        f_exp = sem("f_exp")
        f_turned = sem("f_turned")
        tokc_made = sem("tokc_made")
        c_stored = sem("c_stored")
        head_ssq = sem("head_ssq")
        head_std = sem("head_std")
        head_rec = sem("head_rec")
        head_done = sem("head_done")
        v_evac = sem("v_evac")
        lf_loaded = sem("lf_loaded")
        kv_turned = sem("kv_turned")
        vtok_made = sem("vtok_made")
        ktok_made = sem("ktok_made")
        kv_stored = sem("kv_stored")
        lf_stored = sem("lf_stored")
        csum_done = sem("csum_done")
        csum_evac = sem("csum_evac")
        new_chain = sem("new_chain")
        new_spread = sem("new_spread")
        q_staged = sem("q_staged")
        v_staged = sem("v_staged")
        bias_sub = sem("bias_sub")
        c_loaded = [sem("c_loaded0"), sem("c_loaded1")]
        cdiag_made = sem("cdiag_made")
        score_done = sem("score_done")
        logit_made = sem("logit_made")
        max_made = sem("max_made")
        exp_made = sem("exp_made")
        rinv_made = sem("rinv_made")
        normed = sem("normed")
        p_turned = sem("p_turned")
        pT_act = sem("pT_act")
        pT_dve = sem("pT_dve")
        pv_done = sem("pv_done")
        out_evac = sem("out_evac")
        page_loaded = [sem(f"page_loaded{i}") for i in range(4)]
        vpage_loaded = [sem("vpage_loaded0"), sem("vpage_loaded1")]
        k_turned = sem("k_turned")
        kcT_act = sem("kcT_act")
        kcT_dve = sem("kcT_dve")
        new_scored = sem("new_scored")
        q_packed = sem("q_packed")
        c_cached = sem("c_cached")
        cdec_loaded = [sem("cdec_loaded0"), sem("cdec_loaded1")]
        cdec_zeroed = sem("cdec_zeroed")
        half_scored = sem("half_scored")
        s_small = sem("s_small")
        s_logit = sem("s_logit")
        s_max = sem("s_max")
        s_bias = sem("s_bias")
        s_exp = sem("s_exp")
        s_pnew = sem("s_pnew")
        s_turned = sem("s_turned")
        spT_made = sem("spT_made")
        p_newT_made = sem("p_newT_made")
        s_pv = sem("s_pv")
        s_scaled = sem("s_scaled")
        s_outT = sem("s_outT")
        s_out = sem("s_out")
        mix_hi = sem("mix_hi")
        mix_lo = sem("mix_lo")
        relu_made = sem("relu_made")
        relu_sq = sem("relu_sq")
        u_hi_made = sem("u_hi_made")
        u_lo_made = sem("u_lo_made")
        y_turned = sem("y_turned")
        y_evac_act = sem("y_evac_act")
        y_evac_dve = sem("y_evac_dve")
        y_stored = sem("y_stored")

        U_V, U_K, U_Q, U_O, U_M = 2, 10, 18, 50, 82
        T_V, T_K, T_Q, T_O, T_M = 1, 5, 9, 25, 41
        BLK_U, BLK_T = 32, 24
        assert U_M + BLK_U * NBLK == 338

        w_f_v = w_fgate[0].rearrange("(k p) n -> p k n", p=P)
        w_qkv_v = w_qkv[0].rearrange("(k p) n -> p k n", p=P)
        w_o_v = w_o[0].rearrange("(k p) n -> p k n", p=P)
        w_up_v = w_up[0].rearrange("(k p) n -> p k n", p=P)
        w_down_v = w_down[0].rearrange("(k p) n -> p k n", p=P)

        block = ctx.enter_context(nc.Block())

        @block.sync
        def _(sp):
            def load_unit(i, k, src):
                if not isinstance(i, int) or 4 * i + k >= 4:
                    sp.wait_ge(w_lo_made, 4 * i + (k - 3))
                sp.dma_start(w_raw[:, k % 4, :, 0:src.shape[2]], src).then_inc(w_loaded[k % 4], 16)

            def cols(view, half, col):
                return view[:, half * UC:(half + 1) * UC, col:col + P] if isinstance(col, int) else \
                    view[:, half * UC:(half + 1) * UC, bass.ds(col, P)]

            gw = D // 4
            for n in range(4):
                sp.dma_start(x_tok[:, 0:QT, n * gw:(n + 1) * gw],
                             x_prompt[0].rearrange("(t p) d -> p t d", p=P)[:, :, n * gw:(n + 1) * gw]
                             ).then_inc(x_loaded[n], 16)
                sp.dma_start(x_tok[0:NS, QT, n * gw:(n + 1) * gw],
                             x_sample.rearrange("b i d -> (b i) d")[:, n * gw:(n + 1) * gw]
                             ).then_inc(x_loaded[n], 16)
            load_unit(0, 0, w_f_v[:, 0:UC, :])
            load_unit(0, 1, w_f_v[:, UC:KC, :])
            load_unit(0, 2, cols(w_qkv_v, 0, D + KVC))
            load_unit(0, 3, cols(w_qkv_v, 1, D + KVC))
            with nc.allow_non_contiguous_dma(reason="small vectors, one element a partition"):
                sp.dma_start(g_attn[:], attn_norm[0].rearrange("(c p) -> p c", p=P)).then_inc(const_loaded, 16)
                sp.dma_start(g_mlp[:], mlp_norm[0].rearrange("(c p) -> p c", p=P)).then_inc(const_loaded, 16)
                sp.dma_start(g_qk1[:, 0:1], k_norm.rearrange("o p -> p o")).then_inc(const_loaded, 16)
                sp.dma_start(g_qk1[:, 1:2], q_norm.rearrange("o p -> p o")).then_inc(const_loaded, 16)
                sp.dma_start(bf[:], b_fgate.rearrange("o h -> h o")).then_inc(const_loaded, 16)

            load_unit(1, 0, cols(w_qkv_v, 0, D + KVC + P))
            load_unit(1, 1, cols(w_qkv_v, 1, D + KVC + P))
            for n in range(2, NKV):
                for half in range(2):
                    u = U_V + 2 * n + half
                    load_unit(u // 4, u % 4, cols(w_qkv_v, half, D + KVC + n * P))
            for n in range(NKV):
                for half in range(2):
                    u = U_K + 2 * n + half
                    load_unit(u // 4, u % 4, cols(w_qkv_v, half, D + n * P))
                if n == 0:
                    sp.wait_ge(f_chain, 5)
                    sp.dma_start(c_rows, cT[:, 0:SEQ]).then_inc(c_stored, 16)
            with sp.Fori(0, NH // 2) as i:
                for k in range(4):
                    load_unit(i + (U_Q + k) // 4, (U_Q + k) % 4, cols(w_qkv_v, k % 2, i * (2 * P) + (k // 2) * P))
            for u in range(U_O, U_O + 4):
                k = u - U_O
                load_unit(u // 4, u % 4, cols(w_o_v, k % 2, (k // 2) * P))

            sp.wait_ge(tokc_made, 1)
            sp.dma_start(nf_prompt[0, 0].rearrange("(t p) h -> p t h", p=P), tokc[:, 0:QT, :]).then_inc(lf_stored, 16)
            sp.dma_start(nf_sample[0].rearrange("b i h -> (b i) h"), tokc[0:NS, QT, :]).then_inc(lf_stored, 16)
            sp.wait_ge(vtok_made, 2 * NKV)
            sp.dma_start(nv_prompt[0, 0].rearrange("(t p) g d -> p t (g d)", p=P), v_tok[:, 0:QT, :]).then_inc(kv_stored, 16)
            sp.dma_start(nv_sample[0].rearrange("b i g d -> (b i) (g d)"), v_tok[0:NS, QT, :]).then_inc(kv_stored, 16)
            sp.wait_ge(ktok_made, 2 * NKV)
            sp.dma_start(nk_prompt[0, 0].rearrange("(t p) g d -> p t (g d)", p=P), k_tok[:, 0:QT, :]).then_inc(kv_stored, 16)
            sp.dma_start(nk_sample[0].rearrange("b i g d -> (b i) (g d)"), k_tok[0:NS, QT, :]).then_inc(kv_stored, 16)

            sp.wait_ge(c_stored, 16)

            def load_c_row(i, k):
                if not isinstance(i, int) or 4 * i + k >= 2:
                    sp.wait_ge(max_made, 16 * i + 4 * (k - 1))
                row = c_rows[bass.ds(4 * i + k, 1), :] if not isinstance(i, int) else c_rows[4 * i + k:4 * i + k + 1, :]
                sp.dma_start(c_row[:, k % 2, :], row.rearrange("o s -> (o s)").partition_broadcast(P)
                             ).then_inc(c_loaded[k % 2], 16)

            for k in range(4):
                load_c_row(0, k)
            with sp.Fori(1, NKV) as i:
                for k in range(4):
                    load_c_row(i, k)

            sp.wait_ge(pages_loaded, 16)
            kp = cache_k[0].rearrange("n p g d -> n p (g d)")
            vp = cache_v[0].rearrange("n p g d -> n p (g d)")

            def load_pages(i, k):
                first = isinstance(i, int)
                regs = [sp.value_load(pages[0:1, bass.ds((2 * i + k) * NPG + p, 1)] if not first else
                                      pages[0:1, (2 * i + k) * NPG + p:(2 * i + k) * NPG + p + 1],
                                      min_val=0, max_val=NPOOL - 1) for p in range(NPG)]

                def load_v(p):
                    sp.dma_start(v_page[:, k % 2, p, :], vp[bass.ds(regs[p], 1)].rearrange("o p f -> p (o f)")
                                 ).then_inc(vpage_loaded[k % 2], 16)

                for p in range(NPG):
                    if not (first and 2 * i + k == 0 and p < 4):
                        sp.wait_ge(k_turned, (2 * i + k) * NPG + (p - 3))
                    sp.dma_start(k_page[:, p % 4, :], kp[bass.ds(regs[p], 1)].rearrange("o p f -> p (o f)")
                                 ).then_inc(page_loaded[p % 4], 16)
                    if first and 2 * i + k == 0:
                        if p == 3:
                            sp.wait_ge(out_evac, NH)
                    elif p == 0 and not first:
                        sp.wait_ge(s_pv, 2 * i + (k - 1))
                    if not (first and 2 * i + k == 0):
                        load_v(p)
                    elif p >= 4:
                        load_v(p - 4)
                        load_v(p)

            load_pages(0, 0)
            load_pages(0, 1)
            with sp.Fori(1, NB // 2) as i:
                for k in range(2):
                    load_pages(i, k)

            for u in range(U_O + 4, U_O + 6):
                k = u - U_O
                load_unit(u // 4, u % 4, cols(w_o_v, k % 2, (k // 2) * P))
            with sp.Fori(0, 6) as i:
                for k in range(4):
                    u = U_O + 6 + k
                    load_unit(i + u // 4, u % 4, cols(w_o_v, k % 2, i * (2 * P) + (3 + k // 2) * P))
            for u in range(U_O + 30, U_O + 32):
                k = u - U_O
                load_unit(u // 4, u % 4, cols(w_o_v, k % 2, (k // 2) * P))
            with sp.Fori(0, NBLK) as j:
                with sp.Fori(0, FB // 2) as i:
                    for k in range(4):
                        u = U_M + k
                        load_unit(j * (BLK_U // 4) + i + u // 4, u % 4,
                                  cols(w_up_v, k % 2, j * (FB * P) + i * (2 * P) + (k // 2) * P))
                with sp.Fori(0, KC // 4) as i:
                    for k in range(4):
                        u = U_M + 2 * FB + k
                        sp.wait_ge(w_lo_made, j * BLK_U + i * 4 + (u - 3))
                        sp.dma_start(w_raw[:, u % 4, :, :],
                                     w_down_v[:, bass.ds(j * FB, FB), bass.ds(i * (4 * P) + k * P, P)]
                                     ).then_inc(w_loaded[u % 4], 16)
            for c in range(KC):
                sp.wait_ge(y_evac_act, c + 1)
                sp.dma_start(y_prompt[0].rearrange("(t p) d -> p t d", p=P)[:, :, c * P:(c + 1) * P],
                             x_tok[:, 0:QT, c * P:(c + 1) * P]).then_inc(y_stored, 16)
                sp.wait_ge(y_evac_dve, c + 1)
                sp.dma_start(y_sample.rearrange("b i d -> (b i) d")[:, c * P:(c + 1) * P],
                             x_tok[0:NS, QT, c * P:(c + 1) * P]).then_inc(y_stored, 16)
            sp.wait_ge(y_stored, 32 * KC)
            sp.wait_ge(kv_stored, 64)
            sp.wait_ge(lf_stored, 32)

        @block.gpsimd
        def _(pool):
            nc.gpsimd.memset(ident[:], 0.0).then_inc(const_made, 1)
            nc.gpsimd.memset(ones[:], 1.0).then_inc(const_made, 1)
            nc.gpsimd.memset(causal[:], 0.0).then_inc(const_made, 1)
            nc.gpsimd.memset(eps_t[:], EPS).then_inc(const_made, 1)
            pool.wait_ge(const_made, 4)
            nc.gpsimd.affine_select(out=ident[:], in_=ident[:], compare_op=ALU.not_equal, fill=1.0, base=0,
                                    pattern=[[-1, P]], channel_multiplier=1).then_inc(const_made, 1)
            nc.gpsimd.affine_select(out=tri[:], in_=ones[:], compare_op=ALU.is_ge, fill=0.0, base=0,
                                    pattern=[[1, P]], channel_multiplier=-1).then_inc(const_made, 1)
            nc.gpsimd.affine_select(out=causal[:], in_=causal[:], compare_op=ALU.is_ge, fill=BIG, base=0,
                                    pattern=[[-1, P]], channel_multiplier=1).then_inc(const_made, 1)
            nc.gpsimd.memset(earlier[:], 0.0).then_inc(const_made, 1)
            nc.gpsimd.affine_select(out=own[:], in_=ones[:, 0:NB * NB].rearrange("p (a b) -> p a b", a=NB),
                                    compare_op=ALU.is_equal, fill=0.0, base=0,
                                    pattern=[[1, NB], [-1, NB]], channel_multiplier=0).then_inc(const_made, 1)
            nc.gpsimd.affine_select(out=expand[:].rearrange("p (g h i) -> p g h i", g=NKV, i=DS),
                                    in_=ones[0:NH, :].rearrange("p (g h i) -> p g h i", g=NKV, i=DS),
                                    compare_op=ALU.is_equal, fill=0.0, base=0,
                                    pattern=[[-GRP, NKV], [-1, R // DS], [0, DS]], channel_multiplier=1
                                    ).then_inc(const_made, 1)
            nc.gpsimd.affine_select(out=s_outr[:].rearrange("p (i a) -> p i a", i=DS),
                                    in_=ones[:].rearrange("p (i a) -> p i a", i=DS),
                                    compare_op=ALU.is_equal, fill=0.0, base=0,
                                    pattern=[[-1, DS], [-DS, P // DS]], channel_multiplier=1
                                    ).then_inc(const_made, 1)
            n_const = 11
            for d in range(1, NPG):
                pool.wait_ge(const_made, n_const)
                nc.gpsimd.affine_select(out=earlier[:], in_=earlier[:], compare_op=ALU.not_equal, fill=1.0,
                                        base=d * NH, pattern=[[-1, P]], channel_multiplier=1
                                        ).then_inc(const_made, 1)
                n_const += 1
            pool.dma_start(pages[:], page_table.rearrange("(o b) n -> o (b n)", o=1)).then_inc(pages_loaded, 16)
            pool.wait_ge(const_loaded, 16 * 5)
            nc.gpsimd.tensor_copy(g_kq[:, 0:NKV], g_qk1[:, 0:1].to_broadcast([P, NKV])).then_inc(gains_made, 1)
            nc.gpsimd.tensor_copy(g_kq[:, NKV:NKV + NH], g_qk1[:, 1:2].to_broadcast([P, NH])).then_inc(gains_made, 1)

            pool.wait_ge(pages_loaded, 16)

            def load_cached_gates(a, b):
                with pool.Fori(a, b) as i:
                    regs = [pool.value_load(pages[0:1, bass.ds(i * NPG + p, 1)], min_val=0, max_val=NPOOL - 1)
                            for p in range(NPG)]
                    for p in range(NPG):
                        pool.dma_start(lf_page[:, bass.ds(i * NPG + p, 1), :],
                                       cache_logf[0, bass.ds(regs[p], 1)].rearrange("o p h -> p o h")
                                       ).then_inc(lf_loaded, 16)

            def add_squares(c0):
                for c in range(3, KC, 2):
                    pool.wait_ge(sq_made, c0 + c + 1)
                    if c > 3:
                        pool.wait_ge(sq_added_pool, (c0 // KC) * 7 + (c - 3) // 2)
                    nc.gpsimd.tensor_tensor(tmp_c[:, 1, :], tmp_c[:, 1, :], tmp_b[:, 1, :], ALU.add
                                            ).then_inc(sq_added_pool, 1)

            def lo_of_chunks(n0):
                for c in range(1, KC, 2):
                    pool.wait_ge(act_hi_made, n0 + c + 1)
                    nc.gpsimd.tensor_tensor(act_lo[:, c, :], tmp_a[:, 1, :], act_hi[:, c, :], ALU.subtract
                                            ).then_inc(act_lo_pool, 1)

            load_cached_gates(0, 1)
            add_squares(0)
            lo_of_chunks(0)
            load_cached_gates(1, NB)

            pool.wait_ge(csum_evac, 3)
            for p in range(NPG):
                pool.dma_start(c_cache[:, :, p, :].rearrange("b h p -> h b p"), c_pg[p * NH:(p + 1) * NH]
                               ).then_inc(c_cached, 16)

            def stage(i, k):
                later = not isinstance(i, int) or 4 * i + k >= 2
                if not later and k == 0:
                    pool.wait_ge(kv_stored, 64)
                if later:
                    pool.wait_ge(score_done, 16 * i + 4 * (k - 1))
                nc.gpsimd.tensor_copy(q_st[:, k % 2, :], kq[:, bass.ds(4 * i + (k + NKV), 1), 0:SEQ].rearrange("p o s -> p (o s)")
                                      if not isinstance(i, int) else kq[:, 4 * i + k + NKV, 0:SEQ]).then_inc(q_staged, 1)
                if later:
                    pool.wait_ge(max_made, 16 * i + 4 * (k - 1))
                pool.wait_ge(c_loaded[k % 2], 32 * i + 16 * (k // 2) + 16)
                nc.gpsimd.tensor_tensor(c_diag[:, k % 2], c_row[:, k % 2].rearrange("p (t s) -> p t s", s=P),
                                        causal[:].unsqueeze(1).to_broadcast([P, QT, P]), ALU.add
                                        ).then_inc(cdiag_made, 1)
                if k == 3:
                    if not isinstance(i, int) or i >= 1:
                        pool.wait_ge(pv_done, 4 * i)
                    nc.gpsimd.tensor_copy(v_st[:], v_tok[:, 0:QT, bass.ds(i * P, P)] if not isinstance(i, int)
                                          else v_tok[:, 0:QT, i * P:(i + 1) * P]).then_inc(v_staged, 1)

            for k in range(4):
                stage(0, k)
            with pool.Fori(1, NKV) as i:
                for k in range(4):
                    stage(i, k)

            pool.wait_ge(c_cached, 16 * NPG)
            pool.wait_ge(cdec_zeroed, 1)

            def pack(i, k):
                c0 = SEQ + 2 * DS * i + DS * k
                if not isinstance(i, int):
                    pool.wait_ge(new_scored, 2 * i + (k - 1))
                src = kq[:, NKV:NKV + NH, c0:c0 + DS] if isinstance(i, int) else kq[:, NKV:NKV + NH, bass.ds(c0, DS)]
                nc.gpsimd.tensor_copy(q_pack[:, k, :, 0:RQ].rearrange("p g (h i) -> p g h i", i=DS),
                                      src.rearrange("p (g h) i -> p g h i", g=NKV))
                nc.gpsimd.tensor_copy(k_pack[:, k], kq[:, 0:NKV, c0:c0 + DS] if isinstance(i, int) else
                                      kq[:, 0:NKV, bass.ds(c0, DS)]).then_inc(q_packed, 1)
                if not isinstance(i, int):
                    pool.wait_ge(s_logit, 4 * i + 2 * (k - 1))
                for g in range(NKV):
                    rows = c_cache[2 * i + k, g * GRP:(g + 1) * GRP].rearrange("h n p -> h (n p)") \
                        if isinstance(i, int) else \
                        c_cache[bass.ds(2 * i + k, 1), g * GRP:(g + 1) * GRP].rearrange("o h n p -> (o h) (n p)")
                    pool.dma_start(c_dec[g * R:g * R + RQ, k, :],
                                   rows.unsqueeze(1).to_broadcast([GRP, DS, PAST])).then_inc(cdec_loaded[k], 16)

            pack(0, 0)
            pack(0, 1)
            with pool.Fori(1, NB // 2) as i:
                for k in range(2):
                    pack(i, k)

            add_squares(KC)
            lo_of_chunks(KC)

        @block.scalar
        def _(act):
            def split(i, k):
                act.wait_ge(w_loaded[k % 4], 16 * i + (k // 4) * 16 + 16)
                if not isinstance(i, int) or 4 * i + k >= 2:
                    act.wait_ge(unit_used, 4 * i + (k - 1))
                nc.scalar.copy(w_hi[:, k % 2], w_raw[:, k % 4]).then_inc(w_hi_made, 1)

            act.wait_ge(const_made, 4)
            for c in range(KC):
                act.wait_ge(xT_made, c + 1)
                if c >= 4:
                    (act.wait_ge(sq_added_dve, (c - 2) // 2) if c % 2 == 0 else
                     act.wait_ge(sq_added_pool, (c - 3) // 2))
                dst = tmp_c[:, c, :] if c < 2 else tmp_b[:, c % 2, :]
                nc.scalar.activation(dst, xT[:, c, :], ACT.Square).then_inc(sq_made, 1)

            def root_of_mean(n):
                act.wait_ge(ssq_ready, n + 1)
                nc.scalar.activation(halves(tmp_c[:, 0, :]), acc(2), ACT.Sqrt, bias=eps_t[:], scale=1.0 / D
                                     ).then_inc(std_ready, 1)

            def hi_of_chunks(n0):
                for c in range(KC):
                    act.wait_ge(scaled, n0 + c + 1)
                    nc.scalar.copy(act_hi[:, c, :], tmp_a[:, c % 2, :]).then_inc(act_hi_made, 1)

            act.wait_ge(gains_made, 3)
            split(0, 0)
            split(0, 1)
            root_of_mean(0)
            hi_of_chunks(0)

            split(0, 2)
            split(0, 3)
            act.wait_ge(unit_used, U_V)
            nc.scalar.copy(halves(fz[:, 0, :]), acc(0, NH)).then_inc(acc_free[0], 1)
            act.wait_ge(f_chain, 3)
            nc.scalar.activation(fe[:, 0, :], fz[:, 1, :], ACT.Exp).then_inc(f_exp, 1)
            act.wait_ge(f_exp, 1)
            nc.scalar.activation(fe[:, 1, :], fe[:, 0, :], ACT.Ln, bias=1.0).then_inc(f_exp, 1)

            def v_tile(i, k):
                u = U_V + 2 * k
                split(i + (u + 2) // 4, (u + 2) % 4)
                split(i + (u + 3) // 4, (u + 3) % 4)
                t = T_V + k
                act.wait_ge(unit_used, 4 * i + u + 2)
                nc.scalar.copy(halves(vT[:, 2 * i + k, :]), acc(t % 2)).then_inc(acc_free[t % 2], 1)

            for i in range(NKV // 2):
                for k in range(2):
                    v_tile(i, k)

            def head_root(m):
                if not (isinstance(m, int) and m == 0):
                    act.wait_ge(head_rec, m)
                act.wait_ge(head_ssq, m + 1)
                nc.scalar.activation(halves(tmp_c[:, 0, :]), acc(2), ACT.Sqrt, bias=eps_t[:], scale=1.0 / HD
                                     ).then_inc(head_std, 1)

            def kq_tile(i, k, u0, t0, m0):
                u, t, m = u0 + 2 * k, t0 + k, m0 + k
                first = isinstance(i, int) and m + 2 * i == 0
                split(i + (u + 2) // 4, (u + 2) % 4)
                if not first:
                    head_root(2 * i + m - 1)
                split(i + (u + 3) // 4, (u + 3) % 4)
                act.wait_ge(unit_used, 4 * i + u + 2)
                if not (isinstance(i, int) and m + 2 * i < 2):
                    act.wait_ge(head_done, 2 * i + m - 1)
                elif first:
                    act.wait_ge(f_chain, 5)
                nc.scalar.copy(halves(tmp_a[:, m % 2, :]), acc(t % 2))
                nc.scalar.activation(halves(tmp_b[:, m % 2, :]), acc(t % 2), ACT.Square).then_inc(acc_free[t % 2], 1)

            for i in range(NKV // 2):
                for k in range(2):
                    kq_tile(i, k, U_K, T_K, 0)
            with act.Fori(0, NH // 2) as i:
                for k in range(2):
                    kq_tile(i, k, U_Q, T_Q, NKV)
            head_root(NKV + NH - 1)

            for g in range(NKV):
                act.wait_ge(kv_turned, 2 * g + 1)
                nc.scalar.copy(v_tok[:, 0:QT, g * P:(g + 1) * P],
                               psf[:, 0:SEQ].rearrange("p (t d) -> p t d", d=P)).then_inc(vtok_made, 1)
                nc.scalar.copy(v_tok[0:NS, QT, g * P:(g + 1) * P], psf[0:NS, SEQ:SEQ + P]).then_inc(vtok_made, 1)

            def logits(i, k):
                for t in range(QT):
                    w = (t + 1) * P
                    act.wait_ge(score_done, 16 * i + 4 * k + t + 1)
                    if t == 0 and not isinstance(i, int):
                        act.wait_ge(p_turned, 4 * i + (k - 3))
                    bias = tokc[:, TT + t, bass.ds(4 * i + k, 1)] if not isinstance(i, int) else \
                        tokc[:, TT + t, 4 * i + k:4 * i + k + 1]
                    nc.scalar.activation(probs[:, k, t, 0:w], ps[:, t, 0:w], ACT.Identity, bias=bias, scale=SCALE
                                         ).then_inc(logit_made, 1)

            def exps(i, k):
                if not isinstance(i, int) or 4 * i + k >= 2:
                    act.wait_ge(rinv_made, 4 * i + (k - 1))
                for t in range(QT):
                    w = (t + 1) * P
                    act.wait_ge(max_made, 16 * i + 4 * k + t + 1)
                    nc.scalar.activation(probs[:, k, t, 0:w], probs[:, k, t, 0:w], ACT.Exp,
                                         bias=nmax[:, k % 2, t:t + 1], accum_out=rsum[:, k % 2, t:t + 1]
                                         ).then_inc(exp_made, 1)

            def take_pT(i, k):
                act.wait_ge(p_turned, 4 * i + k + 1)
                if not isinstance(i, int) or 4 * i + k >= 2:
                    act.wait_ge(pv_done, 4 * i + (k - 1))
                nc.scalar.copy(pT[:, k % 2, 0:4 * P], ps[:, 4, :]).then_inc(pT_act, 1)

            def take_out(i, k):
                act.wait_ge(pv_done, 4 * i + k + 1)
                dst = kq[:, bass.ds(4 * i + (k + NKV), 1), 0:SEQ].rearrange("p o s -> p (o s)") \
                    if not isinstance(i, int) else kq[:, 4 * i + k + NKV, 0:SEQ]
                nc.scalar.copy(dst, ps[:, 7, :]).then_inc(out_evac, 1)

            act.wait_ge(kv_stored, 64)
            for k in range(4):
                logits(0, k)
                exps(0, k)
                if k >= 2:
                    take_pT(0, k - 2)
                if k >= 3:
                    take_out(0, k - 3)
            with act.Fori(1, NKV) as i:
                for k in range(4):
                    logits(i, k)
                    exps(i, k)
                    take_pT(*((i, k - 2) if k >= 2 else (i - 1, k + 2)))
                    take_out(*((i, k - 3) if k >= 3 else (i - 1, k + 1)))
            take_pT(NKV - 1, 2)
            take_out(NKV - 1, 1)
            take_pT(NKV - 1, 3)
            take_out(NKV - 1, 2)
            take_out(NKV - 1, 3)

            def take_kT(i, k, p):
                act.wait_ge(k_turned, 2 * NPG * i + NPG * k + p + 1)
                if p % 4 == 0 and not (isinstance(i, int) and 2 * i + k == 0):
                    act.wait_ge(half_scored, 4 * i + 2 * k + p // 4 - 1)
                nc.scalar.copy(kcT[:, p // 4, :, (p % 4) * P:(p % 4 + 1) * P],
                               ps[:, 0, :].rearrange("p (g n) -> p g n", g=NKV)).then_inc(kcT_act, 1)

            def s_exps(i, k):
                act.wait_ge(s_bias, 2 * i + k + 1)
                if not isinstance(i, int) or 2 * i + k >= 2:
                    act.wait_ge(s_scaled, 2 * i + (k - 1))
                nc.scalar.activation(sprob[:, k, 0:PAST + DS], sprob[:, k, 0:PAST + DS], ACT.Exp,
                                     bias=s_nbias[:, k], accum_out=s_rsum[:, k]).then_inc(s_exp, 1)

            def take_spT(i, k):
                act.wait_ge(s_turned, 2 * i + k + 1)
                if not (isinstance(i, int) and 2 * i + k == 0):
                    act.wait_ge(s_pv, 2 * i + k)
                nc.scalar.copy(spT[:].rearrange("p n r -> p (n r)"), psf[:, 5 * 512:7 * 512]).then_inc(spT_made, 1)

            def s_step(i, k, prev):
                take_kT(i, k, 0)
                take_kT(i, k, 2)
                if prev is not None:
                    s_exps(*prev)
                take_kT(i, k, 4)
                if prev is not None:
                    take_spT(*prev)
                take_kT(i, k, 6)

            s_step(0, 0, None)
            s_step(0, 1, (0, 0))
            s_step(1, 0, (0, 1))
            s_step(1, 1, (1, 0))
            with act.Fori(2, NB // 2) as i:
                s_step(i, 0, (i - 1, 1))
                s_step(i, 1, (i, 0))
            s_exps(NB // 2 - 1, 1)
            take_spT(NB // 2 - 1, 1)

            act.wait_ge(s_out, NB)
            for c in range(KC):
                nc.scalar.copy(act_hi[:, c, :], kq[:, NKV + c, :]).then_inc(mix_hi, 1)

            def o_tile(i, k, start):
                u, t = U_O + 2 * k, T_O + k
                split(i + (u + 2) // 4, (u + 2) % 4)
                split(i + (u + 3) // 4, (u + 3) % 4)
                act.wait_ge(acc_free[t % 2], i + t // 2 + 1)
                if not start:
                    (act.wait_ge(sq_added_dve, 6 + i) if k == 0 else act.wait_ge(sq_added_pool, 6 + i))
                src = xT[:, 2 * i + k, :] if isinstance(i, int) else \
                    xT[:, bass.ds(2 * i + k, 1), :].rearrange("p o t -> p (o t)")
                nc.scalar.activation(tmp_c[:, k, :] if start else tmp_b[:, k, :], src, ACT.Square
                                     ).then_inc(sq_made, 1)

            o_tile(0, 0, True)
            o_tile(0, 1, True)
            with act.Fori(1, KC // 2) as i:
                for k in range(2):
                    o_tile(i, k, False)
            root_of_mean(1)
            hi_of_chunks(KC)

            def up_tile(j, i, k):
                u, t = U_M + 2 * k, T_M + k
                split(j * (BLK_U // 4) + i + (u + 2) // 4, (u + 2) % 4)
                split(j * (BLK_U // 4) + i + (u + 3) // 4, (u + 3) % 4)
                act.wait_ge(unit_used, j * BLK_U + 4 * i + (u + 2))
                nc.scalar.activation(halves(tmp_a[:, k, :]), acc(t % 2), ACT.Relu).then_inc(acc_free[t % 2], 1)
                act.wait_ge(relu_sq, j * FB + 2 * i + (k + 1))
                nc.scalar.copy(u_hi[:, bass.ds(2 * i + k, 1), :].rearrange("p o t -> p (o t)"), tmp_b[:, k, :]
                               ).then_inc(u_hi_made, 1)

            def up_tiles(j):
                with act.Fori(0, FB // 2) as i:
                    for k in range(2):
                        up_tile(j, i, k)

            def down_units(j, i, ks):
                for k in ks:
                    u = U_M + 2 * FB + k
                    split(j * (BLK_U // 4) + i + (u + 2) // 4, (u + 2) % 4)

            with act.Fori(0, NBLK - 1) as j:
                up_tiles(j)
                with act.Fori(0, KC // 4) as i:
                    down_units(j, i, range(4))
            up_tiles(NBLK - 1)
            with act.Fori(0, KC // 4 - 1) as i:
                down_units(NBLK - 1, i, range(4))
            down_units(NBLK - 1, KC // 4 - 1, range(2))

            for c in range(KC):
                act.wait_ge(y_turned, c + 1)
                nc.scalar.copy(x_tok[:, 0:QT, c * P:(c + 1) * P],
                               psf[:, 1024 * (c % 4):1024 * (c % 4) + SEQ].rearrange("p (t d) -> p t d", d=P)
                               ).then_inc(y_evac_act, 1)

        @block.vector
        def _(dve):
            def split(i, k):
                dve.wait_ge(w_hi_made, 4 * i + k + 1)
                nc.vector.tensor_tensor(w_lo[:, k % 2], w_raw[:, k % 4], w_hi[:, k % 2], ALU.subtract
                                        ).then_inc(w_lo_made, 1)

            for k in range(2):
                nc.vector.memset(w_raw[:, k, :, NH:P], 0.0)
            nc.vector.memset(q_pack[:], 0.0).then_inc(gains_made, 1)

            for c in range(KC + 1):
                if c < KC:
                    dve.wait_ge(x_turned, c + 1)
                    nc.vector.tensor_copy(xT[:, c, :], psf[:, 1024 * (c % 2):1024 * (c % 2) + T]).then_inc(xT_made, 1)
                if c >= 3 and c % 2 == 1:
                    dve.wait_ge(sq_made, c)
                    nc.vector.tensor_tensor(tmp_c[:, 0, :], tmp_c[:, 0, :], tmp_b[:, 0, :], ALU.add
                                            ).then_inc(sq_added_dve, 1)

            def scale_chunks(n, gain):
                dve.wait_ge(std_ready, n + 1)
                nc.vector.reciprocal(tmp_b[:, 0, :], tmp_c[:, 0, :]).then_inc(rstd_ready, 1)
                dve.wait_ge(rstd_ready, n + 1)
                for c in range(KC):
                    if c >= 2 and c % 2 == 1:
                        dve.wait_ge(act_lo_pool, 8 * n + (c - 1) // 2)
                    nc.vector.scalar_tensor_tensor(out=tmp_a[:, c % 2, :], in0=xT[:, c, :], scalar=gain[:, c:c + 1],
                                                   in1=tmp_b[:, 0, :], op0=ALU.mult, op1=ALU.mult
                                                   ).then_inc(scaled, 1)
                    if c % 2 == 1:
                        dve.wait_ge(act_hi_made, KC * n + c)
                        nc.vector.tensor_tensor(act_lo[:, c - 1, :], tmp_a[:, 0, :], act_hi[:, c - 1, :], ALU.subtract
                                                ).then_inc(act_lo_dve, 1)
                        dve.wait_ge(act_lo_dve, 8 * n + c // 2 + 1)

            dve.wait_ge(const_made, 11)
            nc.vector.tensor_reduce(tok_sel[:], s_outr[:].rearrange("p (i a) -> p i a", i=DS), AX.X, ALU.add
                                    ).then_inc(sel_made, 1)
            nc.vector.memset(tok_mask[:, 0:1], 0.0).then_inc(sel_made, 1)
            for n in range(1, DS):
                dve.wait_ge(sel_made, n + 1)
                nc.vector.scalar_tensor_tensor(out=tok_mask[:, n:n + 1], in0=tok_sel[:, n - 1:n], scalar=BIG,
                                               in1=tok_mask[:, n - 1:n], op0=ALU.mult, op1=ALU.add
                                               ).then_inc(sel_made, 1)
            split(0, 0)
            split(0, 1)
            dve.wait_ge(const_loaded, 16 * 5)
            scale_chunks(0, g_attn)

            split(0, 2)
            split(0, 3)
            dve.wait_ge(acc_free[0], 1)
            nc.vector.tensor_scalar(fz[:, 0, :], fz[:, 0, :], bf[:, 0:1], None, ALU.add).then_inc(f_chain, 1)
            dve.wait_ge(f_chain, 1)
            nc.vector.tensor_scalar(fz[:, 1, :], fz[:, 0, :], 0.0, -2.0, ALU.max, ALU.mult).then_inc(f_chain, 1)
            dve.wait_ge(f_chain, 2)
            nc.vector.tensor_tensor(fz[:, 1, :], fz[:, 1, :], fz[:, 0, :], ALU.add).then_inc(f_chain, 1)
            dve.wait_ge(f_exp, 2)
            nc.vector.scalar_tensor_tensor(out=lfT[:], in0=fz[:, 0, :], scalar=0.0, in1=fe[:, 1, :],
                                           op0=ALU.min, op1=ALU.subtract).then_inc(f_chain, 1)
            dve.wait_ge(f_chain, 4)
            new_lf = lfT[:, SEQ:T].rearrange("p (b i) -> p b i", i=DS)
            new_c = cT[:, SEQ:T].rearrange("p (b i) -> p b i", i=DS)
            nc.vector.tensor_copy(new_c[:, :, 0], new_lf[:, :, 0]).then_inc(new_chain, 1)
            for n in range(1, DS):
                dve.wait_ge(new_chain, n)
                nc.vector.tensor_tensor(new_c[:, :, n], new_c[:, :, n - 1], new_lf[:, :, n], ALU.add
                                        ).then_inc(new_chain, 1)
            nc.vector.tensor_tensor_scan(cT[:, 0:SEQ], ones[0:NH, 0:1].to_broadcast([NH, SEQ]), lfT[:, 0:SEQ], 0.0,
                                         ALU.mult, ALU.add).then_inc(f_chain, 1)

            def v_tile(i, k):
                u = U_V + 2 * k
                split(i + (u + 2) // 4, (u + 2) % 4)
                split(i + (u + 3) // 4, (u + 3) % 4)

            v_tile(0, 0)
            dve.wait_ge(f_turned, 1)
            nc.vector.tensor_copy(tokc[:, 0:QT], ps[:, 6, 0:QT * NH].rearrange("p (t h) -> p t h", h=NH))
            nc.vector.tensor_copy(tokc[0:NS, QT], ps[0:NS, 6, QT * NH:TT * NH])
            nc.vector.tensor_copy(tokc[:, TT:], ps[:, 6, TT * NH:(TT + QT) * NH].rearrange("p (t h) -> p t h", h=NH)
                                  ).then_inc(tokc_made, 1)
            nc.vector.tensor_copy(new_sum[:].rearrange("p b i -> p (b i)"), ps[:, 7, 0:NS]).then_inc(new_spread, 1)
            dve.wait_ge(new_spread, 1)
            dve.wait_ge(sel_made, 1 + DS)
            nc.vector.tensor_tensor(new_key[:], new_sum[:], tok_mask[:].unsqueeze(1).to_broadcast([P, NB, DS]),
                                    ALU.add).then_inc(new_spread, 1)
            dve.wait_ge(new_spread, 2)
            nc.vector.tensor_tensor(new_sum[:], new_sum[:], tok_sel[:].unsqueeze(1).to_broadcast([P, NB, DS]),
                                    ALU.mult).then_inc(new_spread, 1)
            dve.wait_ge(new_spread, 3)
            nc.vector.tensor_reduce(new_q[:], new_sum[:], AX.X, ALU.add).then_inc(new_spread, 1)
            v_tile(0, 1)
            for i in range(1, NKV // 2):
                for k in range(2):
                    v_tile(i, k)

            def norm_head(m, s):
                if not (isinstance(m, int) and m == 0):
                    dve.wait_ge(head_done, m)
                dve.wait_ge(head_std, m + 1)
                nc.vector.reciprocal(tmp_c[:, 1, :], tmp_c[:, 0, :]).then_inc(head_rec, 1)
                dve.wait_ge(head_rec, m + 1)
                dst = kq[:, m, :] if isinstance(m, int) else kq[:, bass.ds(m, 1), :].rearrange("p o t -> p (o t)")
                gain = g_kq[:, m:m + 1] if isinstance(m, int) else g_kq[:, bass.ds(m, 1)]
                nc.vector.scalar_tensor_tensor(out=dst, in0=tmp_a[:, s, :], scalar=gain, in1=tmp_c[:, 1, :],
                                               op0=ALU.mult, op1=ALU.mult).then_inc(head_done, 1)

            def kq_tile(i, k, u0, m0):
                u, m = u0 + 2 * k, m0 + k
                split(i + (u + 2) // 4, (u + 2) % 4)
                if k == 1 and m0:
                    dve.wait_ge(c_cached, 16 * NPG)
                if not (isinstance(i, int) and m + 2 * i == 0):
                    norm_head(2 * i + (m - 1), (m - 1) % 2)
                split(i + (u + 3) // 4, (u + 3) % 4)

            dve.wait_ge(gains_made, 3)
            dve.wait_ge(c_stored, 16)
            for i in range(NKV // 2):
                for k in range(2):
                    kq_tile(i, k, U_K, 0)
            dve.wait_ge(csum_done, 1)
            nc.vector.tensor_copy(c_pg[:].rearrange("p b n -> p (b n)"), psf[:, 3072:4096]).then_inc(csum_evac, 1)
            dve.wait_ge(csum_done, 2)
            nc.vector.tensor_copy(pg_off[:], ps[:, 6, 0:NB]).then_inc(csum_evac, 1)
            dve.wait_ge(csum_evac, 2)
            nc.vector.tensor_tensor(c_pg[:], c_pg[:], pg_off[:].unsqueeze(2).to_broadcast([P, NB, PAGE]), ALU.add
                                    ).then_inc(csum_evac, 1)
            with dve.Fori(0, NH // 2) as i:
                for k in range(2):
                    kq_tile(i, k, U_Q, NKV)
            norm_head(NKV + NH - 1, 1)
            dve.wait_ge(head_done, NKV + NH)
            nc.vector.memset(c_dec[:], 0.0).then_inc(cdec_zeroed, 1)

            for g in range(NKV):
                dve.wait_ge(kv_turned, 2 * g + 2)
                nc.vector.tensor_copy(k_tok[:, 0:QT, g * P:(g + 1) * P],
                                      psf[:, 1024:1024 + SEQ].rearrange("p (t d) -> p t d", d=P)
                                      ).then_inc(ktok_made, 1)
                nc.vector.tensor_copy(k_tok[0:NS, QT, g * P:(g + 1) * P], psf[0:NS, 1024 + SEQ:1024 + SEQ + P]
                                      ).then_inc(ktok_made, 1)

            def bias_and_max(i, k):
                dve.wait_ge(cdiag_made, 4 * i + k + 1)
                for t in range(QT):
                    dve.wait_ge(logit_made, 16 * i + 4 * k + t + 1)
                    if t:
                        nc.vector.tensor_tensor(probs[:, k, t, 0:t * P], probs[:, k, t, 0:t * P],
                                                c_row[:, k % 2, 0:t * P], ALU.subtract)
                    ins = nc.vector.tensor_tensor(probs[:, k, t, t * P:(t + 1) * P], probs[:, k, t, t * P:(t + 1) * P],
                                                  c_diag[:, k % 2, t], ALU.subtract)
                    ins.then_inc(bias_sub, 1)
                    dve.wait_ge(bias_sub, 16 * i + 4 * k + t + 1)
                    nc.vector.tensor_reduce(nmax[:, k % 2, t:t + 1], probs[:, k, t, 0:(t + 1) * P], AX.X, ALU.max,
                                            negate=True).then_inc(max_made, 1)

            def normalise(i, k):
                dve.wait_ge(exp_made, 16 * i + 4 * k + 4)
                nc.vector.reciprocal(rinv[:, k % 2, :], rsum[:, k % 2, :]).then_inc(rinv_made, 1)
                dve.wait_ge(rinv_made, 4 * i + k + 1)
                for t in range(QT):
                    w = (t + 1) * P
                    ins = nc.vector.tensor_scalar(probs[:, k, t, 0:w], probs[:, k, t, 0:w],
                                                  rinv[:, k % 2, t:t + 1], None, ALU.mult)
                ins.then_inc(normed, 1)

            def take_pT(i, k):
                dve.wait_ge(p_turned, 4 * i + k + 1)
                if not isinstance(i, int) or 4 * i + k >= 2:
                    dve.wait_ge(pv_done, 4 * i + (k - 1))
                nc.vector.tensor_copy(pT[:, k % 2, 4 * P:10 * P], psf[:, 5 * 512:5 * 512 + 6 * P]).then_inc(pT_dve, 1)

            dve.wait_ge(kv_stored, 64)
            for k in range(4):
                bias_and_max(0, k)
                if k >= 1:
                    normalise(0, k - 1)
                if k >= 2:
                    take_pT(0, k - 2)
            with dve.Fori(1, NKV) as i:
                for k in range(4):
                    bias_and_max(i, k)
                    normalise(*((i, k - 1) if k >= 1 else (i - 1, 3)))
                    take_pT(*((i, k - 2) if k >= 2 else (i - 1, k + 2)))
            normalise(NKV - 1, 3)
            take_pT(NKV - 1, 2)
            take_pT(NKV - 1, 3)

            def take_kT(i, k, p):
                dve.wait_ge(k_turned, 2 * NPG * i + NPG * k + p + 1)
                if p % 4 == 1 and not (isinstance(i, int) and 2 * i + k == 0):
                    dve.wait_ge(half_scored, 4 * i + 2 * k + p // 4 - 1)
                nc.vector.tensor_copy(kcT[:, p // 4, :, (p % 4) * P:(p % 4 + 1) * P],
                                      ps[:, 1, :].rearrange("p (g n) -> p g n", g=NKV)).then_inc(kcT_dve, 1)

            def s_logits(i, k):
                b = 2 * i + k
                sl = (lambda t, n: t[:, b, :] if n else t[:, b:b + 1]) if isinstance(i, int) else \
                    (lambda t, n: t[:, bass.ds(b, 1), :].rearrange("p o i -> p (o i)") if n else t[:, bass.ds(b, 1)])
                dve.wait_ge(cdec_loaded[k], 64 * i + 64)
                c_end = c_dec[:, k, PAST - 1:PAST]
                nc.vector.tensor_scalar(s_ckn[:, k], sl(new_key, 1), c_end, None, ALU.add)
                nc.vector.tensor_tensor(s_cq[:, k], sl(new_q, 0), c_end, ALU.add).then_inc(s_small, 1)
                dve.wait_ge(new_scored, 2 * i + k + 1)
                nc.vector.scalar_tensor_tensor(out=sprob[:, k, 0:PAST], in0=psf[:, 1024:1024 + PAST], scalar=SCALE,
                                               in1=c_dec[:, k], op0=ALU.mult, op1=ALU.subtract).then_inc(s_logit, 1)
                dve.wait_ge(s_small, 2 * i + k + 1)
                nc.vector.scalar_tensor_tensor(out=sprob[:, k, PAST:PAST + DS], in0=psf[:, 1024 + PAST:1024 + PAST + DS],
                                               scalar=SCALE, in1=s_ckn[:, k], op0=ALU.mult, op1=ALU.subtract
                                               ).then_inc(s_logit, 1)
                dve.wait_ge(s_logit, 4 * i + 2 * k + 2)
                nc.vector.tensor_reduce(s_nmax[:, k], sprob[:, k, 0:PAST + DS], AX.X, ALU.max, negate=True
                                        ).then_inc(s_max, 1)
                dve.wait_ge(s_max, 2 * i + k + 1)
                nc.vector.scalar_tensor_tensor(out=s_nbias[:, k], in0=s_nmax[:, k], scalar=s_cq[:, k], in1=s_cq[:, k],
                                               op0=ALU.subtract, op1=ALU.add).then_inc(s_bias, 1)

            def s_spread(i, k):
                dve.wait_ge(s_exp, 2 * i + k + 1)
                b = 2 * i + k
                row = own[:, b, :] if isinstance(i, int) else own[:, bass.ds(b, 1), :].rearrange("p o b -> p (o b)")
                nc.vector.tensor_tensor(p_new[:].rearrange("p (b i) -> p b i", i=DS),
                                        sprob[:, k, PAST:PAST + DS].unsqueeze(1).to_broadcast([P, NB, DS]),
                                        row.unsqueeze(2).to_broadcast([P, NB, DS]), ALU.mult).then_inc(s_pnew, 1)
                nc.vector.reciprocal(s_rinv[:, k], s_rsum[:, k])

            def take_new(i, k):
                dve.wait_ge(s_turned, 2 * i + k + 1)
                nc.vector.tensor_copy(p_newT[:], ps[0:NS, 7, P:2 * P]).then_inc(p_newT_made, 1)

            def s_scale(i, k):
                dve.wait_ge(s_pv, 2 * i + k + 1)
                nc.vector.tensor_scalar(s_outr[:], ps[:, 7, 0:P], s_rinv[:, k], None, ALU.mult).then_inc(s_scaled, 1)

            def s_output(i, k):
                dve.wait_ge(s_outT, 2 * i + k + 1)
                c0 = SEQ + 2 * DS * i + DS * k
                dst = kq[:, NKV:NKV + NH, c0:c0 + DS] if isinstance(i, int) else kq[:, NKV:NKV + NH, bass.ds(c0, DS)]
                src = ps[:, 7, 2 * P:3 * P].rearrange("p (g r) -> p g r", g=NKV)[:, :, 0:RQ]
                nc.vector.tensor_copy(dst.rearrange("p (g h) i -> p g h i", g=NKV),
                                      src.rearrange("p g (h i) -> p g h i", i=DS)).then_inc(s_out, 1)

            def s_step(i, k, prev, prev2):
                if prev is not None:
                    s_logits(*prev)
                take_kT(i, k, 1)
                if prev2 is not None:
                    s_output(*prev2)
                take_kT(i, k, 3)
                if prev is not None:
                    s_spread(*prev)
                take_kT(i, k, 5)
                if prev is not None:
                    take_new(*prev)
                take_kT(i, k, 7)
                if prev is not None:
                    s_scale(*prev)

            s_step(0, 0, None, None)
            s_step(0, 1, (0, 0), None)
            s_step(1, 0, (0, 1), (0, 0))
            s_step(1, 1, (1, 0), (0, 1))
            with dve.Fori(2, NB // 2) as i:
                s_step(i, 0, (i - 1, 1), (i - 1, 0))
                s_step(i, 1, (i, 0), (i - 1, 1))
            last = (NB // 2 - 1, 1)
            s_logits(*last)
            s_output(NB // 2 - 1, 0)
            s_spread(*last)
            take_new(*last)
            s_scale(*last)
            s_output(*last)

            for c in range(KC):
                dve.wait_ge(mix_hi, c + 1)
                nc.vector.tensor_tensor(act_lo[:, c, :], kq[:, NKV + c, :], act_hi[:, c, :], ALU.subtract
                                        ).then_inc(mix_lo, 1)

            def o_tile(i, k, start):
                u, t = U_O + 2 * k, T_O + k
                split(i + (u + 2) // 4, (u + 2) % 4)
                split(i + (u + 3) // 4, (u + 3) % 4)
                dve.wait_ge(unit_used, 4 * i + u + 2)
                dst = xT[:, 2 * i + k, :] if isinstance(i, int) else \
                    xT[:, bass.ds(2 * i + k, 1), :].rearrange("p o t -> p (o t)")
                nc.vector.tensor_tensor(halves(dst), halves(dst), acc(t % 2), ALU.add).then_inc(acc_free[t % 2], 1)
                if k == 0 and not start:
                    dve.wait_ge(sq_made, KC + 2 * i + k + 1)
                    nc.vector.tensor_tensor(tmp_c[:, 0, :], tmp_c[:, 0, :], tmp_b[:, 0, :], ALU.add
                                            ).then_inc(sq_added_dve, 1)

            o_tile(0, 0, True)
            o_tile(0, 1, True)
            with dve.Fori(1, KC // 2) as i:
                for k in range(2):
                    o_tile(i, k, False)
            scale_chunks(1, g_mlp)

            def up_tile(j, i, k):
                u = U_M + 2 * k
                split(j * (BLK_U // 4) + i + (u + 2) // 4, (u + 2) % 4)
                split(j * (BLK_U // 4) + i + (u + 3) // 4, (u + 3) % 4)
                t = T_M + k
                dve.wait_ge(acc_free[t % 2], j * (BLK_T // 2) + i + (t // 2 + 1))
                dve.wait_ge(u_lo_made, j * FB + 2 * i + k)
                nc.vector.tensor_tensor(tmp_b[:, k, :], tmp_a[:, k, :], tmp_a[:, k, :], ALU.mult).then_inc(relu_sq, 1)
                dve.wait_ge(u_hi_made, j * FB + 2 * i + (k + 1))
                sl = lambda t: t[:, bass.ds(2 * i + k, 1), :].rearrange("p o t -> p (o t)")
                nc.vector.tensor_tensor(sl(u_lo), tmp_b[:, k, :], sl(u_hi), ALU.subtract).then_inc(u_lo_made, 1)

            def up_tiles(j):
                with dve.Fori(0, FB // 2) as i:
                    for k in range(2):
                        up_tile(j, i, k)

            def down_tile(j, i, k, ahead=True):
                u, t = U_M + 2 * FB + k, T_M + FB + k
                if ahead:
                    split(j * (BLK_U // 4) + i + (u + 2) // 4, (u + 2) % 4)
                dve.wait_ge(unit_used, j * BLK_U + 4 * i + (u + 1))
                dst = xT[:, bass.ds(4 * i + k, 1), :].rearrange("p o t -> p (o t)") if not isinstance(i, int) \
                    else xT[:, 4 * i + k, :]
                nc.vector.tensor_tensor(halves(dst), halves(dst), acc(t % 2), ALU.add).then_inc(acc_free[t % 2], 1)

            with dve.Fori(0, NBLK - 1) as j:
                up_tiles(j)
                with dve.Fori(0, KC // 4) as i:
                    for k in range(4):
                        down_tile(j, i, k)
            up_tiles(NBLK - 1)
            with dve.Fori(0, KC // 4 - 1) as i:
                for k in range(4):
                    down_tile(NBLK - 1, i, k)
            for k in range(4):
                down_tile(NBLK - 1, KC // 4 - 1, k, ahead=k < 2)

            for c in range(KC):
                dve.wait_ge(y_turned, c + 1)
                nc.vector.tensor_copy(x_tok[0:NS, QT, c * P:(c + 1) * P],
                                      psf[0:NS, 1024 * (c % 4) + SEQ:1024 * (c % 4) + SEQ + P]).then_inc(y_evac_dve, 1)

        @block.tensor
        def _(pe):
            token_tiles = [(t * P, P) for t in range(QT)] + [(SEQ, NS)]

            pe.wait_ge(const_made, 5)
            for c in range(KC):
                if c % 4 == 0:
                    pe.wait_ge(x_loaded[c // 4], 32)
                if c >= 2:
                    pe.wait_ge(xT_made, c - 1)
                for t, (t0, n) in enumerate(token_tiles):
                    o = 1024 * (c % 2) + t0
                    ins = pe.transpose(psf[:, o:o + n], x_tok[0:n, t, c * P:(c + 1) * P], ident[0:n, 0:n])
                ins.then_inc(x_turned, 1)

            def column_sums(srcs, out, signal):
                for a in range(2):
                    for n, src in enumerate(srcs):
                        ins = pe.matmul(out[:, a, :], ones[:], src[:, a * HALF:(a + 1) * HALF],
                                        start=n == 0, stop=n == len(srcs) - 1)
                ins.then_inc(signal, 1)

            def unit(i, k, out, hi, lo, first, last, chunk_waits=None):
                pe.wait_ge(w_lo_made, 4 * i + k + 1)
                s = k % 2
                for c in range(UC):
                    if chunk_waits is not None:
                        chunk_waits(c)
                    for a in range(2):
                        h, l = hi(c)[:, a * HALF:(a + 1) * HALF], lo(c)[:, a * HALF:(a + 1) * HALF]
                        pe.matmul(out[:, a, :], w_hi[:, s, c, :], l, start=first and c == 0, stop=False)
                        pe.matmul(out[:, a, :], w_hi[:, s, c, :], h, start=False, stop=False)
                    for a in range(2):
                        h = hi(c)[:, a * HALF:(a + 1) * HALF]
                        ins = pe.matmul(out[:, a, :], w_lo[:, s, c, :], h, start=False, stop=last and c == UC - 1)
                ins.then_inc(unit_used, 1)
                return ins

            def model_tile(i, u, t, waits=None, between=None, wait_acc=True):
                if wait_acc:
                    pe.wait_ge(acc_free[t % 2], i + t // 2)
                out = acc(t % 2)
                for half in range(2):
                    uu = u + half
                    unit(i + uu // 4, uu % 4, out, lambda c: act_hi[:, half * UC + c, :],
                         lambda c: act_lo[:, half * UC + c, :], half == 0, half == 1,
                         None if waits is None else (lambda c: waits(half * UC + c)))
                    if half == 0 and between is not None:
                        between()

            def norm_waits(n):
                def waits(c):
                    (pe.wait_ge(act_lo_dve, 8 * n + c // 2 + 1) if c % 2 == 0 else
                     pe.wait_ge(act_lo_pool, 8 * n + c // 2 + 1))
                return waits

            pe.wait_ge(sq_added_dve, 7)
            pe.wait_ge(sq_added_pool, 7)
            column_sums([tmp_c[:, 0, :], tmp_c[:, 1, :]], acc(2), ssq_ready)

            model_tile(0, 0, 0, waits=norm_waits(0), wait_acc=False)

            def turn_gates():
                pe.wait_ge(const_made, 11 + NPG - 1)
                pe.wait_ge(f_chain, 5)
                pe.wait_ge(new_chain, DS)
                for n in range(TT + QT):
                    t0, w = token_tiles[n] if n < TT else token_tiles[n - TT]
                    src = (lfT if n < TT else cT)[:, t0:t0 + w]
                    pe.transpose(ps[0:w, 6, n * NH:(n + 1) * NH], src, ident[0:NH, 0:NH])
                pe.matmul(ps[:, 7, 0:NS], expand[:], cT[:, SEQ:T], start=True, stop=True).then_inc(f_turned, 1)

            for i in range(NKV // 2):
                for k in range(2):
                    u, t = U_V + 2 * k, T_V + k
                    model_tile(i, u, t, wait_acc=not (i == 0 and k == 0), between=turn_gates if i + k == 0 else None)

            def head_sums(i, m):
                t, s = T_K + m, m % 2
                pe.wait_ge(acc_free[t % 2], i + t // 2 + 1)
                if not (isinstance(i, int) and 2 * i + m == 0):
                    pe.wait_ge(head_std, 2 * i + m)
                column_sums([tmp_b[:, s, :]], acc(2), head_ssq)

            def kq_tile(i, k, u0, t0, m0):
                u, t, m = u0 + 2 * k, t0 + k, m0 + k
                first = isinstance(i, int) and m + 2 * i == 0
                model_tile(i, u, t, between=None if first else (lambda: head_sums(i, m - 1)))

            for i in range(NKV // 2):
                for k in range(2):
                    kq_tile(i, k, U_K, T_K, 0)
            pe.wait_ge(lf_loaded, 16 * NB * NPG)
            pe.wait_ge(new_spread, 1)
            for b in range(NB):
                ins = pe.matmul(psf[:, 3072 + b * PAGE:3072 + (b + 1) * PAGE],
                                lf_page[:, b * NPG:(b + 1) * NPG, :].rearrange("p n h -> p (n h)"), tri[:],
                                start=True, stop=True)
            ins.then_inc(csum_done, 1)
            pe.wait_ge(csum_evac, 1)
            pe.matmul(ps[:, 6, 0:NB], earlier[:], c_pg[:, :, PAGE - 1], start=True, stop=True).then_inc(csum_done, 1)
            with pe.Fori(0, NH // 2) as i:
                for k in range(2):
                    kq_tile(i, k, U_Q, T_Q, NKV)
            head_sums(0, NKV + NH - 1)

            pe.wait_ge(acc_free[0], T_O // 2)
            pe.wait_ge(acc_free[1], T_O // 2)
            for g in range(NKV):
                for which, (src, made, off) in enumerate(((vT, vtok_made, 0), (kq, ktok_made, 1024))):
                    if g:
                        pe.wait_ge(made, 2 * g)
                    for t, (t0, w) in enumerate(token_tiles):
                        ins = pe.transpose(psf[0:w, off + t * P:off + (t + 1) * P], src[:, g, t0:t0 + w], ident[:])
                    ins.then_inc(kv_turned, 1)

            pe.wait_ge(vtok_made, 2 * NKV)
            pe.wait_ge(ktok_made, 2 * NKV)
            pe.wait_ge(head_std, NKV + NH)

            def scores(i, k):
                pe.wait_ge(q_staged, 4 * i + k + 1)
                if not (isinstance(i, int) and 4 * i + k == 0):
                    pe.wait_ge(logit_made, 16 * i + 4 * k)
                for t in range(QT):
                    w = (t + 1) * P
                    keys = kq[:, i, 0:w] if isinstance(i, int) else kq[:, bass.ds(i, 1), 0:w].rearrange("p o s -> p (o s)")
                    pe.matmul(ps[:, t, 0:w], q_st[:, k % 2, t * P:(t + 1) * P], keys, start=True, stop=True
                              ).then_inc(score_done, 1)

            PT_AT = [0, 4 * P, 8 * P, 7 * P]

            def turn_probs(i, k):
                pe.wait_ge(normed, 4 * i + k + 1)
                if not (isinstance(i, int) and 4 * i + k == 0):
                    pe.wait_ge(pT_act, 4 * i + k)
                    pe.wait_ge(pT_dve, 4 * i + k)
                for j in range(QT):
                    for t in range(j, QT):
                        o = 4 * 512 + PT_AT[j] + (t - j) * P
                        ins = pe.transpose(psf[:, o:o + P], probs[:, k, t, j * P:(j + 1) * P], ident[:])
                ins.then_inc(p_turned, 1)

            def values(i, k):
                pe.wait_ge(v_staged, i + 1)
                pe.wait_ge(pT_act, 4 * i + k + 1)
                pe.wait_ge(pT_dve, 4 * i + k + 1)
                if not (isinstance(i, int) and 4 * i + k == 0):
                    pe.wait_ge(out_evac, 4 * i + k)
                for j in range(QT):
                    w = (QT - j) * P
                    ins = pe.matmul(ps[:, 7, j * P:SEQ], v_st[:, j, :], pT[:, k % 2, PT_AT[j]:PT_AT[j] + w],
                                    start=j == 0, stop=j == QT - 1, skip_group_check=True)
                ins.then_inc(pv_done, 1)

            for k in range(4):
                scores(0, k)
                if k >= 2:
                    turn_probs(0, k - 2)
                if k >= 3:
                    values(0, k - 3)
            with pe.Fori(1, NKV) as i:
                for k in range(4):
                    scores(i, k)
                    turn_probs(*((i, k - 2) if k >= 2 else (i - 1, k + 2)))
                    values(*((i, k - 3) if k >= 3 else (i - 1, k + 1)))
            turn_probs(NKV - 1, 2)
            values(NKV - 1, 1)
            turn_probs(NKV - 1, 3)
            values(NKV - 1, 2)
            values(NKV - 1, 3)
            pe.wait_ge(out_evac, NH)

            def turn_page(i, k, p):
                if not (isinstance(i, int) and 2 * i + k == 0 and p < 2):
                    (pe.wait_ge(kcT_act, NPG * i + NPG // 2 * k + p // 2) if p % 2 == 0 else
                     pe.wait_ge(kcT_dve, NPG * i + NPG // 2 * k + p // 2))
                pe.wait_ge(page_loaded[p % 4], 64 * i + 32 * k + 16 * (p // 4) + 16)
                for g in range(NKV):
                    ins = pe.transpose(ps[:, p % 2, g * P:(g + 1) * P], k_page[:, p % 4, g * P:(g + 1) * P], ident[:])
                ins.then_inc(k_turned, 1)

            def score_half(i, k, half):
                pe.wait_ge(kcT_act, NPG * i + NPG // 2 * k + 2 * half + 2)
                pe.wait_ge(kcT_dve, NPG * i + NPG // 2 * k + 2 * half + 2)
                if half == 0:
                    pe.wait_ge(q_packed, 2 * i + k + 1)
                    if not (isinstance(i, int) and 2 * i + k == 0):
                        pe.wait_ge(s_logit, 4 * i + 2 * k)
                o = 1024 + 512 * half
                for g in range(NKV):
                    ins = pe.matmul(psf[g * R:(g + 1) * R, o:o + 512], q_pack[:, k, g, :], kcT[:, half, g, :],
                                    start=True, stop=True)
                ins.then_inc(half_scored, 1)

            def score_new(i, k):
                for g in range(NKV):
                    ins = pe.matmul(psf[g * R:(g + 1) * R, 2048:2048 + DS], q_pack[:, k, g, :], k_pack[:, k, g, :],
                                    start=True, stop=True)
                ins.then_inc(new_scored, 1)

            def turn_sprob(i, k):
                pe.wait_ge(s_pnew, 2 * i + k + 1)
                if not (isinstance(i, int) and 2 * i + k == 0):
                    pe.wait_ge(spT_made, 2 * i + k)
                    pe.wait_ge(s_out, 2 * i + k)
                for p in range(NPG):
                    pe.transpose(psf[:, 2560 + p * P:2560 + (p + 1) * P], sprob[:, k, p * PAGE:(p + 1) * PAGE], ident[:])
                pe.transpose(ps[0:NS, 7, P:2 * P], p_new[:], ident[:]).then_inc(s_turned, 1)

            def s_values(i, k):
                pe.wait_ge(vpage_loaded[k], 16 * NPG * i + 16 * NPG)
                pe.wait_ge(spT_made, 2 * i + k + 1)
                pe.wait_ge(p_newT_made, 2 * i + k + 1)
                for p in range(NPG):
                    for g in range(NKV):
                        pe.matmul(ps[g * R:(g + 1) * R, 7, 0:P], spT[:, p, g * R:(g + 1) * R],
                                  v_page[:, k, p, g * P:(g + 1) * P], start=p == 0, stop=False)
                for g in range(NKV):
                    ins = pe.matmul(ps[g * R:(g + 1) * R, 7, 0:P], p_newT[:, g * R:(g + 1) * R],
                                    v_tok[0:NS, QT, g * P:(g + 1) * P], start=False, stop=True)
                ins.then_inc(s_pv, 1)

            def turn_out(i, k):
                pe.wait_ge(s_scaled, 2 * i + k + 1)
                pe.transpose(ps[:, 7, 2 * P:3 * P], s_outr[:], ident[:]).then_inc(s_outT, 1)

            def s_step(i, k, prev, prev2):
                turn_page(i, k, 0)
                if prev2 is not None:
                    turn_out(*prev2)
                for p in range(1, 5):
                    turn_page(i, k, p)
                score_half(i, k, 0)
                if prev is not None:
                    turn_sprob(*prev)
                for p in range(5, NPG):
                    turn_page(i, k, p)
                score_half(i, k, 1)
                score_new(i, k)
                if prev is not None:
                    s_values(*prev)

            s_step(0, 0, None, None)
            s_step(0, 1, (0, 0), None)
            s_step(1, 0, (0, 1), (0, 0))
            s_step(1, 1, (1, 0), (0, 1))
            with pe.Fori(2, NB // 2) as i:
                s_step(i, 0, (i - 1, 1), (i - 1, 0))
                s_step(i, 1, (i, 0), (i - 1, 1))
            last = (NB // 2 - 1, 1)
            turn_out(NB // 2 - 1, 0)
            turn_sprob(*last)
            s_values(*last)
            turn_out(*last)

            for k in range(2):
                u, t = U_O + 2 * k, T_O + k
                model_tile(0, u, t, waits=(lambda c: pe.wait_ge(mix_lo, c + 1)) if k == 0 else None)
            with pe.Fori(1, KC // 2) as i:
                for k in range(2):
                    u, t = U_O + 2 * k, T_O + k
                    model_tile(i, u, t)
            pe.wait_ge(sq_added_dve, 14)
            pe.wait_ge(sq_added_pool, 14)
            column_sums([tmp_c[:, 0, :], tmp_c[:, 1, :]], acc(2), ssq_ready)

            def up_tiles(j, i, waits=None):
                for k in range(2):
                    u, t = U_M + 2 * k, T_M + k
                    pe.wait_ge(acc_free[t % 2], j * (BLK_T // 2) + i + t // 2)
                    for half in range(2):
                        uu = u + half
                        unit(j * (BLK_U // 4) + i + uu // 4, uu % 4, acc(t % 2),
                             lambda c: act_hi[:, half * UC + c, :], lambda c: act_lo[:, half * UC + c, :],
                             half == 0, half == 1,
                             None if waits is None or k else (lambda c: waits(half * UC + c)))

            def down_tiles(j, i, waits=None):
                for k in range(4):
                    u, t = U_M + 2 * FB + k, T_M + FB + k
                    pe.wait_ge(acc_free[t % 2], j * (BLK_T // 2) + 2 * i + t // 2)
                    unit(j * (BLK_U // 4) + i + u // 4, u % 4, acc(t % 2), lambda c: u_hi[:, c, :],
                         lambda c: u_lo[:, c, :], True, True, waits if k == 0 else None)

            def mlp_block(j, first_waits=None):
                if first_waits is not None:
                    up_tiles(j, 0, first_waits)
                with pe.Fori(1 if first_waits is not None else 0, FB // 2) as i:
                    up_tiles(j, i)
                down_tiles(j, 0, lambda c: pe.wait_ge(u_lo_made, FB * j + c + 1))
                with pe.Fori(1, KC // 4) as i:
                    down_tiles(j, i)

            mlp_block(0, norm_waits(1))
            with pe.Fori(1, NBLK) as j:
                mlp_block(j)

            pe.wait_ge(acc_free[0], (T_M + NBLK * BLK_T) // 2 + 1)
            pe.wait_ge(acc_free[1], (T_M + NBLK * BLK_T) // 2)
            for c in range(KC):
                if c >= 4:
                    pe.wait_ge(y_evac_act, c - 3)
                    pe.wait_ge(y_evac_dve, c - 3)
                o = 1024 * (c % 4)
                for t in range(QT):
                    pe.transpose(psf[:, o + t * P:o + (t + 1) * P], xT[:, c, t * P:(t + 1) * P], ident[:])
                pe.transpose(psf[0:NS, o + SEQ:o + SEQ + P], xT[:, c, SEQ:T], ident[:]).then_inc(y_turned, 1)


_INS = ["x_prompt", "x_sample", "cache_k", "cache_v", "cache_logf", "page_table", "attn_norm", "w_qkv", "q_norm",
        "k_norm", "w_fgate", "b_fgate", "w_o", "mlp_norm", "w_up", "w_down"]


def kernel(**inputs):
    import numpy as _np
    import concourse.bacc as _bacc
    from concourse import mybir as _mybir
    from concourse.bass_utils import run_bass_kernel_spmd as _run

    nc = _bacc.Bacc("TRN2", target_bir_lowering=False, num_devices=1)
    arrays, args = {}, []
    for name in _INS:
        a = _np.ascontiguousarray(inputs[name])
        arrays[f"in_{name}"] = a
        args.append(nc.dram_tensor(f"in_{name}", a.shape, _mybir.dt.from_np(a.dtype), kind="ExternalInput").ap())
    xp, xs = inputs["x_prompt"].shape, inputs["x_sample"].shape
    depth, _, _, nkv, hd = inputs["cache_k"].shape
    nfox, _, _, nh = inputs["cache_logf"].shape
    outs = [xp, xs, (depth, *xp[:2], nkv, hd), (depth, *xp[:2], nkv, hd), (nfox, *xp[:2], nh),
            (depth, *xs[:2], nkv, hd), (depth, *xs[:2], nkv, hd), (nfox, *xs[:2], nh)]
    for i, shape in enumerate(outs):
        args.append(nc.dram_tensor(f"out_{i}", shape, F32, kind="ExternalOutput").ap())
    fox_layer(nc, *args)
    r = _run(nc, [arrays], core_ids=[0])
    return tuple(r.results[0][f"out_{i}"] for i in range(len(outs)))
```

```python
from contextlib import ExitStack

import concourse.bass as bass
from concourse import mybir

F32 = mybir.dt.float32
F32R = mybir.dt.float32r
I32 = mybir.dt.int32
ACT = mybir.ActivationFunctionType
ALU = mybir.AluOpType
AX = mybir.AxisListType

P = 128
BIG = 1.0e30


def fox_layer(nc, x_prompt, x_sample, cache_k, cache_v, cache_logf, page_table, attn_norm, w_qkv, q_norm,
              k_norm, w_fgate, b_fgate, w_o, mlp_norm, w_up, w_down,
              y_prompt, y_sample, nk_prompt, nv_prompt, nf_prompt, nk_sample, nv_sample, nf_sample):
    _, SEQ, D = x_prompt.shape
    NB, DS, _ = x_sample.shape
    _, NPOOL, PAGE, NKV, HD = cache_k.shape
    NH = cache_logf.shape[3]
    NPG = page_table.shape[1]
    DFF = w_up.shape[2]
    GRP = NH // NKV
    NS = NB * DS
    T = SEQ + NS
    HALF = T // 2
    QT = SEQ // P
    TT = QT + 1
    KC = D // P
    UC = 8
    FB = UC
    NBLK = DFF // P // FB
    KVC = NKV * HD
    SCALE = float(HD) ** -0.5
    EPS = 1e-6
    PAST = NPG * PAGE
    R = 32
    RQ = GRP * DS
    assert PAGE == P and HD == P and SEQ == 4 * P and HALF * 4 <= 2048 and NPG == 8 and KC == 2 * UC
    assert NH == 16 and GRP == 4 and NB == 8 and NKV * R == P and NPG * NH == P

    with ExitStack() as ctx:
        def sem(name):
            return ctx.enter_context(nc.semaphore(name))

        base = -(-nc.sbuf_base // 64) * 64
        top = [base]

        def at(name, shape, dt, offset=None):
            n = 4
            for s in shape[1:]:
                n *= s
            if offset is None:
                offset = top[0]
                top[0] += -(-n // 64) * 64
            return nc.alloc_sbuf_tensor_at(name, shape, dt, offset=offset), offset, offset + n

        xT, _, _ = at("xT", [P, KC, T], F32)
        act_hi, act_at, _ = at("act_hi", [P, KC, T], F32R)
        act_lo, _, act_end = at("act_lo", [P, KC, T], F32R)
        kq, kq_at, _ = at("kq", [P, NKV + NH, T], F32)
        vT, vT_at, _ = at("vT", [P, NKV, T], F32)
        w_raw, w_raw_at, _ = at("w_raw", [P, 4, UC, P], F32)
        w_hi, _, _ = at("w_hi", [P, 2, UC, P], F32R)
        w_lo, _, _ = at("w_lo", [P, 2, UC, P], F32R)
        tmp_a, tmp_a_at, _ = at("tmp_a", [P, 2, T], F32)
        tmp_b, tmp_b_at, _ = at("tmp_b", [P, 2, T], F32)
        tmp_c, tmp_c_at, _ = at("tmp_c", [P, 2, T], F32)
        ident, _, _ = at("ident", [P, P], F32)
        ones, _, _ = at("ones", [P, P], F32)
        ones_r, _, _ = at("ones_r", [P, P], F32R)
        tri, _, _ = at("tri", [P, P], F32)
        earlier, _, _ = at("earlier", [P, P], F32)
        causal, _, _ = at("causal", [P, P], F32)
        expand, _, _ = at("expand", [NH, P], F32)
        own, _, _ = at("own", [P, NB, NB], F32)
        tok_sel, _, _ = at("tok_sel", [P, DS], F32)
        tok_mask, _, _ = at("tok_mask", [P, DS], F32)
        eps_t, _, _ = at("eps_t", [P, 1], F32)
        g_attn, _, _ = at("g_attn", [P, KC], F32)
        g_mlp, _, _ = at("g_mlp", [P, KC], F32)
        g_kq, _, _ = at("g_kq", [P, NKV + NH], F32)
        g_qk1, _, _ = at("g_qk1", [P, 2], F32)
        bf, _, _ = at("bf", [NH, 1], F32)
        pages, _, _ = at("pages", [1, NB * NPG], I32)
        tokc, _, _ = at("tokc", [P, TT + QT, NH], F32)
        nmax, _, _ = at("nmax", [P, 2, QT], F32)
        rsum, _, _ = at("rsum", [P, 2, QT], F32)
        rinv, _, _ = at("rinv", [P, 2, QT], F32)
        pg_off, _, _ = at("pg_off", [P, NB], F32)
        new_sum, _, _ = at("new_sum", [P, NB, DS], F32)
        new_key, _, _ = at("new_key", [P, NB, DS], F32)
        new_q, _, _ = at("new_q", [P, NB], F32)
        s_ckn, _, _ = at("s_ckn", [P, 2, DS], F32)
        s_cq, _, _ = at("s_cq", [P, 2, 1], F32)
        s_nmax, _, _ = at("s_nmax", [P, 2, 1], F32)
        s_nbias, _, _ = at("s_nbias", [P, 2, 1], F32)
        s_rsum, _, _ = at("s_rsum", [P, 2, 1], F32)
        s_rinv, _, _ = at("s_rinv", [P, 2, 1], F32)
        p_new, _, _ = at("p_new", [P, NS], F32)
        p_newT, _, _ = at("p_newT", [NS, P], F32)
        s_outr, _, _ = at("s_outr", [P, P], F32)
        k_pack, _, _ = at("k_pack", [P, 2, NKV, DS], F32)
        q_pack, _, end = at("q_pack", [P, 2, NKV, R], F32)
        assert end <= nc.sbuf_usable_end, (end, nc.sbuf_usable_end)

        y_tok, _, e = at("y_tok", [P, TT, D], F32, act_at)
        assert e <= act_end
        x_tok, _, e = at("x_tok", [P, TT, D], F32, kq_at)
        assert e <= vT_at
        u_hi, _, e = at("u_hi", [P, FB, T], F32R, kq_at)
        u_lo, _, e = at("u_lo", [P, FB, T], F32R, e)
        fz, _, _ = at("fz", [NH, 2, T], F32, tmp_a_at)
        fe, _, o = at("fe", [NH, T], F32, tmp_b_at)
        lfT, _, _ = at("lfT", [NH, T], F32, o)
        cT, _, _ = at("cT", [NH, T], F32, tmp_c_at)
        sq_hi, _, _ = at("sq_hi", [P, T], F32R, tmp_b_at + 4 * T)
        sq_lo, _, _ = at("sq_lo", [P, T], F32R, tmp_b_at)
        rstd = tmp_c[:, 1, :]
        v_tok, _, o = at("v_tok", [P, TT, KVC], F32, act_at)
        scr = o
        probs, _, o = at("probs", [P, 4, QT, SEQ], F32, scr)
        k_tok, _, _ = at("k_tok", [P, TT, KVC], F32, o)
        pT, _, o = at("pT", [P, 2, 10 * P], F32, o)
        c_row, _, o = at("c_row", [P, 2, SEQ], F32, o)
        c_diag, _, o = at("c_diag", [P, 2, QT, P], F32, o)
        q_st, _, o = at("q_st", [P, 2, SEQ], F32, o)
        v_st, _, o = at("v_st", [P, QT, P], F32, o)
        assert o <= act_end
        v_page, _, o = at("v_page", [P, 2, NPG, KVC], F32, scr)
        kcT, _, o = at("kcT", [P, 2, NKV, 4 * P], F32, o)
        sprob, _, o = at("sprob", [P, 2, PAST + NS], F32, o)
        assert o <= act_end
        k_low, _, o = at("k_low", [P, 4, KVC], F32, vT_at)
        assert o <= vT_at + 4 * NKV * T
        k_high, _, o = at("k_high", [P, 4, KVC], F32, w_raw_at + 4 * 2 * UC * P)
        assert o <= w_raw_at + 4 * 4 * UC * P
        c_dec, _, o = at("c_dec", [P, 2, PAST], F32, tmp_a_at)
        assert o <= tmp_c_at
        spT, _, _ = at("spT", [P, NPG, P], F32, tmp_c_at)
        lf_page, _, _ = at("lf_page", [P, NB * NPG, NH], F32, kq_at + 4 * T * (NKV + NH - 4))
        c_pg, _, _ = at("c_pg", [P, NB, PAGE], F32, kq_at + 4 * T * (NKV + NH - 2))
        ps = ctx.enter_context(nc.psum_tensor("ps", [P, 8, 512], F32))
        psf = ps[:, :, :].rearrange("p b n -> p (b n)")
        c_rows = nc.dram_tensor("c_rows", [NH, SEQ], F32).ap()
        c_cache = nc.dram_tensor("c_cache", [NB, NH, NPG, PAGE], F32).ap()

        TURN_AT = [3072, 2048]

        def halves(ap):
            return ap.rearrange("p (a n) -> p a n", a=2)

        def acc(slot, rows=P):
            return ps[0:rows, 2 * slot:2 * slot + 2, 0:HALF]

        const_made = sem("const_made")
        const_loaded = sem("const_loaded")
        gain_loaded = sem("gain_loaded")
        gains_made = sem("gains_made")
        sel_made = sem("sel_made")
        pages_loaded = sem("pages_loaded")
        x_loaded = [sem(f"x_loaded{i}") for i in range(4)]
        x_turned = sem("x_turned")
        xT_made = sem("xT_made")
        sq_made = sem("sq_made")
        sq_added = sem("sq_added")
        ssq_ready = sem("ssq_ready")
        std_ready = sem("std_ready")
        rstd_ready = sem("rstd_ready")
        act_hi_made = sem("act_hi_made")
        act_lo_made = sem("act_lo_made")
        w_loaded = [sem(f"w_loaded{i}") for i in range(4)]
        w_hi_made = sem("w_hi_made")
        w_lo_made = sem("w_lo_made")
        unit_used = sem("unit_used")
        acc_free = [sem("acc_free0"), sem("acc_free1")]
        f_chain = sem("f_chain")
        f_exp = sem("f_exp")
        f_turned = sem("f_turned")
        tokc_made = sem("tokc_made")
        c_stored = sem("c_stored")
        head_ssq = sem("head_ssq")
        head_sq = sem("head_sq")
        head_lo = sem("head_lo")
        head_std = sem("head_std")
        head_rec = sem("head_rec")
        head_done = sem("head_done")
        lf_loaded = sem("lf_loaded")
        kv_turned = sem("kv_turned")
        vtok_made = sem("vtok_made")
        ktok_made = sem("ktok_made")
        kv_stored = sem("kv_stored")
        lf_stored = sem("lf_stored")
        csum_done = sem("csum_done")
        csum_evac = sem("csum_evac")
        new_chain = sem("new_chain")
        new_spread = sem("new_spread")
        q_staged = sem("q_staged")
        v_staged = sem("v_staged")
        bias_sub = sem("bias_sub")
        c_loaded = [sem("c_loaded0"), sem("c_loaded1")]
        cdiag_made = sem("cdiag_made")
        score_done = sem("score_done")
        logit_made = sem("logit_made")
        max_made = sem("max_made")
        exp_made = sem("exp_made")
        rinv_made = sem("rinv_made")
        normed = sem("normed")
        p_turned = sem("p_turned")
        pT_act = sem("pT_act")
        pT_dve = sem("pT_dve")
        pv_done = sem("pv_done")
        out_evac = sem("out_evac")
        page_loaded = [sem(f"page_loaded{i}") for i in range(8)]
        v_low_loaded = [sem("v_low_loaded0"), sem("v_low_loaded1")]
        v_high_loaded = [sem("v_high_loaded0"), sem("v_high_loaded1")]
        k_turned = sem("k_turned")
        kcT_act = sem("kcT_act")
        kcT_dve = sem("kcT_dve")
        new_scored = sem("new_scored")
        q_packed = sem("q_packed")
        c_cached = sem("c_cached")
        cdec_loaded = [sem("cdec_loaded0"), sem("cdec_loaded1")]
        cdec_zeroed = sem("cdec_zeroed")
        half_scored = sem("half_scored")
        s_small = sem("s_small")
        s_logit = sem("s_logit")
        s_max = sem("s_max")
        s_bias = sem("s_bias")
        s_exp = sem("s_exp")
        s_pnew = sem("s_pnew")
        s_turned = sem("s_turned")
        spT_made = sem("spT_made")
        p_newT_made = sem("p_newT_made")
        s_pv = sem("s_pv")
        s_scaled = sem("s_scaled")
        s_outT = sem("s_outT")
        s_out = sem("s_out")
        mix_hi = sem("mix_hi")
        mix_lo = sem("mix_lo")
        relu_sq = sem("relu_sq")
        u_hi_made = sem("u_hi_made")
        u_lo_made = sem("u_lo_made")
        y_turned = sem("y_turned")
        y_evac = sem("y_evac")
        y_stored = sem("y_stored")

        U_V, U_K, U_Q, U_O, U_M = 2, 10, 18, 50, 82
        T_V, T_K, T_Q, T_O, T_M = 1, 5, 9, 25, 41
        BLK_U, BLK_T = 32, 24
        assert U_M + BLK_U * NBLK == 338

        w_f_v = w_fgate[0].rearrange("(k p) n -> p k n", p=P)
        w_qkv_v = w_qkv[0].rearrange("(k p) n -> p k n", p=P)
        w_o_v = w_o[0].rearrange("(k p) n -> p k n", p=P)
        w_up_v = w_up[0].rearrange("(k p) n -> p k n", p=P)
        w_down_v = w_down[0].rearrange("(k p) n -> p k n", p=P)

        kp = cache_k[0].rearrange("n p g d -> n p (g d)")
        vp = cache_v[0].rearrange("n p g d -> n p (g d)")

        def k_slot(p):
            return k_low[:, p, :] if p < 4 else k_high[:, p - 4, :]

        def page_numbers(engine, i, k, which):
            return [engine.value_load(pages[0:1, bass.ds((2 * i + k) * NPG + p, 1)] if not isinstance(i, int) else
                                      pages[0:1, (2 * i + k) * NPG + p:(2 * i + k) * NPG + p + 1],
                                      min_val=0, max_val=NPOOL - 1) for p in which]

        block = ctx.enter_context(nc.Block())

        @block.sync
        def _(sp):
            def load_unit(i, k, src):
                if not isinstance(i, int) or 4 * i + k >= 4:
                    sp.wait_ge(w_lo_made, 4 * i + (k - 3))
                sp.dma_start(w_raw[:, k % 4, :, 0:src.shape[2]], src).then_inc(w_loaded[k % 4], 16)

            def cols(view, half, col):
                return view[:, half * UC:(half + 1) * UC, col:col + P] if isinstance(col, int) else \
                    view[:, half * UC:(half + 1) * UC, bass.ds(col, P)]

            gw = D // 4
            for n in range(4):
                sp.dma_start(x_tok[:, 0:QT, n * gw:(n + 1) * gw],
                             x_prompt[0].rearrange("(t p) d -> p t d", p=P)[:, :, n * gw:(n + 1) * gw]
                             ).then_inc(x_loaded[n], 16)
                sp.dma_start(x_tok[0:NS, QT, n * gw:(n + 1) * gw],
                             x_sample.rearrange("b i d -> (b i) d")[:, n * gw:(n + 1) * gw]
                             ).then_inc(x_loaded[n], 16)
                if n == 0:
                    with nc.allow_non_contiguous_dma(reason="a small vector, one element a partition"):
                        sp.dma_start(g_attn[:], attn_norm[0].rearrange("(c p) -> p c", p=P)).then_inc(gain_loaded, 16)
            with nc.allow_non_contiguous_dma(reason="small vectors, one element a partition"):
                sp.dma_start(g_mlp[:], mlp_norm[0].rearrange("(c p) -> p c", p=P)).then_inc(const_loaded, 16)
                sp.dma_start(g_qk1[:, 0:1], k_norm.rearrange("o p -> p o")).then_inc(const_loaded, 16)
                sp.dma_start(g_qk1[:, 1:2], q_norm.rearrange("o p -> p o")).then_inc(const_loaded, 16)
                sp.dma_start(bf[:], b_fgate.rearrange("o h -> h o")).then_inc(const_loaded, 16)
            load_unit(0, 0, w_f_v[:, 0:UC, :])
            load_unit(0, 1, w_f_v[:, UC:KC, :])
            load_unit(0, 2, cols(w_qkv_v, 0, D + KVC))
            load_unit(0, 3, cols(w_qkv_v, 1, D + KVC))

            load_unit(1, 0, cols(w_qkv_v, 0, D + KVC + P))
            load_unit(1, 1, cols(w_qkv_v, 1, D + KVC + P))
            for n in range(2, NKV):
                for half in range(2):
                    u = U_V + 2 * n + half
                    load_unit(u // 4, u % 4, cols(w_qkv_v, half, D + KVC + n * P))
            for n in range(NKV):
                for half in range(2):
                    u = U_K + 2 * n + half
                    load_unit(u // 4, u % 4, cols(w_qkv_v, half, D + n * P))
                if n == 0:
                    sp.wait_ge(f_chain, 5)
                    sp.dma_start(c_rows, cT[:, 0:SEQ]).then_inc(c_stored, 16)
            with sp.Fori(0, NH // 2) as i:
                for k in range(4):
                    load_unit(i + (U_Q + k) // 4, (U_Q + k) % 4, cols(w_qkv_v, k % 2, i * (2 * P) + (k // 2) * P))
            for u in range(U_O, U_O + 4):
                k = u - U_O
                load_unit(u // 4, u % 4, cols(w_o_v, k % 2, (k // 2) * P))

            sp.wait_ge(c_stored, 16)
            sp.wait_ge(kv_turned, 1)

            def load_c_row(i, k):
                if not isinstance(i, int) or 4 * i + k >= 2:
                    sp.wait_ge(max_made, 16 * i + 4 * (k - 1))
                row = c_rows[bass.ds(4 * i + k, 1), :] if not isinstance(i, int) else c_rows[4 * i + k:4 * i + k + 1, :]
                sp.dma_start(c_row[:, k % 2, :], row.rearrange("o s -> (o s)").partition_broadcast(P)
                             ).then_inc(c_loaded[k % 2], 16)

            for k in range(2):
                load_c_row(0, k)

            sp.wait_ge(tokc_made, 1)
            sp.dma_start(nf_prompt[0, 0].rearrange("(t p) h -> p t h", p=P), tokc[:, 0:QT, :]).then_inc(lf_stored, 16)
            sp.dma_start(nf_sample[0].rearrange("b i h -> (b i) h"), tokc[0:NS, QT, :]).then_inc(lf_stored, 16)
            sp.wait_ge(vtok_made, 2 * NKV)
            sp.dma_start(nv_prompt[0, 0].rearrange("(t p) g d -> p t (g d)", p=P), v_tok[:, 0:QT, :]).then_inc(kv_stored, 16)
            sp.dma_start(nv_sample[0].rearrange("b i g d -> (b i) (g d)"), v_tok[0:NS, QT, :]).then_inc(kv_stored, 16)
            sp.wait_ge(ktok_made, 2 * NKV)
            sp.dma_start(nk_prompt[0, 0].rearrange("(t p) g d -> p t (g d)", p=P), k_tok[:, 0:QT, :]).then_inc(kv_stored, 16)
            sp.dma_start(nk_sample[0].rearrange("b i g d -> (b i) (g d)"), k_tok[0:NS, QT, :]).then_inc(kv_stored, 16)

            for k in range(2, 4):
                load_c_row(0, k)
            with sp.Fori(1, NKV) as i:
                for k in range(4):
                    load_c_row(i, k)

            sp.wait_ge(pages_loaded, 16)

            def load_pages(i, k):
                regs = page_numbers(sp, i, k, range(NPG))
                for p in range(NPG):
                    if not (isinstance(i, int) and 2 * i + k == 0):
                        sp.wait_ge(k_turned, (2 * i + k) * NPG + (p - 7))
                    elif p == 4:
                        sp.wait_ge(w_lo_made, U_O + 2)
                    sp.dma_start(k_slot(p), kp[bass.ds(regs[p], 1)].rearrange("o p f -> p (o f)")
                                 ).then_inc(page_loaded[p], 16)
                    if p < 4:
                        continue
                    if p == 4 and isinstance(i, int) and 2 * i + k == 0:
                        sp.wait_ge(out_evac, NH)
                    elif p == 4 and not (isinstance(i, int) and i == 0):
                        sp.wait_ge(s_pv, 2 * i + (k - 1))
                    sp.dma_start(v_page[:, k, p - 4, :], vp[bass.ds(regs[p - 4], 1)].rearrange("o p f -> p (o f)")
                                 ).then_inc(v_low_loaded[k], 16)

            load_pages(0, 0)
            load_pages(0, 1)
            with sp.Fori(1, NB // 2) as i:
                for k in range(2):
                    load_pages(i, k)

            sp.wait_ge(k_turned, NB * NPG)
            for u in range(U_O + 4, U_O + 6):
                k = u - U_O
                load_unit(u // 4, u % 4, cols(w_o_v, k % 2, (k // 2) * P))
            with sp.Fori(0, 6) as i:
                for k in range(4):
                    u = U_O + 6 + k
                    load_unit(i + u // 4, u % 4, cols(w_o_v, k % 2, i * (2 * P) + (3 + k // 2) * P))
            for u in range(U_O + 30, U_O + 32):
                k = u - U_O
                load_unit(u // 4, u % 4, cols(w_o_v, k % 2, (k // 2) * P))
            with sp.Fori(0, NBLK) as j:
                with sp.Fori(0, FB // 2) as i:
                    for k in range(4):
                        u = U_M + k
                        load_unit(j * (BLK_U // 4) + i + u // 4, u % 4,
                                  cols(w_up_v, k % 2, j * (FB * P) + i * (2 * P) + (k // 2) * P))
                with sp.Fori(0, KC // 4) as i:
                    for k in range(4):
                        u = U_M + 2 * FB + k
                        sp.wait_ge(w_lo_made, j * BLK_U + i * 4 + (u - 3))
                        sp.dma_start(w_raw[:, u % 4, :, :],
                                     w_down_v[:, bass.ds(j * FB, FB), bass.ds(i * (4 * P) + k * P, P)]
                                     ).then_inc(w_loaded[u % 4], 16)
            for c in range(KC):
                sp.wait_ge(y_evac, 2 * c + 1)
                sp.dma_start(y_prompt[0].rearrange("(t p) d -> p t d", p=P)[:, :, c * P:(c + 1) * P],
                             y_tok[:, 0:QT, c * P:(c + 1) * P]).then_inc(y_stored, 16)
                sp.wait_ge(y_evac, 2 * c + 2)
                sp.dma_start(y_sample.rearrange("b i d -> (b i) d")[:, c * P:(c + 1) * P],
                             y_tok[0:NS, QT, c * P:(c + 1) * P]).then_inc(y_stored, 16)
            sp.wait_ge(y_stored, 32 * KC)
            sp.wait_ge(kv_stored, 64)
            sp.wait_ge(lf_stored, 32)

        @block.gpsimd
        def _(pool):
            nc.gpsimd.memset(ident[:], 0.0).then_inc(const_made, 1)
            nc.gpsimd.memset(ones[:], 1.0).then_inc(const_made, 1)
            nc.gpsimd.memset(causal[:], 0.0).then_inc(const_made, 1)
            nc.gpsimd.memset(eps_t[:], EPS).then_inc(const_made, 1)
            pool.wait_ge(const_made, 4)
            nc.gpsimd.affine_select(out=ident[:], in_=ident[:], compare_op=ALU.not_equal, fill=1.0, base=0,
                                    pattern=[[-1, P]], channel_multiplier=1).then_inc(const_made, 1)
            nc.gpsimd.affine_select(out=tri[:], in_=ones[:], compare_op=ALU.is_ge, fill=0.0, base=0,
                                    pattern=[[1, P]], channel_multiplier=-1).then_inc(const_made, 1)
            nc.gpsimd.affine_select(out=causal[:], in_=causal[:], compare_op=ALU.is_ge, fill=BIG, base=0,
                                    pattern=[[-1, P]], channel_multiplier=1).then_inc(const_made, 1)
            nc.gpsimd.memset(earlier[:], 0.0).then_inc(const_made, 1)
            nc.gpsimd.affine_select(out=own[:], in_=ones[:, 0:NB * NB].rearrange("p (a b) -> p a b", a=NB),
                                    compare_op=ALU.is_equal, fill=0.0, base=0,
                                    pattern=[[1, NB], [-1, NB]], channel_multiplier=0).then_inc(const_made, 1)
            nc.gpsimd.affine_select(out=expand[:].rearrange("p (g h i) -> p g h i", g=NKV, i=DS),
                                    in_=ones[0:NH, :].rearrange("p (g h i) -> p g h i", g=NKV, i=DS),
                                    compare_op=ALU.is_equal, fill=0.0, base=0,
                                    pattern=[[-GRP, NKV], [-1, R // DS], [0, DS]], channel_multiplier=1
                                    ).then_inc(const_made, 1)
            nc.gpsimd.affine_select(out=s_outr[:].rearrange("p (i a) -> p i a", i=DS),
                                    in_=ones[:].rearrange("p (i a) -> p i a", i=DS),
                                    compare_op=ALU.is_equal, fill=0.0, base=0,
                                    pattern=[[-1, DS], [-DS, P // DS]], channel_multiplier=1
                                    ).then_inc(const_made, 1)
            n_const = 11
            for d in range(1, NPG):
                pool.wait_ge(const_made, n_const)
                nc.gpsimd.affine_select(out=earlier[:], in_=earlier[:], compare_op=ALU.not_equal, fill=1.0,
                                        base=d * NH, pattern=[[-1, P]], channel_multiplier=1
                                        ).then_inc(const_made, 1)
                n_const += 1
            pool.dma_start(pages[:], page_table.rearrange("(o b) n -> o (b n)", o=1)).then_inc(pages_loaded, 16)
            pool.wait_ge(const_loaded, 16 * 4)
            nc.gpsimd.tensor_copy(g_kq[:, 0:NKV], g_qk1[:, 0:1].to_broadcast([P, NKV])).then_inc(gains_made, 1)
            nc.gpsimd.tensor_copy(g_kq[:, NKV:NKV + NH], g_qk1[:, 1:2].to_broadcast([P, NH])).then_inc(gains_made, 1)

            def load_cached_gates(a, b):
                with pool.Fori(a, b) as i:
                    regs = [pool.value_load(pages[0:1, bass.ds(i * NPG + p, 1)], min_val=0, max_val=NPOOL - 1)
                            for p in range(NPG)]
                    for p in range(NPG):
                        pool.dma_start(lf_page[:, bass.ds(i * NPG + p, 1), :],
                                       cache_logf[0, bass.ds(regs[p], 1)].rearrange("o p h -> p o h")
                                       ).then_inc(lf_loaded, 16)

            def add_squares(n):
                for c in range(1, KC):
                    pool.wait_ge(sq_made, KC * n + c + 1)
                    if n or c > 1:
                        pool.wait_ge(sq_added, (KC - 1) * n + c - 1)
                    nc.gpsimd.tensor_tensor(tmp_c[:, 0, :], tmp_c[:, 0, :], tmp_b[:, c % 2, :], ALU.add
                                            ).then_inc(sq_added, 1)

            add_squares(0)
            pool.wait_ge(pages_loaded, 16)
            pool.wait_ge(x_turned, KC)
            load_cached_gates(0, NB)

            pool.wait_ge(csum_evac, 3)
            for p in range(NPG):
                pool.dma_start(c_cache[:, :, p, :].rearrange("b h p -> h b p"), c_pg[p * NH:(p + 1) * NH]
                               ).then_inc(c_cached, 16)

            def stage(i, k):
                later = not isinstance(i, int) or 4 * i + k >= 2
                if not later and k == 0:
                    pool.wait_ge(kv_turned, 1)
                if later:
                    pool.wait_ge(score_done, 16 * i + 4 * (k - 1))
                nc.gpsimd.tensor_copy(q_st[:, k % 2, :], kq[:, bass.ds(4 * i + (k + NKV), 1), 0:SEQ].rearrange("p o s -> p (o s)")
                                      if not isinstance(i, int) else kq[:, 4 * i + k + NKV, 0:SEQ]).then_inc(q_staged, 1)
                if later:
                    pool.wait_ge(max_made, 16 * i + 4 * (k - 1))
                pool.wait_ge(c_loaded[k % 2], 32 * i + 16 * (k // 2) + 16)
                nc.gpsimd.tensor_tensor(c_diag[:, k % 2], c_row[:, k % 2].rearrange("p (t s) -> p t s", s=P),
                                        causal[:].unsqueeze(1).to_broadcast([P, QT, P]), ALU.add
                                        ).then_inc(cdiag_made, 1)
                if k == 3:
                    if not isinstance(i, int) or i >= 1:
                        pool.wait_ge(pv_done, 4 * i)
                    elif isinstance(i, int):
                        pool.wait_ge(vtok_made, 2 * NKV)
                    nc.gpsimd.tensor_copy(v_st[:], v_tok[:, 0:QT, bass.ds(i * P, P)] if not isinstance(i, int)
                                          else v_tok[:, 0:QT, i * P:(i + 1) * P]).then_inc(v_staged, 1)

            for k in range(4):
                stage(0, k)
            pool.wait_ge(head_done, NKV + NH)
            nc.gpsimd.memset(c_dec[:], 0.0).then_inc(cdec_zeroed, 1)
            with pool.Fori(1, NKV) as i:
                for k in range(4):
                    stage(i, k)

            pool.wait_ge(c_cached, 16 * NPG)
            pool.wait_ge(cdec_zeroed, 1)

            def load_high_values(i, k, regs):
                if not isinstance(i, int) or i >= 1:
                    pool.wait_ge(s_pv, 2 * i + (k - 1))
                elif k == 0:
                    pool.wait_ge(out_evac, NH)
                for p in range(NPG // 2, NPG):
                    pool.dma_start(v_page[:, k, p, :], vp[bass.ds(regs[p - NPG // 2], 1)].rearrange("o p f -> p (o f)")
                                   ).then_inc(v_high_loaded[k], 16)

            def pack(i, k, before):
                c0 = SEQ + 2 * DS * i + DS * k
                if before is not None:
                    regs = page_numbers(pool, *before, range(NPG // 2, NPG))
                if not isinstance(i, int) or i >= 1:
                    pool.wait_ge(new_scored, 2 * i + (k - 1))
                src = kq[:, NKV:NKV + NH, c0:c0 + DS] if isinstance(i, int) else kq[:, NKV:NKV + NH, bass.ds(c0, DS)]
                nc.gpsimd.tensor_copy(q_pack[:, k, :, 0:RQ].rearrange("p g (h i) -> p g h i", i=DS),
                                      src.rearrange("p (g h) i -> p g h i", g=NKV))
                nc.gpsimd.tensor_copy(k_pack[:, k], kq[:, 0:NKV, c0:c0 + DS] if isinstance(i, int) else
                                      kq[:, 0:NKV, bass.ds(c0, DS)]).then_inc(q_packed, 1)
                if before is not None:
                    load_high_values(*before, regs)
                if not isinstance(i, int) or i >= 1:
                    pool.wait_ge(s_logit, 4 * i + 2 * (k - 1))
                for g in range(NKV):
                    rows = c_cache[2 * i + k, g * GRP:(g + 1) * GRP].rearrange("h n p -> h (n p)") \
                        if isinstance(i, int) else \
                        c_cache[bass.ds(2 * i + k, 1), g * GRP:(g + 1) * GRP].rearrange("o h n p -> (o h) (n p)")
                    pool.dma_start(c_dec[g * R:g * R + RQ, k, :],
                                   rows.unsqueeze(1).to_broadcast([GRP, DS, PAST])).then_inc(cdec_loaded[k], 16)

            pack(0, 0, None)
            pack(0, 1, (0, 0))
            pack(1, 0, (0, 1))
            pack(1, 1, (1, 0))
            with pool.Fori(2, NB // 2) as i:
                pack(i, 0, (i - 1, 1))
                pack(i, 1, (i, 0))
            load_high_values(NB // 2 - 1, 1, page_numbers(pool, NB // 2 - 1, 1, range(NPG // 2, NPG)))

            add_squares(1)

        @block.scalar
        def _(act):
            def split(i, k):
                act.wait_ge(w_loaded[k % 4], 16 * i + (k // 4) * 16 + 16)
                if not isinstance(i, int) or 4 * i + k >= 2:
                    act.wait_ge(unit_used, 4 * i + (k - 1))
                nc.scalar.copy(w_hi[:, k % 2], w_raw[:, k % 4]).then_inc(w_hi_made, 1)

            def gained_hi(gain, c):
                nc.scalar.activation(act_hi[:, c, :], xT[:, c, :], ACT.Identity, scale=gain[:, c:c + 1]
                                     ).then_inc(act_hi_made, 1)

            act.wait_ge(const_made, 4)
            act.wait_ge(gain_loaded, 16)
            for c in range(KC):
                act.wait_ge(xT_made, c + 1)
                gained_hi(g_attn, c)
                if c >= 3:
                    act.wait_ge(sq_added, c - 2)
                dst = tmp_c[:, 0, :] if c == 0 else tmp_b[:, c % 2, :]
                nc.scalar.activation(dst, xT[:, c, :], ACT.Square).then_inc(sq_made, 1)
                if c == KC - 4:
                    act.wait_ge(gains_made, 3)
                    split(0, 0)
            split(0, 1)

            def root_of_mean(n):
                act.wait_ge(ssq_ready, n + 1)
                nc.scalar.activation(halves(tmp_a[:, 0, :]), acc(2), ACT.Sqrt, bias=eps_t[:], scale=1.0 / D
                                     ).then_inc(std_ready, 1)

            split(0, 2)
            split(0, 3)
            root_of_mean(0)
            split(1, 0)
            act.wait_ge(f_chain, 3)
            nc.scalar.activation(fe[:], fz[:, 1, :], ACT.Exp).then_inc(f_exp, 1)
            act.wait_ge(f_exp, 1)
            nc.scalar.activation(fe[:], fe[:], ACT.Ln, bias=1.0).then_inc(f_exp, 1)
            split(1, 1)

            for u in range(U_V + 4, U_K + 2):
                split(u // 4, u % 4)

            def head_root(m):
                if not (isinstance(m, int) and m == 0):
                    act.wait_ge(head_done, m)
                act.wait_ge(head_ssq, m + 1)
                nc.scalar.activation(halves(tmp_c[:, 0, :]), acc(2), ACT.Sqrt, bias=eps_t[:], scale=1.0 / HD
                                     ).then_inc(head_std, 1)

            def kq_tile(i, k, u0, t0, m0):
                u, t, m = u0 + 2 * k, t0 + k, m0 + k
                first = isinstance(i, int) and m + 2 * i == 0
                split(i + (u + 2) // 4, (u + 2) % 4)
                if not first:
                    head_root(2 * i + m - 1)
                split(i + (u + 3) // 4, (u + 3) % 4)
                act.wait_ge(acc_free[t % 2], i + t // 2 + 1)
                nc.scalar.activation(tmp_b[:, 0, :], tmp_a[:, m % 2, :], ACT.Square).then_inc(head_sq, 1)
                act.wait_ge(head_sq, 4 * i + (2 * m + 1))
                nc.scalar.copy(sq_hi[:], tmp_b[:, 0, :]).then_inc(head_sq, 1)

            act.wait_ge(c_stored, 16)
            nc.scalar.copy(ones_r[:], ones[:])
            for i in range(NKV // 2):
                for k in range(2):
                    kq_tile(i, k, U_K, T_K, 0)
            with act.Fori(0, NH // 2) as i:
                for k in range(2):
                    kq_tile(i, k, U_Q, T_Q, NKV)

            def take_v(g):
                act.wait_ge(kv_turned, g + 1)
                o = TURN_AT[g % 2]
                nc.scalar.copy(v_tok[:, 0:QT, g * P:(g + 1) * P],
                               psf[:, o:o + SEQ].rearrange("p (t d) -> p t d", d=P)).then_inc(vtok_made, 1)
                nc.scalar.copy(v_tok[0:NS, QT, g * P:(g + 1) * P], psf[0:NS, o + SEQ:o + SEQ + P]
                               ).then_inc(vtok_made, 1)

            def logits(i, k):
                for t in range(QT):
                    w = (t + 1) * P
                    act.wait_ge(score_done, 16 * i + 4 * k + t + 1)
                    if t == 0 and not isinstance(i, int):
                        act.wait_ge(p_turned, 4 * i + (k - 3))
                    bias = tokc[:, TT + t, bass.ds(4 * i + k, 1)] if not isinstance(i, int) else \
                        tokc[:, TT + t, 4 * i + k:4 * i + k + 1]
                    nc.scalar.activation(probs[:, k, t, 0:w], ps[:, t, 0:w], ACT.Identity, bias=bias, scale=SCALE
                                         ).then_inc(logit_made, 1)

            def exps(i, k):
                if not isinstance(i, int) or 4 * i + k >= 2:
                    act.wait_ge(rinv_made, 4 * i + (k - 1))
                for t in range(QT):
                    w = (t + 1) * P
                    act.wait_ge(max_made, 16 * i + 4 * k + t + 1)
                    nc.scalar.activation(probs[:, k, t, 0:w], probs[:, k, t, 0:w], ACT.Exp,
                                         bias=nmax[:, k % 2, t:t + 1], accum_out=rsum[:, k % 2, t:t + 1]
                                         ).then_inc(exp_made, 1)

            def take_pT(i, k):
                act.wait_ge(p_turned, 4 * i + k + 1)
                if not isinstance(i, int) or 4 * i + k >= 2:
                    act.wait_ge(pv_done, 4 * i + (k - 1))
                nc.scalar.copy(pT[:, k % 2, 0:4 * P], ps[:, 4, :]).then_inc(pT_act, 1)

            def take_out(i, k):
                act.wait_ge(pv_done, 4 * i + k + 1)
                dst = kq[:, bass.ds(4 * i + (k + NKV), 1), 0:SEQ].rearrange("p o s -> p (o s)") \
                    if not isinstance(i, int) else kq[:, 4 * i + k + NKV, 0:SEQ]
                nc.scalar.copy(dst, ps[:, 7, :]).then_inc(out_evac, 1)

            take_v(0)
            for k in range(4):
                logits(0, k)
                if k == 0:
                    head_root(NKV + NH - 1)
                    for g in range(1, NKV):
                        take_v(g)
                exps(0, k)
                if k == 2:
                    act.wait_ge(kv_stored, 64)
                if k >= 2:
                    take_pT(0, k - 2)
                if k >= 3:
                    take_out(0, k - 3)
            with act.Fori(1, NKV) as i:
                for k in range(4):
                    logits(i, k)
                    exps(i, k)
                    take_pT(*((i, k - 2) if k >= 2 else (i - 1, k + 2)))
                    take_out(*((i, k - 3) if k >= 3 else (i - 1, k + 1)))
            take_pT(NKV - 1, 2)
            take_out(NKV - 1, 1)
            take_pT(NKV - 1, 3)
            take_out(NKV - 1, 2)
            take_out(NKV - 1, 3)

            def take_kT(i, k, p):
                act.wait_ge(k_turned, 2 * NPG * i + NPG * k + p + 1)
                if p % 4 == 0 and not (isinstance(i, int) and 2 * i + k == 0):
                    act.wait_ge(half_scored, 4 * i + 2 * k + p // 4 - 1)
                nc.scalar.copy(kcT[:, p // 4, :, (p % 4) * P:(p % 4 + 1) * P],
                               ps[:, 0, :].rearrange("p (g n) -> p g n", g=NKV)).then_inc(kcT_act, 1)

            def s_exps(i, k):
                act.wait_ge(s_bias, 2 * i + k + 1)
                if not isinstance(i, int) or 2 * i + k >= 2:
                    act.wait_ge(s_scaled, 2 * i + (k - 1))
                nc.scalar.activation(sprob[:, k, 0:PAST + DS], sprob[:, k, 0:PAST + DS], ACT.Exp,
                                     bias=s_nbias[:, k], accum_out=s_rsum[:, k]).then_inc(s_exp, 1)

            def take_spT(i, k):
                act.wait_ge(s_turned, 2 * i + k + 1)
                if not (isinstance(i, int) and 2 * i + k == 0):
                    act.wait_ge(s_pv, 2 * i + k)
                nc.scalar.copy(spT[:].rearrange("p n r -> p (n r)"), psf[:, 5 * 512:7 * 512]).then_inc(spT_made, 1)

            def s_step(i, k, prev):
                take_kT(i, k, 0)
                take_kT(i, k, 2)
                if prev is not None:
                    s_exps(*prev)
                take_kT(i, k, 4)
                if prev is not None:
                    take_spT(*prev)
                take_kT(i, k, 6)

            s_step(0, 0, None)
            s_step(0, 1, (0, 0))
            s_step(1, 0, (0, 1))
            s_step(1, 1, (1, 0))
            with act.Fori(2, NB // 2) as i:
                s_step(i, 0, (i - 1, 1))
                s_step(i, 1, (i, 0))
            s_exps(NB // 2 - 1, 1)
            take_spT(NB // 2 - 1, 1)

            act.wait_ge(s_out, NB)
            for c in range(KC):
                nc.scalar.copy(act_hi[:, c, :], kq[:, NKV + c, :]).then_inc(mix_hi, 1)

            def o_tile(i, k, start):
                u, t = U_O + 2 * k, T_O + k
                split(i + (u + 2) // 4, (u + 2) % 4)
                split(i + (u + 3) // 4, (u + 3) % 4)
                o_square(i, k, start)

            def o_square(i, k, start):
                t = T_O + k
                act.wait_ge(acc_free[t % 2], i + t // 2 + 1)
                if not start:
                    act.wait_ge(sq_added, 2 * i + (KC - 3 + k))
                src = xT[:, 2 * i + k, :] if isinstance(i, int) else \
                    xT[:, bass.ds(2 * i + k, 1), :].rearrange("p o t -> p (o t)")
                nc.scalar.activation(tmp_c[:, 0, :] if start and k == 0 else tmp_b[:, k, :], src, ACT.Square
                                     ).then_inc(sq_made, 1)

            o_tile(0, 0, True)
            o_tile(0, 1, True)
            with act.Fori(1, KC // 2 - 1) as i:
                for k in range(2):
                    o_tile(i, k, False)
            o_tile(KC // 2 - 1, 0, False)
            split(U_M // 4, U_M % 4)
            act.wait_ge(unit_used, U_M)
            for c in range(KC):
                if c == 2:
                    split((U_M + 1) // 4, (U_M + 1) % 4)
                if c == 4:
                    o_square(KC // 2 - 1, 1, False)
                gained_hi(g_mlp, c)
            root_of_mean(1)

            def up_tile(j, i, k):
                u, t = U_M + 2 * k, T_M + k
                split(j * (BLK_U // 4) + i + (u + 2) // 4, (u + 2) % 4)
                split(j * (BLK_U // 4) + i + (u + 3) // 4, (u + 3) % 4)
                act.wait_ge(acc_free[t % 2], j * (BLK_T // 2) + i + (t // 2 + 1))
                nc.scalar.activation(tmp_b[:, k, :], tmp_a[:, k, :], ACT.Square).then_inc(relu_sq, 1)
                act.wait_ge(relu_sq, j * FB + 2 * i + (k + 1))
                nc.scalar.copy(u_hi[:, bass.ds(2 * i + k, 1), :].rearrange("p o t -> p (o t)"), tmp_b[:, k, :]
                               ).then_inc(u_hi_made, 1)

            def up_tiles(j):
                with act.Fori(0, FB // 2) as i:
                    for k in range(2):
                        up_tile(j, i, k)

            def down_units(j, i, ks):
                for k in ks:
                    u = U_M + 2 * FB + k
                    split(j * (BLK_U // 4) + i + (u + 2) // 4, (u + 2) % 4)

            with act.Fori(0, NBLK - 1) as j:
                up_tiles(j)
                with act.Fori(0, KC // 4) as i:
                    down_units(j, i, range(4))
            up_tiles(NBLK - 1)
            with act.Fori(0, KC // 4 - 1) as i:
                down_units(NBLK - 1, i, range(4))

            def take_y(c):
                act.wait_ge(y_turned, c + 1)
                o = 2048 + 1024 * (c % 2)
                nc.scalar.copy(y_tok[:, 0:QT, c * P:(c + 1) * P], psf[:, o:o + SEQ].rearrange("p (t d) -> p t d", d=P)
                               ).then_inc(y_evac, 1)
                nc.scalar.copy(y_tok[0:NS, QT, c * P:(c + 1) * P], psf[0:NS, o + SEQ:o + SEQ + P]).then_inc(y_evac, 1)

            for k in range(2):
                down_units(NBLK - 1, KC // 4 - 1, [k])
                for c in range(3 * k, 3 * k + 3):
                    take_y(c)
            for c in range(6, KC):
                take_y(c)

        @block.vector
        def _(dve):
            def split(i, k):
                dve.wait_ge(w_hi_made, 4 * i + k + 1)
                nc.vector.tensor_tensor(w_lo[:, k % 2], w_raw[:, k % 4], w_hi[:, k % 2], ALU.subtract
                                        ).then_inc(w_lo_made, 1)

            for k in range(2):
                nc.vector.memset(w_raw[:, k, :, NH:P], 0.0)
            nc.vector.memset(q_pack[:], 0.0).then_inc(gains_made, 1)

            def gained_lo(n, gain, c):
                dve.wait_ge(act_hi_made, KC * n + c + 1)
                nc.vector.scalar_tensor_tensor(out=act_lo[:, c, :], in0=xT[:, c, :], scalar=gain[:, c:c + 1],
                                               in1=act_hi[:, c, :], op0=ALU.mult, op1=ALU.subtract
                                               ).then_inc(act_lo_made, 1)

            def rms_inverse(n):
                dve.wait_ge(std_ready, n + 1)
                nc.vector.reciprocal(rstd, tmp_a[:, 0, :]).then_inc(rstd_ready, 1)
                dve.wait_ge(rstd_ready, n + 1)

            def take_scaled(dst, t, u_done, rows=P):
                dve.wait_ge(unit_used, u_done)
                return nc.vector.tensor_tensor(halves(dst), acc(t % 2, rows), halves(rstd[0:rows]), ALU.mult)

            for c in range(KC + 1):
                if c < KC:
                    dve.wait_ge(x_turned, c + 1)
                    o = 2048 + 1024 * (c % 2)
                    nc.vector.tensor_copy(xT[:, c, :], psf[:, o:o + T]).then_inc(xT_made, 1)
                if c:
                    gained_lo(0, g_attn, c - 1)
                if c == KC - 3:
                    split(0, 0)
            split(0, 1)

            dve.wait_ge(const_made, 11)
            nc.vector.tensor_reduce(tok_sel[:], s_outr[:].rearrange("p (i a) -> p i a", i=DS), AX.X, ALU.add
                                    ).then_inc(sel_made, 1)
            nc.vector.memset(tok_mask[:, 0:1], 0.0).then_inc(sel_made, 1)
            for n in range(1, DS):
                dve.wait_ge(sel_made, n + 1)
                nc.vector.scalar_tensor_tensor(out=tok_mask[:, n:n + 1], in0=tok_sel[:, n - 1:n], scalar=BIG,
                                               in1=tok_mask[:, n - 1:n], op0=ALU.mult, op1=ALU.add
                                               ).then_inc(sel_made, 1)
            split(0, 2)
            split(0, 3)
            rms_inverse(0)
            take_scaled(fz[:, 0, :], 0, U_V, NH).then_inc(acc_free[0], 1)
            dve.wait_ge(acc_free[0], 1)
            dve.wait_ge(const_loaded, 16 * 4)
            nc.vector.tensor_scalar(fz[:, 0, :], fz[:, 0, :], bf[:, 0:1], None, ALU.add).then_inc(f_chain, 1)
            dve.wait_ge(f_chain, 1)
            nc.vector.tensor_scalar(fz[:, 1, :], fz[:, 0, :], 0.0, -2.0, ALU.max, ALU.mult).then_inc(f_chain, 1)
            dve.wait_ge(f_chain, 2)
            nc.vector.tensor_tensor(fz[:, 1, :], fz[:, 1, :], fz[:, 0, :], ALU.add).then_inc(f_chain, 1)
            split(1, 0)
            dve.wait_ge(f_exp, 2)
            nc.vector.scalar_tensor_tensor(out=lfT[:], in0=fz[:, 0, :], scalar=0.0, in1=fe[:],
                                           op0=ALU.min, op1=ALU.subtract).then_inc(f_chain, 1)
            dve.wait_ge(f_chain, 4)
            new_lf = lfT[:, SEQ:T].rearrange("p (b i) -> p b i", i=DS)
            new_c = cT[:, SEQ:T].rearrange("p (b i) -> p b i", i=DS)
            nc.vector.tensor_copy(new_c[:, :, 0], new_lf[:, :, 0]).then_inc(new_chain, 1)
            for n in range(1, DS):
                dve.wait_ge(new_chain, n)
                nc.vector.tensor_tensor(new_c[:, :, n], new_c[:, :, n - 1], new_lf[:, :, n], ALU.add
                                        ).then_inc(new_chain, 1)
            nc.vector.tensor_tensor_scan(cT[:, 0:SEQ], ones[0:NH, 0:1].to_broadcast([NH, SEQ]), lfT[:, 0:SEQ], 0.0,
                                         ALU.mult, ALU.add).then_inc(f_chain, 1)

            split(1, 1)
            def v_take(n):
                take_scaled(vT[:, n, :], T_V + n, U_V + 2 * n + 2).then_inc(acc_free[(T_V + n) % 2], 1)

            def v_tile(n):
                for u in range(U_V + 2 * n + 2, U_V + 2 * n + 4):
                    split(u // 4, u % 4)
                v_take(n)

            v_take(0)
            v_tile(1)
            dve.wait_ge(f_turned, 1)
            nc.vector.tensor_copy(tokc[:, 0:QT], ps[:, 6, 0:QT * NH].rearrange("p (t h) -> p t h", h=NH))
            nc.vector.tensor_copy(tokc[0:NS, QT], ps[0:NS, 6, QT * NH:TT * NH])
            nc.vector.tensor_copy(tokc[:, TT:], ps[:, 6, TT * NH:(TT + QT) * NH].rearrange("p (t h) -> p t h", h=NH)
                                  ).then_inc(tokc_made, 1)
            nc.vector.tensor_copy(new_sum[:].rearrange("p b i -> p (b i)"), ps[:, 7, 0:NS]).then_inc(new_spread, 1)
            dve.wait_ge(new_spread, 1)
            dve.wait_ge(sel_made, 1 + DS)
            nc.vector.tensor_tensor(new_key[:], new_sum[:], tok_mask[:].unsqueeze(1).to_broadcast([P, NB, DS]),
                                    ALU.add).then_inc(new_spread, 1)
            dve.wait_ge(new_spread, 2)
            nc.vector.tensor_tensor(new_sum[:], new_sum[:], tok_sel[:].unsqueeze(1).to_broadcast([P, NB, DS]),
                                    ALU.mult).then_inc(new_spread, 1)
            dve.wait_ge(new_spread, 3)
            nc.vector.tensor_reduce(new_q[:], new_sum[:], AX.X, ALU.add).then_inc(new_spread, 1)
            for n in range(2, NKV):
                v_tile(n)

            def norm_head(m, s):
                if not (isinstance(m, int) and m == 0):
                    dve.wait_ge(head_done, m)
                dve.wait_ge(head_std, m + 1)
                nc.vector.reciprocal(tmp_c[:, 0, :], tmp_c[:, 0, :]).then_inc(head_rec, 1)
                dve.wait_ge(head_rec, m + 1)
                dst = kq[:, m, :] if isinstance(m, int) else kq[:, bass.ds(m, 1), :].rearrange("p o t -> p (o t)")
                gain = g_kq[:, m:m + 1] if isinstance(m, int) else g_kq[:, bass.ds(m, 1)]
                nc.vector.scalar_tensor_tensor(out=dst, in0=tmp_a[:, s, :], scalar=gain, in1=tmp_c[:, 0, :],
                                               op0=ALU.mult, op1=ALU.mult).then_inc(head_done, 1)

            def kq_tile(i, k, u0, t0, m0):
                u, t, m = u0 + 2 * k, t0 + k, m0 + k
                split(i + (u + 2) // 4, (u + 2) % 4)
                if k == 1 and m0 and not isinstance(i, int):
                    dve.wait_ge(c_cached, 16 * NPG)
                if not (isinstance(i, int) and m + 2 * i == 0):
                    norm_head(2 * i + (m - 1), (m - 1) % 2)
                split(i + (u + 3) // 4, (u + 3) % 4)
                take_scaled(tmp_a[:, m % 2, :], t, 4 * i + u + 2).then_inc(acc_free[t % 2], 1)
                dve.wait_ge(head_sq, 4 * i + (2 * m + 2))
                nc.vector.tensor_tensor(sq_lo[:], tmp_b[:, 0, :], sq_hi[:], ALU.subtract).then_inc(head_lo, 1)

            dve.wait_ge(gains_made, 3)
            dve.wait_ge(c_stored, 16)
            for i in range(NKV // 2):
                for k in range(2):
                    kq_tile(i, k, U_K, T_K, 0)
            for k in range(2):
                kq_tile(0, k, U_Q, T_Q, NKV)
            dve.wait_ge(csum_done, 1)
            nc.vector.tensor_copy(c_pg[:].rearrange("p b n -> p (b n)"), psf[:, 3072:4096]).then_inc(csum_evac, 1)
            for k in range(2):
                kq_tile(1, k, U_Q, T_Q, NKV)
            dve.wait_ge(csum_done, 2)
            nc.vector.tensor_copy(pg_off[:], ps[:, 6, 0:NB]).then_inc(csum_evac, 1)
            dve.wait_ge(csum_evac, 2)
            nc.vector.tensor_tensor(c_pg[:], c_pg[:], pg_off[:].unsqueeze(2).to_broadcast([P, NB, PAGE]), ALU.add
                                    ).then_inc(csum_evac, 1)
            with dve.Fori(2, NH // 2) as i:
                for k in range(2):
                    kq_tile(i, k, U_Q, T_Q, NKV)
            def take_k(g):
                dve.wait_ge(kv_turned, NKV + g + 1)
                o = TURN_AT[g % 2]
                nc.vector.tensor_copy(k_tok[:, 0:QT, g * P:(g + 1) * P],
                                      psf[:, o:o + SEQ].rearrange("p (t d) -> p t d", d=P)
                                      ).then_inc(ktok_made, 1)
                nc.vector.tensor_copy(k_tok[0:NS, QT, g * P:(g + 1) * P], psf[0:NS, o + SEQ:o + SEQ + P]
                                      ).then_inc(ktok_made, 1)

            def bias_and_max(i, k):
                dve.wait_ge(cdiag_made, 4 * i + k + 1)
                for t in range(QT):
                    dve.wait_ge(logit_made, 16 * i + 4 * k + t + 1)
                    if t:
                        nc.vector.tensor_tensor(probs[:, k, t, 0:t * P], probs[:, k, t, 0:t * P],
                                                c_row[:, k % 2, 0:t * P], ALU.subtract)
                    ins = nc.vector.tensor_tensor(probs[:, k, t, t * P:(t + 1) * P], probs[:, k, t, t * P:(t + 1) * P],
                                                  c_diag[:, k % 2, t], ALU.subtract)
                    ins.then_inc(bias_sub, 1)
                    dve.wait_ge(bias_sub, 16 * i + 4 * k + t + 1)
                    nc.vector.tensor_reduce(nmax[:, k % 2, t:t + 1], probs[:, k, t, 0:(t + 1) * P], AX.X, ALU.max,
                                            negate=True).then_inc(max_made, 1)

            def normalise(i, k):
                dve.wait_ge(exp_made, 16 * i + 4 * k + 4)
                nc.vector.reciprocal(rinv[:, k % 2, :], rsum[:, k % 2, :]).then_inc(rinv_made, 1)
                dve.wait_ge(rinv_made, 4 * i + k + 1)
                for t in range(QT):
                    w = (t + 1) * P
                    ins = nc.vector.tensor_scalar(probs[:, k, t, 0:w], probs[:, k, t, 0:w],
                                                  rinv[:, k % 2, t:t + 1], None, ALU.mult)
                ins.then_inc(normed, 1)

            def take_pT(i, k):
                dve.wait_ge(p_turned, 4 * i + k + 1)
                if not isinstance(i, int) or 4 * i + k >= 2:
                    dve.wait_ge(pv_done, 4 * i + (k - 1))
                nc.vector.tensor_copy(pT[:, k % 2, 4 * P:10 * P], psf[:, 5 * 512:5 * 512 + 6 * P]).then_inc(pT_dve, 1)

            for k in range(4):
                bias_and_max(0, k)
                if k == 0:
                    for g in range(NKV):
                        take_k(g)
                if k >= 1:
                    normalise(0, k - 1)
                if k == 2:
                    norm_head(NKV + NH - 1, 1)
                if k == 2:
                    dve.wait_ge(kv_stored, 64)
                if k >= 2:
                    take_pT(0, k - 2)
            with dve.Fori(1, NKV) as i:
                for k in range(4):
                    bias_and_max(i, k)
                    normalise(*((i, k - 1) if k >= 1 else (i - 1, 3)))
                    take_pT(*((i, k - 2) if k >= 2 else (i - 1, k + 2)))
            normalise(NKV - 1, 3)
            take_pT(NKV - 1, 2)
            take_pT(NKV - 1, 3)

            def take_kT(i, k, p):
                dve.wait_ge(k_turned, 2 * NPG * i + NPG * k + p + 1)
                if p % 4 == 1 and not (isinstance(i, int) and 2 * i + k == 0):
                    dve.wait_ge(half_scored, 4 * i + 2 * k + p // 4 - 1)
                nc.vector.tensor_copy(kcT[:, p // 4, :, (p % 4) * P:(p % 4 + 1) * P],
                                      ps[:, 1, :].rearrange("p (g n) -> p g n", g=NKV)).then_inc(kcT_dve, 1)

            def s_logits(i, k):
                b = 2 * i + k
                sl = (lambda t, n: t[:, b, :] if n else t[:, b:b + 1]) if isinstance(i, int) else \
                    (lambda t, n: t[:, bass.ds(b, 1), :].rearrange("p o i -> p (o i)") if n else t[:, bass.ds(b, 1)])
                dve.wait_ge(cdec_loaded[k], 64 * i + 64)
                c_end = c_dec[:, k, PAST - 1:PAST]
                nc.vector.tensor_scalar(s_ckn[:, k], sl(new_key, 1), c_end, None, ALU.add)
                nc.vector.tensor_tensor(s_cq[:, k], sl(new_q, 0), c_end, ALU.add).then_inc(s_small, 1)
                dve.wait_ge(new_scored, 2 * i + k + 1)
                nc.vector.scalar_tensor_tensor(out=sprob[:, k, 0:PAST], in0=psf[:, 1024:1024 + PAST], scalar=SCALE,
                                               in1=c_dec[:, k], op0=ALU.mult, op1=ALU.subtract).then_inc(s_logit, 1)
                dve.wait_ge(s_small, 2 * i + k + 1)
                nc.vector.scalar_tensor_tensor(out=sprob[:, k, PAST:PAST + DS], in0=psf[:, 1024 + PAST:1024 + PAST + DS],
                                               scalar=SCALE, in1=s_ckn[:, k], op0=ALU.mult, op1=ALU.subtract
                                               ).then_inc(s_logit, 1)

            def s_maxima(i, k):
                dve.wait_ge(s_logit, 4 * i + 2 * k + 2)
                nc.vector.tensor_reduce(s_nmax[:, k], sprob[:, k, 0:PAST + DS], AX.X, ALU.max, negate=True
                                        ).then_inc(s_max, 1)
                dve.wait_ge(s_max, 2 * i + k + 1)
                nc.vector.scalar_tensor_tensor(out=s_nbias[:, k], in0=s_nmax[:, k], scalar=s_cq[:, k], in1=s_cq[:, k],
                                               op0=ALU.subtract, op1=ALU.add).then_inc(s_bias, 1)

            def s_spread(i, k):
                dve.wait_ge(s_exp, 2 * i + k + 1)
                b = 2 * i + k
                row = own[:, b, :] if isinstance(i, int) else own[:, bass.ds(b, 1), :].rearrange("p o b -> p (o b)")
                nc.vector.tensor_tensor(p_new[:].rearrange("p (b i) -> p b i", i=DS),
                                        sprob[:, k, PAST:PAST + DS].unsqueeze(1).to_broadcast([P, NB, DS]),
                                        row.unsqueeze(2).to_broadcast([P, NB, DS]), ALU.mult).then_inc(s_pnew, 1)
                nc.vector.reciprocal(s_rinv[:, k], s_rsum[:, k])

            def take_new(i, k):
                dve.wait_ge(s_turned, 2 * i + k + 1)
                nc.vector.tensor_copy(p_newT[:], ps[0:NS, 7, P:2 * P]).then_inc(p_newT_made, 1)

            def s_scale(i, k):
                dve.wait_ge(s_pv, 2 * i + k + 1)
                nc.vector.tensor_scalar(s_outr[:], ps[:, 7, 0:P], s_rinv[:, k], None, ALU.mult).then_inc(s_scaled, 1)

            def s_output(i, k):
                dve.wait_ge(s_outT, 2 * i + k + 1)
                c0 = SEQ + 2 * DS * i + DS * k
                dst = kq[:, NKV:NKV + NH, c0:c0 + DS] if isinstance(i, int) else kq[:, NKV:NKV + NH, bass.ds(c0, DS)]
                src = ps[:, 7, 2 * P:3 * P].rearrange("p (g r) -> p g r", g=NKV)[:, :, 0:RQ]
                nc.vector.tensor_copy(dst.rearrange("p (g h) i -> p g h i", g=NKV),
                                      src.rearrange("p g (h i) -> p g h i", i=DS)).then_inc(s_out, 1)

            def s_step(i, k, prev, prev2):
                if prev is not None:
                    s_logits(*prev)
                take_kT(i, k, 1)
                if prev is not None:
                    s_maxima(*prev)
                if prev2 is not None:
                    s_output(*prev2)
                take_kT(i, k, 3)
                if prev is not None:
                    s_spread(*prev)
                take_kT(i, k, 5)
                if prev is not None:
                    take_new(*prev)
                take_kT(i, k, 7)
                if prev is not None:
                    s_scale(*prev)

            dve.wait_ge(pv_done, NH)
            s_step(0, 0, None, None)
            s_step(0, 1, (0, 0), None)
            s_step(1, 0, (0, 1), (0, 0))
            s_step(1, 1, (1, 0), (0, 1))
            with dve.Fori(2, NB // 2) as i:
                s_step(i, 0, (i - 1, 1), (i - 1, 0))
                s_step(i, 1, (i, 0), (i - 1, 1))
            last = (NB // 2 - 1, 1)
            s_logits(*last)
            s_maxima(*last)
            s_output(NB // 2 - 1, 0)
            s_spread(*last)
            take_new(*last)
            s_scale(*last)
            s_output(*last)

            for c in range(KC):
                dve.wait_ge(mix_hi, c + 1)
                nc.vector.tensor_tensor(act_lo[:, c, :], kq[:, NKV + c, :], act_hi[:, c, :], ALU.subtract
                                        ).then_inc(mix_lo, 1)

            def o_tile(i, k):
                u, t = U_O + 2 * k, T_O + k
                split(i + (u + 2) // 4, (u + 2) % 4)
                split(i + (u + 3) // 4, (u + 3) % 4)
                o_add(i, k)

            def o_add(i, k):
                u, t = U_O + 2 * k, T_O + k
                dve.wait_ge(unit_used, 4 * i + u + 2)
                dst = xT[:, 2 * i + k, :] if isinstance(i, int) else \
                    xT[:, bass.ds(2 * i + k, 1), :].rearrange("p o t -> p (o t)")
                nc.vector.tensor_tensor(halves(dst), halves(dst), acc(t % 2), ALU.add).then_inc(acc_free[t % 2], 1)

            o_tile(0, 0)
            o_tile(0, 1)
            with dve.Fori(1, KC // 2 - 1) as i:
                for k in range(2):
                    o_tile(i, k)
            o_tile(KC // 2 - 1, 0)
            split(U_M // 4, U_M % 4)
            for c in range(KC):
                gained_lo(1, g_mlp, c)
                if c == 1:
                    o_add(KC // 2 - 1, 1)
                    split((U_M + 1) // 4, (U_M + 1) % 4)

            def up_tile(j, i, k, first=False):
                u = U_M + 2 * k
                split(j * (BLK_U // 4) + i + (u + 2) // 4, (u + 2) % 4)
                split(j * (BLK_U // 4) + i + (u + 3) // 4, (u + 3) % 4)
                t = T_M + k
                if first:
                    rms_inverse(1)
                dve.wait_ge(unit_used, j * BLK_U + 4 * i + (u + 2))
                nc.vector.scalar_tensor_tensor(out=halves(tmp_a[:, k, :]), in0=acc(t % 2), scalar=0.0, in1=halves(rstd),
                                               op0=ALU.max, op1=ALU.mult).then_inc(acc_free[t % 2], 1)
                dve.wait_ge(u_hi_made, j * FB + 2 * i + (k + 1))
                sl = lambda t: t[:, bass.ds(2 * i + k, 1), :].rearrange("p o t -> p (o t)")
                nc.vector.tensor_tensor(sl(u_lo), tmp_b[:, k, :], sl(u_hi), ALU.subtract).then_inc(u_lo_made, 1)

            def up_tiles(j, done=0):
                with dve.Fori(done, FB // 2) as i:
                    for k in range(2):
                        up_tile(j, i, k)

            def down_tiles(j):
                with dve.Fori(0, KC // 4) as i:
                    for k in range(4):
                        down_tile(j, i, k)

            def down_tile(j, i, k, ahead=True):
                u, t = U_M + 2 * FB + k, T_M + FB + k
                if ahead:
                    split(j * (BLK_U // 4) + i + (u + 2) // 4, (u + 2) % 4)
                dve.wait_ge(unit_used, j * BLK_U + 4 * i + (u + 1))
                dst = xT[:, bass.ds(4 * i + k, 1), :].rearrange("p o t -> p (o t)") if not isinstance(i, int) \
                    else xT[:, 4 * i + k, :]
                nc.vector.tensor_tensor(halves(dst), halves(dst), acc(t % 2), ALU.add).then_inc(acc_free[t % 2], 1)

            for k in range(2):
                up_tile(0, 0, k, first=k == 0)
            up_tiles(0, 1)
            down_tiles(0)
            with dve.Fori(1, NBLK - 1) as j:
                up_tiles(j)
                down_tiles(j)
            up_tiles(NBLK - 1)
            with dve.Fori(0, KC // 4 - 1) as i:
                for k in range(4):
                    down_tile(NBLK - 1, i, k)
            for k in range(4):
                down_tile(NBLK - 1, KC // 4 - 1, k, ahead=k < 2)

        @block.tensor
        def _(pe):
            token_tiles = [(t * P, P) for t in range(QT)] + [(SEQ, NS)]

            pe.wait_ge(const_made, 5)
            for c in range(KC):
                if c % 4 == 0:
                    pe.wait_ge(x_loaded[c // 4], 32)
                if c >= 2:
                    pe.wait_ge(xT_made, c - 1)
                for t, (t0, n) in enumerate(token_tiles):
                    o = 2048 + 1024 * (c % 2) + t0
                    ins = pe.transpose(psf[:, o:o + n], x_tok[0:n, t, c * P:(c + 1) * P], ident[0:n, 0:n])
                ins.then_inc(x_turned, 1)

            def column_sums(src, out, signal):
                for a in range(2):
                    ins = pe.matmul(out[:, a, :], ones[:], src[:, a * HALF:(a + 1) * HALF], start=True, stop=True)
                ins.then_inc(signal, 1)

            def unit(i, k, out, hi, lo, first, last, chunk_waits=None):
                pe.wait_ge(w_lo_made, 4 * i + k + 1)
                s = k % 2
                for c in range(UC):
                    if chunk_waits is not None:
                        chunk_waits(c)
                    for a in range(2):
                        h, l = hi(c)[:, a * HALF:(a + 1) * HALF], lo(c)[:, a * HALF:(a + 1) * HALF]
                        pe.matmul(out[:, a, :], w_hi[:, s, c, :], l, start=first and c == 0, stop=False)
                        pe.matmul(out[:, a, :], w_hi[:, s, c, :], h, start=False, stop=False)
                    for a in range(2):
                        h = hi(c)[:, a * HALF:(a + 1) * HALF]
                        ins = pe.matmul(out[:, a, :], w_lo[:, s, c, :], h, start=False, stop=last and c == UC - 1)
                ins.then_inc(unit_used, 1)
                return ins

            def model_tile(i, u, t, waits=None, between=None, wait_acc=True):
                if wait_acc:
                    pe.wait_ge(acc_free[t % 2], i + t // 2)
                out = acc(t % 2)
                for half in range(2):
                    uu = u + half
                    unit(i + uu // 4, uu % 4, out, lambda c: act_hi[:, half * UC + c, :],
                         lambda c: act_lo[:, half * UC + c, :], half == 0, half == 1,
                         None if waits is None else (lambda c: waits(half * UC + c)))
                    if half == 0 and between is not None:
                        between()

            def norm_waits(n):
                def waits(c):
                    pe.wait_ge(act_lo_made, KC * n + c + 1)
                return waits

            model_tile(0, 0, 0, waits=norm_waits(0), wait_acc=False)
            pe.wait_ge(sq_added, KC - 1)
            column_sums(tmp_c[:, 0, :], acc(2), ssq_ready)

            def turn_gates():
                pe.wait_ge(const_made, 11 + NPG - 1)
                pe.wait_ge(f_chain, 5)
                pe.wait_ge(new_chain, DS)
                for n in range(TT + QT):
                    t0, w = token_tiles[n] if n < TT else token_tiles[n - TT]
                    src = (lfT if n < TT else cT)[:, t0:t0 + w]
                    pe.transpose(ps[0:w, 6, n * NH:(n + 1) * NH], src, ident[0:NH, 0:NH])
                pe.matmul(ps[:, 7, 0:NS], expand[:], cT[:, SEQ:T], start=True, stop=True).then_inc(f_turned, 1)

            for i in range(NKV // 2):
                for k in range(2):
                    u, t = U_V + 2 * k, T_V + k
                    model_tile(i, u, t, wait_acc=not (i == 0 and k == 0), between=turn_gates if 2 * i + k == 1 else None)

            def head_sums(i, m):
                t = T_K + m
                pe.wait_ge(head_lo, 2 * i + m + 1)
                if not (isinstance(i, int) and 2 * i + m == 0):
                    pe.wait_ge(head_std, 2 * i + m)
                for a in range(2):
                    cols = slice(a * HALF, (a + 1) * HALF)
                    pe.matmul(acc(2)[:, a, :], ones_r[:], sq_lo[:, cols], start=True, stop=False)
                    ins = pe.matmul(acc(2)[:, a, :], ones_r[:], sq_hi[:, cols], start=False, stop=True)
                ins.then_inc(head_ssq, 1)

            def kq_tile(i, k, u0, t0, m0):
                u, t, m = u0 + 2 * k, t0 + k, m0 + k
                first = isinstance(i, int) and m + 2 * i == 0
                model_tile(i, u, t, between=None if first else (lambda: head_sums(i, m - 1)))

            for i in range(NKV // 2):
                for k in range(2):
                    kq_tile(i, k, U_K, T_K, 0)
            for k in range(2):
                kq_tile(0, k, U_Q, T_Q, NKV)
            pe.wait_ge(lf_loaded, 16 * NB * NPG)
            pe.wait_ge(new_spread, 1)
            for b in range(NB):
                ins = pe.matmul(psf[:, 3072 + b * PAGE:3072 + (b + 1) * PAGE],
                                lf_page[:, b * NPG:(b + 1) * NPG, :].rearrange("p n h -> p (n h)"), tri[:],
                                start=True, stop=True)
            ins.then_inc(csum_done, 1)
            for k in range(2):
                kq_tile(1, k, U_Q, T_Q, NKV)
            pe.wait_ge(csum_evac, 1)
            pe.matmul(ps[:, 6, 0:NB], earlier[:], c_pg[:, :, PAGE - 1], start=True, stop=True).then_inc(csum_done, 1)
            with pe.Fori(2, NH // 2) as i:
                for k in range(2):
                    kq_tile(i, k, U_Q, T_Q, NKV)

            def turn_kv(n):
                if n == 1:
                    pe.wait_ge(head_std, NKV + NH)
                elif n >= 2:
                    made, g = (vtok_made, n - 2) if n - 2 < NKV else (ktok_made, n - 2 - NKV)
                    pe.wait_ge(made, 2 * g + 2)
                src = vT if n < NKV else kq
                for t, (t0, w) in enumerate(token_tiles):
                    o = TURN_AT[n % 2] + t * P
                    ins = pe.transpose(psf[0:w, o:o + P], src[:, n % NKV, t0:t0 + w], ident[:])
                ins.then_inc(kv_turned, 1)

            def scores(i, k):
                pe.wait_ge(q_staged, 4 * i + k + 1)
                if not (isinstance(i, int) and 4 * i + k == 0):
                    pe.wait_ge(logit_made, 16 * i + 4 * k)
                for t in range(QT):
                    w = (t + 1) * P
                    keys = kq[:, i, 0:w] if isinstance(i, int) else kq[:, bass.ds(i, 1), 0:w].rearrange("p o s -> p (o s)")
                    pe.matmul(ps[:, t, 0:w], q_st[:, k % 2, t * P:(t + 1) * P], keys, start=True, stop=True
                              ).then_inc(score_done, 1)

            PT_AT = [0, 4 * P, 8 * P, 7 * P]

            def turn_probs(i, k):
                pe.wait_ge(normed, 4 * i + k + 1)
                if not (isinstance(i, int) and 4 * i + k == 0):
                    pe.wait_ge(pT_act, 4 * i + k)
                    pe.wait_ge(pT_dve, 4 * i + k)
                for j in range(QT):
                    for t in range(j, QT):
                        o = 4 * 512 + PT_AT[j] + (t - j) * P
                        ins = pe.transpose(psf[:, o:o + P], probs[:, k, t, j * P:(j + 1) * P], ident[:])
                ins.then_inc(p_turned, 1)

            def values(i, k):
                pe.wait_ge(v_staged, i + 1)
                pe.wait_ge(pT_act, 4 * i + k + 1)
                pe.wait_ge(pT_dve, 4 * i + k + 1)
                if not (isinstance(i, int) and 4 * i + k == 0):
                    pe.wait_ge(out_evac, 4 * i + k)
                for j in range(QT):
                    w = (QT - j) * P
                    ins = pe.matmul(ps[:, 7, j * P:SEQ], v_st[:, j, :], pT[:, k % 2, PT_AT[j]:PT_AT[j] + w],
                                    start=j == 0, stop=j == QT - 1, skip_group_check=True)
                ins.then_inc(pv_done, 1)

            turn_kv(0)
            for n in range(2):
                pe.wait_ge(acc_free[n], (T_O + 1 - n) // 2)
            for k in range(4):
                scores(0, k)
                if k == 0:
                    head_sums(0, NKV + NH - 1)
                    for n in range(1, NKV):
                        turn_kv(n)
                if k == 1:
                    for n in range(NKV, 2 * NKV):
                        turn_kv(n)
                    pe.wait_ge(vtok_made, 2 * NKV)
                    pe.wait_ge(ktok_made, 2 * NKV)
                if k >= 2:
                    turn_probs(0, k - 2)
                if k >= 3:
                    values(0, k - 3)
            with pe.Fori(1, NKV) as i:
                for k in range(4):
                    scores(i, k)
                    turn_probs(*((i, k - 2) if k >= 2 else (i - 1, k + 2)))
                    values(*((i, k - 3) if k >= 3 else (i - 1, k + 1)))
            turn_probs(NKV - 1, 2)
            values(NKV - 1, 1)
            turn_probs(NKV - 1, 3)
            values(NKV - 1, 2)
            def turn_page(i, k, p):
                if not (isinstance(i, int) and 2 * i + k == 0 and p < 2):
                    (pe.wait_ge(kcT_act, NPG * i + NPG // 2 * k + p // 2) if p % 2 == 0 else
                     pe.wait_ge(kcT_dve, NPG * i + NPG // 2 * k + p // 2))
                pe.wait_ge(page_loaded[p], 32 * i + 16 * k + 16)
                for g in range(NKV):
                    ins = pe.transpose(ps[:, p % 2, g * P:(g + 1) * P], k_slot(p)[:, g * P:(g + 1) * P], ident[:])
                ins.then_inc(k_turned, 1)

            def score_half(i, k, half):
                pe.wait_ge(kcT_act, NPG * i + NPG // 2 * k + 2 * half + 2)
                pe.wait_ge(kcT_dve, NPG * i + NPG // 2 * k + 2 * half + 2)
                if half == 0:
                    pe.wait_ge(q_packed, 2 * i + k + 1)
                    if not (isinstance(i, int) and 2 * i + k == 0):
                        pe.wait_ge(s_logit, 4 * i + 2 * k)
                o = 1024 + 512 * half
                for g in range(NKV):
                    ins = pe.matmul(psf[g * R:(g + 1) * R, o:o + 512], q_pack[:, k, g, :], kcT[:, half, g, :],
                                    start=True, stop=True)
                ins.then_inc(half_scored, 1)

            def score_new(i, k):
                for g in range(NKV):
                    ins = pe.matmul(psf[g * R:(g + 1) * R, 2048:2048 + DS], q_pack[:, k, g, :], k_pack[:, k, g, :],
                                    start=True, stop=True)
                ins.then_inc(new_scored, 1)

            def turn_sprob(i, k):
                pe.wait_ge(s_pnew, 2 * i + k + 1)
                if not (isinstance(i, int) and 2 * i + k == 0):
                    pe.wait_ge(spT_made, 2 * i + k)
                    pe.wait_ge(s_out, 2 * i + k)
                for p in range(NPG):
                    pe.transpose(psf[:, 2560 + p * P:2560 + (p + 1) * P], sprob[:, k, p * PAGE:(p + 1) * PAGE], ident[:])
                pe.transpose(ps[0:NS, 7, P:2 * P], p_new[:], ident[:]).then_inc(s_turned, 1)

            def s_values(i, k):
                pe.wait_ge(v_low_loaded[k], 8 * NPG * i + 8 * NPG)
                pe.wait_ge(v_high_loaded[k], 8 * NPG * i + 8 * NPG)
                pe.wait_ge(spT_made, 2 * i + k + 1)
                pe.wait_ge(p_newT_made, 2 * i + k + 1)
                for p in range(NPG):
                    for g in range(NKV):
                        pe.matmul(ps[g * R:(g + 1) * R, 7, 0:P], spT[:, p, g * R:(g + 1) * R],
                                  v_page[:, k, p, g * P:(g + 1) * P], start=p == 0, stop=False)
                for g in range(NKV):
                    ins = pe.matmul(ps[g * R:(g + 1) * R, 7, 0:P], p_newT[:, g * R:(g + 1) * R],
                                    v_tok[0:NS, QT, g * P:(g + 1) * P], start=False, stop=True)
                ins.then_inc(s_pv, 1)

            def turn_out(i, k):
                pe.wait_ge(s_scaled, 2 * i + k + 1)
                pe.transpose(ps[:, 7, 2 * P:3 * P], s_outr[:], ident[:]).then_inc(s_outT, 1)

            def s_step(i, k, prev, prev2, done=0):
                for p in range(done, 3):
                    turn_page(i, k, p)
                if prev2 is not None:
                    turn_out(*prev2)
                for p in range(3, 6):
                    turn_page(i, k, p)
                score_half(i, k, 0)
                if prev is not None:
                    turn_sprob(*prev)
                for p in range(6, NPG):
                    turn_page(i, k, p)
                if prev is not None:
                    s_values(*prev)
                score_half(i, k, 1)
                score_new(i, k)

            for p in range(2):
                turn_page(0, 0, p)
            values(NKV - 1, 3)
            s_step(0, 0, None, None, done=2)
            s_step(0, 1, (0, 0), None)
            s_step(1, 0, (0, 1), (0, 0))
            s_step(1, 1, (1, 0), (0, 1))
            with pe.Fori(2, NB // 2) as i:
                s_step(i, 0, (i - 1, 1), (i - 1, 0))
                s_step(i, 1, (i, 0), (i - 1, 1))
            last = (NB // 2 - 1, 1)
            turn_out(NB // 2 - 1, 0)
            turn_sprob(*last)
            s_values(*last)
            turn_out(*last)

            for k in range(2):
                u, t = U_O + 2 * k, T_O + k
                model_tile(0, u, t, waits=(lambda c: pe.wait_ge(mix_lo, c + 1)) if k == 0 else None)
            with pe.Fori(1, KC // 2) as i:
                for k in range(2):
                    u, t = U_O + 2 * k, T_O + k
                    model_tile(i, u, t)
            def up_tiles(j, i, waits=None):
                for k in range(2):
                    u, t = U_M + 2 * k, T_M + k
                    pe.wait_ge(acc_free[t % 2], j * (BLK_T // 2) + i + t // 2)
                    for half in range(2):
                        uu = u + half
                        unit(j * (BLK_U // 4) + i + uu // 4, uu % 4, acc(t % 2),
                             lambda c: act_hi[:, half * UC + c, :], lambda c: act_lo[:, half * UC + c, :],
                             half == 0, half == 1,
                             None if waits is None or k else (lambda c: waits(half * UC + c)))
                        if waits is not None and k == 0 and half == 0:
                            pe.wait_ge(sq_added, 2 * (KC - 1))
                            column_sums(tmp_c[:, 0, :], acc(2), ssq_ready)

            def turn_y(c):
                t = T_M + (NBLK - 1) * BLK_T + FB + c
                pe.wait_ge(acc_free[t % 2], t // 2 + 1)
                if c >= 2:
                    pe.wait_ge(y_evac, 2 * (c - 1))
                o = 2048 + 1024 * (c % 2)
                for n, (t0, w) in enumerate(token_tiles):
                    ins = pe.transpose(psf[0:w, o + n * P:o + (n + 1) * P], xT[:, c, t0:t0 + w], ident[:])
                ins.then_inc(y_turned, 1)

            def down_tiles(j, i, waits=None, turn=False):
                for k in range(4):
                    u, t = U_M + 2 * FB + k, T_M + FB + k
                    pe.wait_ge(acc_free[t % 2], j * (BLK_T // 2) + 2 * i + t // 2)
                    unit(j * (BLK_U // 4) + i + u // 4, u % 4, acc(t % 2), lambda c: u_hi[:, c, :],
                         lambda c: u_lo[:, c, :], True, True, waits if k == 0 else None)
                    if turn:
                        for c in range(3 * k, 3 * k + 3):
                            turn_y(c)

            def mlp_block(j, first_waits=None, turn=False):
                if first_waits is not None:
                    up_tiles(j, 0, first_waits)
                with pe.Fori(1 if first_waits is not None else 0, FB // 2) as i:
                    up_tiles(j, i)
                down_tiles(j, 0, lambda c: pe.wait_ge(u_lo_made, FB * j + c + 1))
                with pe.Fori(1, KC // 4 - turn) as i:
                    down_tiles(j, i)
                if turn:
                    down_tiles(j, KC // 4 - 1, turn=True)
                    for c in range(12, KC):
                        turn_y(c)

            mlp_block(0, norm_waits(1))
            with pe.Fori(1, NBLK - 1) as j:
                mlp_block(j)
            mlp_block(NBLK - 1, turn=True)


_INS = ["x_prompt", "x_sample", "cache_k", "cache_v", "cache_logf", "page_table", "attn_norm", "w_qkv", "q_norm",
        "k_norm", "w_fgate", "b_fgate", "w_o", "mlp_norm", "w_up", "w_down"]


def kernel(**inputs):
    import numpy as _np
    import concourse.bacc as _bacc
    from concourse import mybir as _mybir
    from concourse.bass_utils import run_bass_kernel_spmd as _run

    nc = _bacc.Bacc("TRN2", target_bir_lowering=False, num_devices=1)
    arrays, args = {}, []
    for name in _INS:
        a = _np.ascontiguousarray(inputs[name])
        arrays[f"in_{name}"] = a
        args.append(nc.dram_tensor(f"in_{name}", a.shape, _mybir.dt.from_np(a.dtype), kind="ExternalInput").ap())
    xp, xs = inputs["x_prompt"].shape, inputs["x_sample"].shape
    depth, _, _, nkv, hd = inputs["cache_k"].shape
    nfox, _, _, nh = inputs["cache_logf"].shape
    outs = [xp, xs, (depth, *xp[:2], nkv, hd), (depth, *xp[:2], nkv, hd), (nfox, *xp[:2], nh),
            (depth, *xs[:2], nkv, hd), (depth, *xs[:2], nkv, hd), (nfox, *xs[:2], nh)]
    for i, shape in enumerate(outs):
        args.append(nc.dram_tensor(f"out_{i}", shape, F32, kind="ExternalOutput").ap())
    fox_layer(nc, *args)
    r = _run(nc, [arrays], core_ids=[0])
    return tuple(r.results[0][f"out_{i}"] for i in range(len(outs)))
```
